# Optimizing a Trainium2 kernel written in Bass

```python
import jax, jax.numpy as jnp
from jax import lax
import numpy as np

D_MODEL = 2048
BATCH = 1
SEQ = 256
DEPTH = 1

CHUNK = 64
EPS = 1e-6
NEG_INF = -1e30

MIX_WIDTH = D_MODEL
POOL_WIDTH = D_MODEL // 2
POOL_WINDOWS = (2, 4, 8, 16)
POOL_GROUPS = len(POOL_WINDOWS)
POOL_GROUP_DIM = POOL_WIDTH // POOL_GROUPS
V_HEAD_DIM = 128
MLA_WIDTH = MIX_WIDTH - POOL_WIDTH
MLA_HEADS = MLA_WIDTH // V_HEAD_DIM
QK_NOPE_DIM = 128
QK_ROPE_DIM = 64
QK_HEAD_DIM = QK_NOPE_DIM + QK_ROPE_DIM
Q_LORA_RANK = 512
KV_LORA_RANK = 256
ROPE_THETA = 10000.0
IN_WIDTH = POOL_WIDTH + Q_LORA_RANK + KV_LORA_RANK + QK_ROPE_DIM
Q_BLOCK = 128

PEER_HEADS = 8
PEER_N_KEYS = 128
PEER_N_EXPERTS = PEER_N_KEYS * PEER_N_KEYS
PEER_QUERY_DIM = 256
PEER_HALF_DIM = PEER_QUERY_DIM // 2
PEER_TOPK = 16
PEER_TOKEN_BLOCK = 128

kernel_name = "hybrid_pool_mla_peer_block"

def rms_norm(x, g):
    xf = x.astype(jnp.float32)
    y = xf * lax.rsqrt(jnp.mean(xf * xf, axis=-1, keepdims=True) + EPS)
    return (y * g.astype(jnp.float32)).astype(x.dtype)

def modulate(h, shift, scale):
    return h * (1 + scale[:, None, :]) + shift[:, None, :]

def apply_rope(x, cos, sin):
    x1, x2 = jnp.split(x.astype(jnp.float32), 2, axis=-1)
    return jnp.concatenate([x1 * cos - x2 * sin, x2 * cos + x1 * sin], axis=-1).astype(x.dtype)

def multiscale_pool(u, w_pool, pool_scale):
    b, s, _ = u.shape
    ug = u.astype(jnp.float32).reshape(b, s, POOL_GROUPS, POOL_GROUP_DIM)
    cs0 = jnp.concatenate([jnp.zeros_like(ug[:, :1]), jnp.cumsum(ug, axis=1)], axis=1)
    t = jnp.arange(s)
    groups = []
    for g, w in enumerate(POOL_WINDOWS):
        c_g = cs0[:, :, g]
        lagged = jnp.pad(c_g[:, : s + 1 - w], ((0, 0), (w - 1, 0), (0, 0)))
        count = jnp.minimum(t + 1, w).astype(jnp.float32)[None, :, None]
        groups.append((c_g[:, 1:] - lagged) / count - ug[:, :, g])
    z = jnp.stack(groups, axis=2).astype(u.dtype)
    y = jnp.einsum('bsgc,gcd->bsgd', z, w_pool)
    return y.reshape(b, s, POOL_WIDTH) * pool_scale

def mla_attention(c_q, c_kv, k_pe, cos, sin, q_norm_g, w_uq, kv_norm_g, w_ukv):
    b, s, _ = c_q.shape
    q = (rms_norm(c_q, q_norm_g) @ w_uq).reshape(b, s, MLA_HEADS, QK_HEAD_DIM)
    q_nope = q[..., :QK_NOPE_DIM]
    q_pe = apply_rope(q[..., QK_NOPE_DIM:], cos[:, :, None, :], sin[:, :, None, :])
    kv = (rms_norm(c_kv, kv_norm_g) @ w_ukv).reshape(b, s, MLA_HEADS, QK_NOPE_DIM + V_HEAD_DIM)
    k_nope = kv[..., :QK_NOPE_DIM]
    v = kv[..., QK_NOPE_DIM:]
    k_pe = apply_rope(k_pe, cos, sin)
    scale = QK_HEAD_DIM ** -0.5
    chunk_id = jnp.arange(s) // CHUNK
    outs = []
    for i in range(s // Q_BLOCK):
        qs, qe = i * Q_BLOCK, (i + 1) * Q_BLOCK
        kend = qe
        sc = (jnp.einsum('bqhd,bkhd->bhqk', q_nope[:, qs:qe], k_nope[:, :kend])
              + jnp.einsum('bqhr,bkr->bhqk', q_pe[:, qs:qe], k_pe[:, :kend])).astype(jnp.float32) * scale
        mask = chunk_id[qs:qe, None] >= chunk_id[None, :kend]
        sc = jnp.where(mask[None, None], sc, NEG_INF)
        p = jax.nn.softmax(sc, axis=-1).astype(v.dtype)
        outs.append(jnp.einsum('bhqk,bkhd->bqhd', p, v[:, :kend]))
    return jnp.concatenate(outs, axis=1).reshape(b, s, MLA_WIDTH)

def peer_ffn(h, w_q, sub_keys, expert_u, expert_v):
    b, s, d = h.shape
    t = b * s
    hf = h.reshape(t, d)
    q = (hf @ w_q).reshape(t, PEER_HEADS, 2, PEER_HALF_DIM)
    sc = jnp.einsum('thpd,hpnd->thpn', q, sub_keys).astype(jnp.float32)
    sv, si = lax.top_k(sc, PEER_TOPK)
    cand = (sv[:, :, 0, :, None] + sv[:, :, 1, None, :]).reshape(t, PEER_HEADS, PEER_TOPK * PEER_TOPK)
    cidx = (si[:, :, 0, :, None] * PEER_N_KEYS + si[:, :, 1, None, :]).reshape(t, PEER_HEADS, PEER_TOPK * PEER_TOPK)
    best, pos = lax.top_k(cand, PEER_TOPK)
    eidx = jnp.take_along_axis(cidx, pos, axis=-1).reshape(t, PEER_HEADS * PEER_TOPK)
    gate = jax.nn.softmax(best, axis=-1).reshape(t, PEER_HEADS * PEER_TOPK)
    nb = t // PEER_TOKEN_BLOCK

    def block(args):
        xb, ib, gb = args
        u = jnp.take(expert_u, ib, axis=0)
        a = jnp.einsum('ted,td->te', u, xb).astype(jnp.float32)
        act = (jax.nn.gelu(a, approximate=False) * gb).astype(xb.dtype)
        vv = jnp.take(expert_v, ib, axis=0)
        return jnp.einsum('te,ted->td', act, vv)

    out = lax.map(block, (hf.reshape(nb, PEER_TOKEN_BLOCK, d),
                          eidx.reshape(nb, PEER_TOKEN_BLOCK, -1),
                          gate.reshape(nb, PEER_TOKEN_BLOCK, -1)))
    return out.reshape(b, s, d)

def setup_inputs(seed: int = 0) -> dict:
    key = jax.random.key(seed)
    ks = jax.random.split(key, 24)
    f32 = jnp.float32

    def nrm(k, shape, s):
        return jax.random.normal(k, shape, f32) * s

    def gain(k, shape):
        return 1.0 + 0.05 * jax.random.normal(k, shape, f32)

    x = jax.random.normal(ks[0], (BATCH, SEQ, D_MODEL), f32)
    c = jax.random.normal(ks[1], (BATCH, D_MODEL), f32)
    offset = jax.random.randint(ks[2], (BATCH, 1), 0, 64, dtype=jnp.int32) * CHUNK
    positions = (offset + jnp.arange(SEQ, dtype=jnp.int32)[None, :]).astype(jnp.int32)
    L = DEPTH
    return {
        "x": x,
        "c": c,
        "positions": positions,
        "ada_w": nrm(ks[3], (L, D_MODEL, 6 * D_MODEL), 0.5 * D_MODEL ** -0.5),
        "ada_b": nrm(ks[4], (L, 6 * D_MODEL), 0.02),
        "pre_mix_g": gain(ks[5], (L, D_MODEL)),
        "post_mix_g": gain(ks[6], (L, D_MODEL)),
        "pre_ffn_g": gain(ks[7], (L, D_MODEL)),
        "post_ffn_g": gain(ks[8], (L, D_MODEL)),
        "w_in": nrm(ks[9], (L, D_MODEL, IN_WIDTH), D_MODEL ** -0.5),
        "pool_w": nrm(ks[10], (L, POOL_GROUPS, POOL_GROUP_DIM, POOL_GROUP_DIM), POOL_GROUP_DIM ** -0.5),
        "pool_scale": 1.0 + 0.1 * jax.random.normal(ks[11], (L, POOL_WIDTH), f32),
        "q_norm_g": gain(ks[12], (L, Q_LORA_RANK)),
        "w_uq": nrm(ks[13], (L, Q_LORA_RANK, MLA_HEADS * QK_HEAD_DIM), Q_LORA_RANK ** -0.5),
        "kv_norm_g": gain(ks[14], (L, KV_LORA_RANK)),
        "w_ukv": nrm(ks[15], (L, KV_LORA_RANK, MLA_HEADS * (QK_NOPE_DIM + V_HEAD_DIM)), KV_LORA_RANK ** -0.5),
        "w_out": nrm(ks[16], (L, MIX_WIDTH, D_MODEL), MIX_WIDTH ** -0.5),
        "peer_wq": nrm(ks[17], (L, D_MODEL, PEER_HEADS * PEER_QUERY_DIM), D_MODEL ** -0.5),
        "peer_sub_keys": nrm(ks[18], (L, PEER_HEADS, 2, PEER_N_KEYS, PEER_HALF_DIM), PEER_HALF_DIM ** -0.5),
        "peer_u": nrm(ks[19], (L, PEER_N_EXPERTS, D_MODEL), D_MODEL ** -0.5),
        "peer_v": nrm(ks[20], (L, PEER_N_EXPERTS, D_MODEL), PEER_HEADS ** -0.5),
    }

def reference(x, c, positions, ada_w, ada_b, pre_mix_g, post_mix_g, pre_ffn_g, post_ffn_g,
              w_in, pool_w, pool_scale, q_norm_g, w_uq, kv_norm_g, w_ukv, w_out,
              peer_wq, peer_sub_keys, peer_u, peer_v):
    half = QK_ROPE_DIM // 2
    inv_freq = ROPE_THETA ** (-jnp.arange(half, dtype=jnp.float32) / half)
    ang = positions.astype(jnp.float32)[..., None] * inv_freq
    cos, sin = jnp.cos(ang), jnp.sin(ang)
    c_act = jax.nn.silu(c)
    for l in range(DEPTH):
        mod = c_act @ ada_w[l] + ada_b[l]
        shift1, scale1, gate1, shift2, scale2, gate2 = jnp.split(mod, 6, axis=-1)

        h = modulate(rms_norm(x, pre_mix_g[l]), shift1, scale1)
        proj = h @ w_in[l]
        o1 = POOL_WIDTH
        o2 = o1 + Q_LORA_RANK
        o3 = o2 + KV_LORA_RANK
        y_pool = multiscale_pool(proj[..., :o1], pool_w[l], pool_scale[l])
        y_mla = mla_attention(proj[..., o1:o2], proj[..., o2:o3], proj[..., o3:], cos, sin,
                              q_norm_g[l], w_uq[l], kv_norm_g[l], w_ukv[l])
        y = jnp.concatenate([y_pool, y_mla], axis=-1) @ w_out[l]
        x = x + gate1[:, None, :] * rms_norm(y, post_mix_g[l])

        h = modulate(rms_norm(x, pre_ffn_g[l]), shift2, scale2)
        y = peer_ffn(h, peer_wq[l], peer_sub_keys[l], peer_u[l], peer_v[l])
        x = x + gate2[:, None, :] * rms_norm(y, post_ffn_g[l])
    return x


_drawn_inputs = setup_inputs


def setup_inputs(seed=0):
    import zlib

    import numpy as np

    out = dict(_drawn_inputs(seed))
    spreads = {}
    factors = {'post_ffn_g': 3.884, 'q_norm_g': 3.305}
    for name, (base, spread) in spreads.items():
        noise = np.random.default_rng([zlib.crc32(name.encode()), seed]).standard_normal(out[name].shape)
        drawn = base * np.exp(spread * noise) if base else spread * noise
        out[name] = __import__('jax').numpy.asarray(drawn.astype(out[name].dtype))
    for name, factor in factors.items():
        out[name] = (out[name] * factor).astype(out[name].dtype)
    return out
```

```python
import concourse.bass as bass
from concourse import mybir

F32 = mybir.dt.float32
F32R = mybir.dt.float32r
U32 = mybir.dt.uint32
I32 = mybir.dt.int32
ALU = mybir.AluOpType
ACT = mybir.ActivationFunctionType
AX_X = mybir.AxisListType.X

P = 128
D = 2048
T = 256
TT = T // P
KT = D // P
W = 512
POOL_W = 1024
WINDOWS = (2, 4, 8, 16)
HEADS = 8
NOPE = 128
ROPE = 64
HALF = ROPE // 2
QR = 512
KVR = 256
LAT = QR + KVR + ROPE
SCALE = float(NOPE + ROPE) ** -0.5
EPS = 1e-6
PH = 8
NK = 128
TOPK = 16
QUAD = 32
TILES = NK * NK // P
HF = 1024
RING = 3
BIG = 3.0e38

C_ID, C_ONE, C_IOTA, C_MASK = 0, P, 2 * P, 3 * P
C_FREQ = C_MASK + 3 * P
C_CNT = C_FREQ + HALF
C_I16 = C_CNT + 4 * 16
C_ALL = C_I16 + 16

V_G1, V_G2 = 0, KT
V_QN = 2 * KT
V_KVN = V_QN + QR // P
V_PS = V_KVN + KVR // P
V_ALL = V_PS + POOL_W // P

TWO_PI_A = 6.28125
TWO_PI_B = 0.0019340515136718750
TWO_PI_C = 1.2556659146019e-06


def pair(i):
    return 2 * (i // 2 + 1)


def chunk_plan():
    ada = [("ada", n) for n in range(24)]
    plan = ada[:8] + [("win", 0), ada[8], ("win", 1), ada[9], ("win", 2), ada[10], ("win", 3),
                      ("uq", 0), ("ukv", 0), ada[11], ada[12], ada[13]]
    plan += [("wout", 0), ada[14], ("wout", 1), ada[15], ("wout", 2), ada[16], ("wout", 3)]
    plan += ada[17:24] + [("wq", 0), ("wq", 1), ("wq", 2), ("wq", 3), ("keys", 0)]
    return plan


def hybrid_block(nc, x, c, positions, ada_w, ada_b, pre_mix_g, post_mix_g, pre_ffn_g, post_ffn_g,
                 w_in, pool_w, pool_scale, q_norm_g, w_uq, kv_norm_g, w_ukv, w_out,
                 peer_wq, peer_sub_keys, peer_u, peer_v, consts, out):
    plan = chunk_plan()
    where = {}
    per_slot = [0, 0, 0]
    for n, key in enumerate(plan):
        slot = n % 3
        per_slot[slot] += 64 if key[0] == "wq" else 32 if key[0] in ("uq",) else 16
        where[key] = (slot, per_slot[slot], n)

    base = (nc.sbuf_base + 31) // 32 * 32

    def at(name, off, shape, dt=F32):
        return nc.alloc_sbuf_tensor_at(name, [P] + shape, dt, offset=base + 4 * off)

    ring = [at(f"ring{s}", 8192 * s, [8192]) for s in range(3)]
    xs = at("xs", 24576, [TT, D])
    hT = at("hT", 28672, [KT, T])
    qnT = at("qnT", 28672, [HEADS, T])
    knT = at("knT", 30720, [HEADS, T])
    y1 = at("y1", 28672, [TT, D])
    h2T = at("h2T", 28672, [KT, T])
    qT = at("qT", 24576, [KT, T])
    keyT = at("keyT", 8192, [KT, NK])
    sc = at("sc", 20480, [TT, KT, NK])
    tmpk = at("tmpk", 18432, [2048])
    tmpk2 = at("tmpk2", 16384, [2048])
    acts = at("acts", 0, [TILES, T])
    S = 32768
    cst = at("cst", S, [3 * P])
    vcols = at("vcols", S + 384, [V_ALL])
    mod1 = at("mod1", S + 432, [2, KT])
    mod2 = at("mod2", S + 464, [2, KT])
    stat = at("stat", S + 496, [64])
    c_col = at("c_col", S + 560, [KT])
    c_act = at("c_act", S + 576, [KT])
    i16 = at("i16", S + 592, [16])
    cnt = at("cnt", S + 608, [4, 16])
    pos_i = at("pos_i", S + 672, [TT], I32)
    pos_f = at("pos_f", S + 680, [TT])
    rowbuf = at("rowbuf", S + 688, [W])
    diag = at("diag", S + 1280, [TT, P])
    slotT = at("slotT", S + 1536, [3, T])
    aH = [at("aH0", S + 1280, [T], F32R), at("aH1", S + 1536, [T], F32R)]
    aL = [at("aL0", S + 1792, [T], F32R), at("aL1", S + 2048, [T], F32R)]
    M = S + 2304
    uT = at("uT", M, [POOL_W // P, T])
    vv = at("vv", M, [TT, POOL_W])
    gate1 = at("gate1", M, [D])
    zT = at("zT", M + 2048, [POOL_W // P, T])
    s_sb = at("s_sb", M + 2048, [2, 384])
    pT = at("pT", M + 2816, [2, 384])
    post1 = at("post1", M + 2048, [D])
    catT = at("catT", M + 4096, [KT, T])
    acc = at("acc", M + 8192, [2, W])
    init = at("init", M + 9216, [2, W])
    lat = at("lat", M + 10240, [TT, LAT])
    cT = at("cT", M + 11904, [6, T])
    qpeT = at("qpeT", M + 13440, [4, T])
    kpeT = at("kpeT", M + 14464, [T])
    qrope = at("qrope", M + 14720, [TT, 8 * ROPE])
    krope = at("krope", M + 15744, [TT, 2 * ROPE])
    trig = at("trig", M + 16000, [2, TT, HALF])
    tmpr = at("tmpr", M + 16128, [2, 256])
    x1q = at("x1q", M + 10240, [TT, D])
    mask = at("mask", M + 16640, [3 * P])
    freq = at("freq", M + 17024, [HALF])
    vrow = at("vrow", M + 17056, [P])
    ang = at("ang", M + 17184, [4, TT * HALF])
    junk = at("junk", M, [D])
    s16 = at("s16", M + 8192, [TT, KT, TOPK])
    i16u = at("i16u", M + 8704, [TT, KT, TOPK], U32)
    i16f = at("i16f", M + 9216, [TT, KT, TOPK])
    best = at("best", M + 9728, [TT, PH * TOPK])
    posu = at("posu", M + 9984, [TT, PH * TOPK], U32)
    posa = at("posa", M + 10240, [TT, PH * TOPK], U32)
    posf = at("posf", M + 10496, [2, TT, PH * TOPK])
    slots = at("slots", M + 11008, [3, TT, PH * TOPK])
    gsum = at("gsum", M + 11776, [TT, PH])
    gtmp = at("gtmp", M + 11792, [TT, PH * TOPK])
    h2H = at("h2H", M, [KT, T], F32R)
    h2L = at("h2L", M + 4096, [KT, T], F32R)
    x1 = at("x1", M, [TT, D])
    gate2 = at("gate2", M + 4096, [D])
    post2 = at("post2", M + 6144, [D])
    raw = at("raw", M + 8192, [RING, HF])
    eL = at("eL", M + 11264, [RING, HF], F32R)
    eH = at("eH", M + 14336, [RING, HF], F32R)
    hotA = at("hotA", M + 14336, [2, 4, P])
    hotB = at("hotB", M + 15360, [2, 4, P])
    aH.append(at("aH2", M + 17408, [T], F32R))
    aL.append(at("aL2", M + 17664, [T], F32R))

    x1_dram = nc.dram_tensor("x1_dram", [TT, P, D], F32).ap()
    gate_dram = nc.dram_tensor("gate_dram", [2, D], F32).ap()

    from contextlib import ExitStack
    with ExitStack() as ctx:
        ps = ctx.enter_context(nc.psum_tensor("ps", [P, 8, W], F32))

        def sem(name):
            return ctx.enter_context(nc.semaphore(name))

        consts_in, vrow_in, x_in, c_in = sem("consts_in"), sem("vrow_in"), sem("x_in"), sem("c_in")
        ring_in = [sem(f"ring_in{s}") for s in range(3)]
        init_in = [sem("init_in0"), sem("init_in1")]
        init_zero = sem("init_zero")
        acc_ready, acc_used = sem("acc_ready"), sem("acc_used")
        row_ready, row_stored = sem("row_ready"), sem("row_stored")
        silu_done = sem("silu_done")
        vec_t, vec_cols = sem("vec_t"), sem("vec_cols")
        mod1_ready, mod2_ready = sem("mod1_ready"), sem("mod2_ready")
        x_sq, x_rs, diag1 = sem("x_sq"), sem("x_rs"), sem("diag1")
        xT_done, hT_done = sem("xT_done"), sem("hT_done")
        u_mm, u_out = sem("u_mm"), sem("u_out")
        lat_mm, lat_out, lat_sq = sem("lat_mm"), sem("lat_out"), sem("lat_sq")
        trig_ready, trig_arg = sem("trig_ready"), sem("trig_arg")
        z_ready, k_roped, lat_diag = sem("z_ready"), sem("k_roped"), sem("lat_diag")
        cT_mm, cT_out = sem("cT_mm"), sem("cT_out")
        qn_mm, qn_out = sem("qn_mm"), sem("qn_out")
        qpe_mm, q_roped, qpeT_mm, qpeT_out = sem("qpe_mm"), sem("q_roped"), sem("qpeT_mm"), sem("qpeT_out")
        kn_mm, kn_out, v_mm, v_out = sem("kn_mm"), sem("kn_out"), sem("v_mm"), sem("v_out")
        pool_mm, pool_out = sem("pool_mm"), sem("pool_out")
        s_mm, s_max, s_exp, s_norm = sem("s_mm"), sem("s_max"), sem("s_exp"), sem("s_norm")
        pT_mm, pT_out, o_mm, o_out = sem("pT_mm"), sem("pT_out"), sem("o_mm"), sem("o_out")
        y_mm, y_out = sem("y_mm"), sem("y_out")
        y_rs, g1_in, x1_done, x1_sq, x1_rs, diag2 = (
            sem("y_rs"), sem("g1_in"), sem("x1_done"), sem("x1_sq"), sem("x1_rs"), sem("diag2"))
        y_rc, x1_stored = sem("y_rc"), sem("x1_stored")
        x1T_mm, h2_out, h2H_out, h2L_out = sem("x1T_mm"), sem("h2_out"), sem("h2H_out"), sem("h2L_out")
        qT_mm, qT_out, key_mm, key_out = sem("qT_mm"), sem("qT_out"), sem("key_mm"), sem("key_out")
        sc_mm, sc_out = sem("sc_mm"), sem("sc_out")
        g_shift, g_exp, slots_ready, slot_mm, slotT_out = (
            sem("g_shift"), sem("g_exp"), sem("slots_ready"), sem("slot_mm"), sem("slotT_out"))
        route_done = sem("route_done")
        raw_in = [sem(f"raw_in{s}") for s in range(RING)]
        u_tr, u_hi, u_lo, u_used = sem("u_tr"), sem("u_hi"), sem("u_lo"), sem("u_used")
        a_out = sem("a_out")
        hotA_ready, hot_ready, hot_mm, gated = sem("hotA_ready"), sem("hot_ready"), sem("hot_mm"), sem("gated")
        v_in = [sem(f"v_in{s}") for s in range(RING)]
        v_hi, v_lo, v_used = sem("v_hi"), sem("v_lo"), sem("v_used")
        act_hi, act_lo = sem("act_hi"), sem("act_lo")
        y2_sq, y2_rc, y2_rs, tail_in, out_ready, out_stored = (
            sem("y2_sq"), sem("y2_rc"), sem("y2_rs"), sem("tail_in"), sem("out_ready"),
            sem("out_stored"))
        dve_chain, act_chain = sem("dve_chain"), sem("act_chain")

        block = ctx.enter_context(nc.Block())

        ident = cst[:, 0:P]
        ones = cst[:, P:2 * P]
        iota = cst[:, 2 * P:3 * P]

        def ring_arrived(eng, key):
            slot, count, _ = where[key]
            eng.wait_ge(ring_in[slot], count)

        def last_use(key):
            kind, i = key
            return {"ada": (acc_ready, i + 1), "win": (u_mm, 4 * (i + 1)) if i < 2 else (lat_mm, 2 * (i - 1)),
                    "uq": (pool_mm, 8), "ukv": (v_mm, 4), "wout": (y_mm, 2 * (i + 1)),
                    "wq": (qT_mm, 4 * (i + 1)), "keys": (key_mm, 4)}[kind]

        def wide(key, cols=W):
            return ring[where[key][0]][:, 0:KT * cols].rearrange("p (k n) -> p k n", k=KT)

        def turned(half_tile):
            return half_tile.rearrange("p (eb k el) -> p k eb el", eb=4, el=QUAD)

        def by_k(half_tile):
            return half_tile.rearrange("p (k eb el) -> p k eb el", eb=4, el=QUAD)

        ada_v = ada_w[0].rearrange("(p k) n -> p k n", k=KT)
        win_v = w_in[0].rearrange("(k p) n -> p k n", p=P)
        wout_v = w_out[0].rearrange("(k p) n -> p k n", p=P)
        wq_v = peer_wq[0].rearrange("(q k l) n -> q l k n", q=4, l=QUAD)
        ub = peer_u[0].rearrange("(i eb el) (q h dd) -> i h q el eb dd", el=QUAD, eb=4, q=4, h=2)
        vb = peer_v[0].rearrange("(i p) (h dd) -> i h p dd", p=P, h=2)

        @block.sync
        def _(sp):
            sp.dma_start(c_col[:], c.rearrange("o (p k) -> (o p) k", k=KT)).then_inc(c_in, 16)
            sp.dma_start(cst[:], consts[:, 0:3 * P]).then_inc(consts_in, 16)
            sp.dma_start(mask[:], consts[:, C_MASK:C_MASK + 3 * P]).then_inc(consts_in, 16)
            sp.dma_start(freq[:], consts[:, C_FREQ:C_FREQ + HALF]).then_inc(consts_in, 16)
            sp.dma_start(cnt[:], consts[:, C_CNT:C_CNT + 64].rearrange("p (g t) -> p g t", g=4)).then_inc(consts_in, 16)
            sp.dma_start(i16[:], consts[:, C_I16:C_I16 + 16]).then_inc(consts_in, 16)

            ada_n = 0
            for n, (kind, i) in enumerate(plan):
                slot = n % 3
                if n >= 3:
                    sp.wait_ge(*last_use(plan[n - 3]))
                dst = ring[slot]
                done = ring_in[slot]
                if kind == "ada":
                    sp.dma_start(wide((kind, i)), ada_v[:, :, i * W:(i + 1) * W]).then_inc(done, 16)
                    if ada_n == 0:
                        sp.wait_ge(init_zero, 1)
                    if ada_n >= 2:
                        sp.wait_ge(acc_ready, ada_n - 1)
                    sp.dma_start(init[0:1, ada_n % 2, :], ada_b[0:1, i * W:(i + 1) * W]).then_inc(init_in[ada_n % 2], 16)
                    ada_n += 1
                elif kind == "win":
                    cols = min(W, POOL_W + LAT - i * W)
                    sp.dma_start(wide((kind, i), cols), win_v[:, :, i * W:i * W + cols]).then_inc(done, 16)
                elif kind == "wout":
                    sp.dma_start(wide((kind, i)), wout_v[:, :, i * W:(i + 1) * W]).then_inc(done, 16)
                elif kind == "uq":
                    sp.dma_start(dst[:, 0:6144].rearrange("p (k n) -> p k n", k=4),
                                 w_uq[0].rearrange("(k p) n -> p k n", p=P)).then_inc(done, 16)
                    sp.dma_start(dst[:, 6144:8192].rearrange("p (g k n) -> p g k n", g=4, k=2),
                                 pool_w[0].rearrange("g (k p) n -> p g k n", p=P)).then_inc(done, 16)
                elif kind == "ukv":
                    sp.dma_start(dst[:, 0:4096].rearrange("p (k n) -> p k n", k=2),
                                 w_ukv[0].rearrange("(k p) n -> p k n", p=P)).then_inc(done, 16)
                elif kind == "wq":
                    for q in range(4):
                        sp.dma_start(wide((kind, i))[q * QUAD:(q + 1) * QUAD],
                                     wq_v[q, :, :, i * W:(i + 1) * W]).then_inc(done, 16)
                elif kind == "keys":
                    sp.dma_start(dst[:, 0:2048].rearrange("p (k n) -> p k n", k=KT),
                                 peer_sub_keys[0].rearrange("h s n d -> n (h s) d")).then_inc(done, 16)

            sp.wait_ge(acc_used, 24)
            sp.wait_ge(q_roped, 1)
            sp.wait_ge(qpeT_out, 1)
            sp.wait_ge(x1T_mm, KT)
            sp.wait_ge(x1_stored, 16)
            sp.wait_ge(slots_ready, 1)
            sp.wait_ge(slot_mm, 1)

            def load_u(tile, h, g, slot, first):
                if not first:
                    sp.wait_ge(u_lo, g - (RING - 1))
                for q in range(4):
                    sp.dma_start(raw[q * QUAD:(q + 1) * QUAD, slot, :].rearrange("p (e d) -> p e d", e=4),
                                 ub[tile, h, q]).then_inc(raw_in[slot], 16)

            def load_u3(t0, first=False):
                for j in range(6):
                    load_u(t0 + j // 2, j % 2, t0 * 2 + j, j % RING, first and j < RING)

            load_u3(0, True)
            with sp.Fori(1, TILES // 3) as r:
                load_u3(r * 3)
            for j in range(4):
                load_u(TILES - 2 + j // 2, j % 2, 2 * (TILES - 2) + j, j % RING, False)

            def load_v(tile, h, g, slot):
                sp.wait_ge(v_lo, g - (RING - 1))
                sp.dma_start(raw[:, slot, :], vb[tile, h]).then_inc(v_in[slot], 16)

            def load_v3(t0):
                for j in range(6):
                    load_v(t0 + j // 2, j % 2, t0 * 2 + j, j % RING)

            sp.wait_ge(u_lo, 2 * TILES)
            for j in range(RING):
                sp.dma_start(raw[:, j, :], vb[j // 2, j % 2]).then_inc(v_in[j], 16)
            for j in range(RING, 6):
                load_v(j // 2, j % 2, j, j % RING)
            with sp.Fori(1, TILES // 3) as r:
                load_v3(r * 3)
            for j in range(4):
                load_v(TILES - 2 + j // 2, j % 2, 2 * (TILES - 2) + j, j % RING)

        @block.gpsimd
        def _(pool):
            xr = x[0].rearrange("(t p) d -> p t d", p=P)
            vr = vrow[:, :]
            pool.memset(init[:], 0.0).then_inc(init_zero, 1)
            pool.memset(vrow[:], 0.0).then_inc(init_zero, 1)
            pool.wait_ge(init_zero, 2)
            pool.dma_start(xs[:], xr).then_inc(x_in, 16)
            pool.dma_start(vr[V_G1:V_G1 + KT], pre_mix_g[0].rearrange("(k p) -> k p", p=P)).then_inc(vrow_in, 16)
            g2q = pre_ffn_g[0].rearrange("(q k l) -> k q l", q=4, l=QUAD)
            pool.dma_start(vr[V_G2:V_G2 + KT].rearrange("k (q l) -> k q l", q=4), g2q).then_inc(vrow_in, 16)
            pool.dma_start(vr[V_QN:V_KVN], q_norm_g[0].rearrange("(k p) -> k p", p=P)).then_inc(vrow_in, 16)
            pool.dma_start(vr[V_KVN:V_PS], kv_norm_g[0].rearrange("(k p) -> k p", p=P)).then_inc(vrow_in, 16)
            pool.dma_start(vr[V_PS:V_ALL], pool_scale[0].rearrange("(k p) -> k p", p=P)).then_inc(vrow_in, 16)
            pool.dma_start(pos_i[:], positions[0].rearrange("(t p) -> p t", p=P),
                           allow_slow_non_contiguous=True).then_inc(vrow_in, 16)
            for n in range(4):
                pool.wait_ge(row_ready, n + 1)
                pool.dma_start(gate_dram[0:1, n * W:(n + 1) * W], rowbuf[0:1, :]).then_inc(row_stored, 16)
            pool.wait_ge(row_stored, 64)
            pool.wait_ge(o_out, HEADS)
            pool.dma_start(gate1[:], gate_dram[0:1, :].broadcast_to([P, D])).then_inc(g1_in, 16)
            pool.dma_start(post1[:], post_mix_g[0:1, :].broadcast_to([P, D])).then_inc(g1_in, 16)
            pool.wait_ge(x1_done, 1)
            pool.dma_start(x1_dram.rearrange("t p d -> p t d"), x1q[:]).then_inc(x1_stored, 16)
            for n in range(4):
                pool.wait_ge(row_ready, n + 5)
                pool.dma_start(gate_dram[1:2, n * W:(n + 1) * W], rowbuf[0:1, :]).then_inc(row_stored, 16)
            pool.wait_ge(row_stored, 128)
            pool.wait_ge(x1_stored, 16)
            pool.wait_ge(u_used, 2 * TILES)
            pool.dma_start(x1[:], x1_dram.rearrange("t p d -> p t d")).then_inc(tail_in, 16)
            pool.dma_start(gate2[:], gate_dram[1:2, :].broadcast_to([P, D])).then_inc(tail_in, 16)
            pool.dma_start(post2[:], post_ffn_g[0:1, :].broadcast_to([P, D])).then_inc(tail_in, 16)
            for tt in range(TT):
                pool.wait_ge(out_ready, tt + 1)
                pool.dma_start(out[0, tt * P:(tt + 1) * P, :], x1[:, tt, :]).then_inc(out_stored, 16)
            pool.wait_ge(out_stored, 32)

        @block.tensor
        def _(pe):
            def transpose_vectors():
                pe.wait_ge(consts_in, 80)
                pe.wait_ge(vrow_in, 96)
                pe.transpose(ps[:, 1, 0:P], vrow[:, :], ident).then_inc(vec_t, 1)

            def ada_columns(n, quads):
                pe.wait_ge(acc_ready, n + 1)
                b = acc[:, n % 2, :]
                if not quads:
                    for j in range(4):
                        mm = pe.matmul(ps[:, 0, n * 4 + j:n * 4 + j + 1], b[:, j * P:(j + 1) * P],
                                       ones[:, 0:1], start=True, stop=True, skip_group_check=True)
                else:
                    m, q = (n - 12) // 4, (n - 12) % 4
                    for k in range(KT):
                        col = 64 + m * KT + k
                        mm = pe.matmul(ps[q * QUAD:(q + 1) * QUAD, 0, col:col + 1], b[:, k * QUAD:(k + 1) * QUAD],
                                       ones[:, 0:1], start=True, stop=True, skip_group_check=True)
                mm.then_inc(acc_used, 1)

            def ada_row(n, rows_before):
                pe.wait_ge(acc_ready, n + 1)
                if rows_before:
                    pe.wait_ge(row_ready, rows_before)
                pe.matmul(ps[0:1, 1, :], ones[:, 0:1], acc[:, n % 2, :], start=True, stop=True).then_inc(acc_used, 1)

            def turn(src, dst_bank, out_done, k, slots_, done, rhs):
                b, half = dst_bank
                for tt in range(TT):
                    mm = pe.matmul(ps[:, b, half * T + tt * P:half * T + (tt + 1) * P], src(tt), rhs(tt),
                                   start=True, stop=True, skip_group_check=True)
                mm.then_inc(done, 1)

            def mm_group(bank_ap, lhs, rhs, k_tiles):
                for k in range(k_tiles):
                    mm = pe.matmul(bank_ap, lhs(k), rhs(k), start=(k == 0), stop=(k == k_tiles - 1),
                                   skip_group_check=True)
                return mm

            transpose_vectors()
            pe.wait_ge(vec_cols, 1)
            for n in range(8):
                ada_columns(n, False)

            pe.wait_ge(x_in, 16)
            pe.wait_ge(diag1, 2)
            for k in range(KT):
                if k >= 4 and k % 2 == 0:
                    pe.wait_ge(hT_done, k - 2)
                turn(lambda tt: xs[:, tt, k * P:(k + 1) * P], (2 + (k // 2) % 2, k % 2), None, k, 4,
                     xT_done, lambda tt: diag[:, tt, :])

            pe.wait_ge(hT_done, KT)
            for n in range(2):
                ring_arrived(pe, ("win", n))
                w = wide(("win", n))
                for j in range(4):
                    b = 4 + 2 * n + j // 2
                    mm = mm_group(ps[:, b, (j % 2) * T:(j % 2 + 1) * T],
                                  lambda k: w[:, k, j * P:(j + 1) * P], lambda k: hT[:, k, :], KT)
                    mm.then_inc(u_mm, 1)
                ada_row(8 + n, n)
            for n in range(2, 4):
                ring_arrived(pe, ("win", n))
                cols = min(W, POOL_W + LAT - n * W)
                w = wide(("win", n), cols)
                for tt in range(TT):
                    if tt == 0:
                        pe.wait_ge(u_out, 4 * (n - 1))
                    b = 4 + 2 * (n - 2) + tt
                    mm = mm_group(ps[:, b, 0:cols], lambda k: hT[:, k, tt * P:(tt + 1) * P],
                                  lambda k: w[:, k, :], KT)
                    mm.then_inc(lat_mm, 1)
                if n == 2:
                    ada_row(10, 2)

            ring_arrived(pe, ("uq", 0))
            uq_slot = ring[where[("uq", 0)][0]]
            wuq = uq_slot[:, 0:6144].rearrange("p (k h n) -> p k h n", k=4, h=HEADS)
            wpl = uq_slot[:, 6144:8192].rearrange("p (g k n) -> p g k n", g=4, k=2)
            pe.wait_ge(lat_diag, 4)
            for r in range(6):
                if r == 4:
                    pe.wait_ge(cT_out, 2)
                turn(lambda tt: lat[:, tt, r * P:(r + 1) * P], (2 + (r // 2) % 2, r % 2), None, r, 4,
                     cT_mm, lambda tt: diag[:, tt, :] if r < 4 else tmpr[:, tt, 0:P])
            pe.wait_ge(cT_out, 6)
            pe.wait_ge(lat_out, 4)
            for h in range(HEADS):
                b = 4 + h // 2
                mm_group(ps[:, b, (h % 2) * T:(h % 2 + 1) * T], lambda k: wuq[:, k, h, 0:NOPE],
                         lambda k: cT[:, k, :], 4).then_inc(qn_mm, 1)
            for tt in range(TT):
                mm_group(ps[:, 2 + tt, :], lambda k: cT[:, k, tt * P:(tt + 1) * P],
                         lambda k: wuq[:, k, :, NOPE:NOPE + ROPE], 4).then_inc(qpe_mm, 1)
            pe.wait_ge(z_ready, 4)
            for j in range(8):
                g = j // 2
                b = 4 + j // 2
                if j % 2 == 0:
                    pe.wait_ge(qn_out, j + 2)
                mm = mm_group(ps[:, b, (j % 2) * T:(j % 2 + 1) * T],
                              lambda k: wpl[:, g, k, (j % 2) * P:(j % 2 + 1) * P],
                              lambda k: zT[:, 2 * g + k, :], 2)
                mm.then_inc(pool_mm, 1)
            ring_arrived(pe, ("ukv", 0))
            wkv = ring[where[("ukv", 0)][0]][:, 0:4096].rearrange("p (k h n) -> p k h n", k=2, h=HEADS)
            for h in range(HEADS):
                b = 4 + h // 2
                if h % 2 == 0:
                    pe.wait_ge(pool_out, h + 2)
                mm_group(ps[:, b, (h % 2) * T:(h % 2 + 1) * T], lambda k: wkv[:, k, h, 0:NOPE],
                         lambda k: cT[:, 4 + k, :], 2).then_inc(kn_mm, 1)
            for tt in range(TT):
                for hh in range(2):
                    b = 4 + tt * 2 + hh
                    pe.wait_ge(kn_out, 2 * (tt * 2 + hh) + 2)
                    mm_group(ps[:, b, :], lambda k: cT[:, 4 + k, tt * P:(tt + 1) * P],
                             lambda k: wkv[:, k, 4 * hh:4 * hh + 4, NOPE:2 * NOPE], 2).then_inc(v_mm, 1)
            pe.wait_ge(k_roped, 1)
            pe.wait_ge(q_roped, 1)
            for tt in range(TT):
                for p in range(4):
                    pe.transpose(ps[:, 2 + p // 2, (p % 2) * T + tt * P:(p % 2) * T + (tt + 1) * P],
                                 qrope[:, tt, p * P:(p + 1) * P], ident)
                mm = pe.transpose(ps[:, 0, T + tt * P:T + (tt + 1) * P], krope[:, tt, :], ident)
            mm.then_inc(qpeT_mm, 1)
            ada_row(11, 3)

            pe.wait_ge(qpeT_out, 1)
            pe.wait_ge(kn_out, HEADS)
            pe.wait_ge(qn_out, HEADS)

            def scores(h):
                b = 4 + h % 2
                if h < 2:
                    pe.wait_ge(v_out, h + 1)
                else:
                    pe.wait_ge(s_max, h - 1)
                r0 = (h % 2) * ROPE
                for qb in range(TT):
                    kend = (qb + 1) * P
                    o = ps[:, b, qb * P:qb * P + kend]
                    pe.matmul(o, qnT[:, h, qb * P:(qb + 1) * P], knT[:, h, 0:kend], start=True, stop=False,
                              skip_group_check=True)
                    mm = pe.matmul(o, qpeT[r0:r0 + ROPE, h // 2, qb * P:(qb + 1) * P],
                                   kpeT[r0:r0 + ROPE, 0:kend], start=False, stop=True, skip_group_check=True)
                mm.then_inc(s_mm, 1)

            def turn_probs(h):
                b = 6 + h % 2
                if h < 2:
                    pe.wait_ge(v_out, h + 3)
                pe.wait_ge(s_norm, h + 1)
                if h >= 2:
                    pe.wait_ge(pT_out, h - 1)
                for j in range(3):
                    mm = pe.transpose(ps[:, b, j * P:(j + 1) * P], s_sb[:, h % 2, j * P:(j + 1) * P], ident)
                mm.then_inc(pT_mm, 1)

            def mix(h):
                b = 2 + h % 2
                pe.wait_ge(pT_out, h + 1)
                if h >= 2:
                    pe.wait_ge(o_out, h - 1)
                v0, v1 = (vv[:, t, h * P:(h + 1) * P] for t in range(2))
                pe.matmul(ps[:, b, 0:P], v0, pT[:, h % 2, 0:P], start=True, stop=True, skip_group_check=True)
                pe.matmul(ps[:, b, P:T], v0, pT[:, h % 2, P:T], start=True, stop=False, skip_group_check=True)
                pe.matmul(ps[:, b, P:T], v1, pT[:, h % 2, T:T + P], start=False, stop=True,
                          skip_group_check=True).then_inc(o_mm, 1)

            pe.wait_ge(v_out, 4)
            for h in range(HEADS + 1):
                if h < HEADS:
                    scores(h)
                if h >= 1:
                    turn_probs(h - 1)
                    mix(h - 1)
            ada_columns(12, True)
            ada_columns(13, True)

            pe.wait_ge(o_out, HEADS)
            for n in range(4):
                ring_arrived(pe, ("wout", n))
                w = wide(("wout", n))
                for tt in range(TT):
                    b = 4 + (n % 2) * 2 + tt
                    if n >= 2:
                        pe.wait_ge(y_out, (n - 2) * 2 + tt + 1)
                    mm_group(ps[:, b, :], lambda k: catT[:, k, tt * P:(tt + 1) * P],
                             lambda k: w[:, k, :], KT).then_inc(y_mm, 1)
                if n < 3:
                    ada_columns(14 + n, True)
            for n in range(17, 20):
                ada_columns(n, True)

            for n in range(20, 24):
                ada_row(n, n - 16)
            pe.wait_ge(diag2, 2)
            for k in range(KT):
                if k >= 4 and k % 2 == 0:
                    pe.wait_ge(h2_out, k - 2)
                turn(lambda tt: x1q[:, tt, k * P:(k + 1) * P],
                     (2 + (k // 2) % 2, k % 2), None, k, 4, x1T_mm, lambda tt: diag[:, tt, :])

            pe.wait_ge(h2_out, KT)
            for n in range(4):
                ring_arrived(pe, ("wq", n))
                w = wide(("wq", n))
                for j in range(4):
                    i = 4 * n + j
                    b = 4 + (i // 2) % 4
                    if i >= 8 and i % 2 == 0:
                        pe.wait_ge(qT_out, i - 6)
                    mm_group(ps[:, b, (i % 2) * T:(i % 2 + 1) * T], lambda k: w[:, k, j * P:(j + 1) * P],
                             lambda k: h2T[:, k, :], KT).then_inc(qT_mm, 1)
            ring_arrived(pe, ("keys", 0))
            keys = ring[where[("keys", 0)][0]][:, 0:2048].rearrange("p (k n) -> p k n", k=KT)
            for i in range(KT):
                b = 2 + (i // 4) % 2
                if i >= 8:
                    pe.wait_ge(key_out, i // 4 - 1)
                mm = pe.transpose(ps[:, b, (i % 4) * P:(i % 4 + 1) * P], keys[:, i, :], ident)
                if i % 4 == 3:
                    mm.then_inc(key_mm, 1)
            pe.wait_ge(qT_out, KT)
            pe.wait_ge(key_out, 4)
            for j in range(8):
                b = 4 + j % 4
                if j >= 4:
                    pe.wait_ge(sc_out, j - 3)
                for i in range(4):
                    tt, hp = j // 4, (j % 4) * 4 + i
                    mm = pe.matmul(ps[:, b, i * P:(i + 1) * P], qT[:, hp, tt * P:(tt + 1) * P], keyT[:, hp, :],
                                   start=True, stop=True, skip_group_check=True)
                mm.then_inc(sc_mm, 1)
            pe.wait_ge(slots_ready, 1)
            for m in range(3):
                for tt in range(TT):
                    mm = pe.transpose(ps[:, 2 + m // 2, (m % 2) * T + tt * P:(m % 2) * T + (tt + 1) * P],
                                      slots[:, m, tt, :], ident)
            mm.then_inc(slot_mm, 1)
            pe.wait_ge(slotT_out, 1)

            def split3(o, lh, ll, rh, rl, start, stop):
                pe.matmul(o, lh, rh, start=start, stop=False, skip_group_check=True)
                pe.matmul(o, lh, rl, start=False, stop=False, skip_group_check=True)
                return pe.matmul(o, ll, rh, start=False, stop=stop, skip_group_check=True)

            def u_tile(tile, bank, first):
                if not first:
                    pe.wait_ge(a_out, tile - 2)
                for h in range(2):
                    slot = (2 * bank + h) % RING
                    pe.wait_ge(u_lo, tile * 2 + (h + 1))
                    for k in range(KT // 2):
                        kk = h * (KT // 2) + k
                        mm = split3(ps[:, bank, 0:T], eH[:, slot, k * P:(k + 1) * P], eL[:, slot, k * P:(k + 1) * P],
                                    h2H[:, kk, :], h2L[:, kk, :], kk == 0, kk == KT - 1)
                    mm.then_inc(u_used, 1)

            pe.wait_ge(h2L_out, KT)
            pe.wait_ge(h2H_out, KT)
            for j in range(3):
                u_tile(j, j, True)
            with pe.Fori(1, TILES // 3) as r:
                for j in range(3):
                    u_tile(r * 3 + j, j, False)
            for j in range(2):
                u_tile(TILES - 2 + j, j, False)

            def scatter(g, half, first):
                if not first:
                    pe.wait_ge(gated, g - 1)
                pe.wait_ge(hot_ready, g + 1)
                for t in range(4):
                    mm = pe.matmul(ps[:, half, t * P:(t + 1) * P], hotA[:, half, t, :], hotB[:, half, t, :],
                                   start=True, stop=True, skip_group_check=True)
                mm.then_inc(hot_mm, 1)

            pe.wait_ge(a_out, TILES)
            scatter(0, 0, True)
            scatter(1, 1, True)
            with pe.Fori(1, T // 8) as r:
                scatter(r * 2, 0, False)
                scatter(r * 2 + 1, 1, False)

            def v_tile(tile, j, start, stop):
                pe.wait_ge(act_lo, tile + 1)
                for h in range(2):
                    slot = (2 * j + h) % RING
                    pe.wait_ge(v_lo, tile * 2 + (h + 1))
                    for tt in range(TT):
                        lh, ll = (a[j][:, tt * P:(tt + 1) * P] for a in (aH, aL))
                        o = [ps[:, tt * 4 + h * 2 + n, :] for n in range(2)]
                        vh, vl = ([e[:, slot, n * W:(n + 1) * W] for n in range(2)] for e in (eH, eL))
                        for n in range(2):
                            pe.matmul(o[n], lh, vh[n], start=start, stop=False, skip_group_check=True)
                            pe.matmul(o[n], lh, vl[n], start=False, stop=False, skip_group_check=True)
                        for n in range(2):
                            mm = pe.matmul(o[n], ll, vh[n], start=False, stop=stop, skip_group_check=True)
                    mm.then_inc(v_used, 1)

            pe.wait_ge(gated, T // 4)
            for j in range(3):
                v_tile(j, j, j == 0, False)
            with pe.Fori(1, TILES // 3) as r:
                for j in range(3):
                    v_tile(r * 3 + j, j, False, False)
            v_tile(TILES - 2, 0, False, False)
            v_tile(TILES - 1, 1, False, True)

        @block.scalar
        def _(act):
            count = [0]

            def seq(ins):
                count[0] += 1
                ins.then_inc(act_chain, 1)
                act.wait_ge(act_chain, count[0])

            act.wait_ge(c_in, 16)
            act.activation(c_act[:], c_col[:], ACT.Silu).then_inc(silu_done, 1)
            act.wait_ge(x_in, 16)
            for tt in range(TT):
                seq(act.activation(hT[:].rearrange("p k t -> p (k t)")[:, 0:D], xs[:, tt, :], ACT.Square,
                                   accum_out=stat[:, tt:tt + 1]))
            act.nop().then_inc(x_sq, 1)
            act.wait_ge(trig_arg, 1)
            act.activation(trig[:, 0].rearrange("p t f -> p (t f)"), ang[:, 2, :], ACT.Sin).then_inc(trig_ready, 1)
            act.activation(trig[:, 1].rearrange("p t f -> p (t f)"), ang[:, 1, :], ACT.Sin).then_inc(trig_ready, 1)
            act.wait_ge(x_rs, 1)
            act.activation(stat[:, 4:6], stat[:, 2:4], ACT.Sqrt).then_inc(x_rs, 1)
            act.wait_ge(mod1_ready, 2)
            act.wait_ge(act_chain, count[0])
            for k in range(KT):
                act.wait_ge(xT_done, pair(k))
                b, half = 2 + (k // 2) % 2, k % 2
                act.activation(hT[:, k, :], ps[:, b, half * T:(half + 1) * T], ACT.Identity,
                               bias=mod1[:, 1, k:k + 1], scale=mod1[:, 0, k:k + 1]).then_inc(hT_done, 1)

            def gate_row(n, stored):
                act.wait_ge(acc_used, n + 1)
                if stored:
                    act.wait_ge(row_stored, stored)
                act.copy(rowbuf[0:1, :], ps[0:1, 1, :]).then_inc(row_ready, 1)

            for j in range(8):
                act.wait_ge(u_mm, pair(j))
                act.copy(uT[:, j, :], ps[:, 4 + j // 2, (j % 2) * T:(j % 2 + 1) * T]).then_inc(u_out, 1)
                if j % 4 == 3:
                    gate_row(8 + j // 4, 16 * (j // 4))
            for n in range(2):
                cols = W if n == 0 else LAT - W
                for tt in range(TT):
                    act.wait_ge(lat_mm, 2 * n + tt + 1)
                    act.copy(lat[:, tt, n * W:n * W + cols], ps[:, 4 + 2 * n + tt, 0:cols]).then_inc(lat_out, 1)
                    r = QR if n == 0 else KVR
                    seq(act.activation(qrope[:, 0, 0:r], ps[:, 4 + 2 * n + tt, 0:r], ACT.Square,
                                       accum_out=stat[:, 8 + 2 * n + tt:9 + 2 * n + tt]))
                if n == 0:
                    gate_row(10, 32)
            act.nop().then_inc(lat_sq, 1)
            act.wait_ge(lat_sq, 2)
            act.activation(stat[:, 16:20], stat[:, 12:16], ACT.Sqrt).then_inc(lat_sq, 1)
            for r in range(6):
                act.wait_ge(cT_mm, pair(r))
                act.activation(cT[:, r, :], ps[:, 2 + (r // 2) % 2, (r % 2) * T:(r % 2 + 1) * T], ACT.Identity,
                               scale=vcols[:, V_QN + r:V_QN + r + 1]).then_inc(cT_out, 1)
            for h in range(HEADS):
                act.wait_ge(qn_mm, pair(h))
                if h == 0:
                    act.wait_ge(u_mm, 8)
                act.copy(qnT[:, h, :], ps[:, 4 + h // 2, (h % 2) * T:(h % 2 + 1) * T]).then_inc(qn_out, 1)
            for j in range(8):
                act.wait_ge(pool_mm, pair(j))
                act.activation(catT[:, j, :], ps[:, 4 + j // 2, (j % 2) * T:(j % 2 + 1) * T], ACT.Identity,
                               scale=vcols[:, V_PS + j:V_PS + j + 1]).then_inc(pool_out, 1)
            for h in range(HEADS):
                act.wait_ge(kn_mm, pair(h))
                act.copy(knT[:, h, :], ps[:, 4 + h // 2, (h % 2) * T:(h % 2 + 1) * T]).then_inc(kn_out, 1)
            for j in range(4):
                act.wait_ge(v_mm, j + 1)
                act.copy(vv[:, j // 2, (j % 2) * W:(j % 2 + 1) * W], ps[:, 4 + j, :]).then_inc(v_out, 1)
            act.wait_ge(qpeT_mm, 1)
            seq(act.copy(qpeT[:].rearrange("p a t -> p (a t)"), ps[:, 2:4, :].rearrange("p a t -> p (a t)")))
            seq(act.copy(kpeT[:], ps[:, 0, T:2 * T]))
            act.nop().then_inc(qpeT_out, 1)
            gate_row(11, 48)

            def exps(h):
                act.wait_ge(s_max, h + 1)
                for qb in range(TT):
                    s = s_sb[:, h % 2, qb * P:qb * P + (qb + 1) * P]
                    e = act.activation(s, s, ACT.Exp, bias=stat[:, 20 + 2 * (h % 2) + qb:21 + 2 * (h % 2) + qb],
                                       accum_out=stat[:, 24 + 2 * (h % 2) + qb:25 + 2 * (h % 2) + qb])
                    e.then_inc(s_exp, 1)

            def outs(h):
                act.wait_ge(pT_mm, h + 1)
                if h >= 2:
                    act.wait_ge(o_mm, h - 1)
                act.copy(pT[:, h % 2, :], ps[:, 6 + h % 2, 0:3 * P]).then_inc(pT_out, 1)
                act.wait_ge(o_mm, h + 1)
                act.copy(catT[:, 8 + h, :], ps[:, 2 + h % 2, 0:T]).then_inc(o_out, 1)

            for h in range(HEADS + 1):
                if h < HEADS:
                    exps(h)
                if h >= 1:
                    outs(h - 1)

            for n in range(4):
                for tt in range(TT):
                    act.wait_ge(y_mm, 2 * n + tt + 1)
                    b = 4 + (n % 2) * 2 + tt
                    if n == 0 and tt == 0:
                        act.wait_ge(s_mm, HEADS)
                    seq(act.activation(y1[:, tt, n * W:(n + 1) * W], ps[:, b, :], ACT.Square,
                                       accum_out=stat[:, 28 + tt * 4 + n:29 + tt * 4 + n]))
                    act.copy(y1[:, tt, n * W:(n + 1) * W], ps[:, b, :]).then_inc(y_out, 1)
            act.wait_ge(y_rc, 1)
            act.activation(stat[:, 38:40], stat[:, 36:38], ACT.Sqrt).then_inc(y_rs, 1)
            for n in range(4):
                gate_row(20 + n, 64 + 16 * n)
            act.wait_ge(x1_done, 1)
            for tt in range(TT):
                seq(act.activation(junk[:], x1q[:, tt, :], ACT.Square, accum_out=stat[:, 40 + tt:41 + tt]))
            act.nop().then_inc(x1_sq, 1)
            act.wait_ge(x1_rs, 1)
            act.activation(stat[:, 44:46], stat[:, 42:44], ACT.Sqrt).then_inc(x1_rs, 1)
            act.wait_ge(mod2_ready, 2)
            for k in range(KT):
                act.wait_ge(x1T_mm, pair(k))
                b, half = 2 + (k // 2) % 2, k % 2
                act.activation(h2T[:, k, :], ps[:, b, half * T:(half + 1) * T], ACT.Identity,
                               bias=mod2[:, 1, k:k + 1], scale=mod2[:, 0, k:k + 1]).then_inc(h2_out, 1)
                if k == 0:
                    act.wait_ge(y_mm, 8)
                act.wait_ge(h2_out, k + 1)
                act.copy(h2H[:, k, :], h2T[:, k, :]).then_inc(h2H_out, 1)
            act.wait_ge(x1_stored, 16)
            act.wait_ge(x1T_mm, KT)
            for i in range(KT):
                act.wait_ge(qT_mm, pair(i))
                act.copy(qT[:, i, :], ps[:, 4 + (i // 2) % 4, (i % 2) * T:(i % 2 + 1) * T]).then_inc(qT_out, 1)
            for j in range(4):
                act.wait_ge(key_mm, j + 1)
                act.copy(keyT[:, 4 * j:4 * j + 4, :].rearrange("p k n -> p (k n)"),
                         ps[:, 2 + j % 2, :]).then_inc(key_out, 1)
            for j in range(8):
                act.wait_ge(sc_mm, j + 1)
                act.copy(sc[:, j // 4, (j % 4) * 4:(j % 4) * 4 + 4, :].rearrange("p k n -> p (k n)"),
                         ps[:, 4 + j % 4, :]).then_inc(sc_out, 1)
            act.wait_ge(g_shift, 1)
            act.activation(gtmp[:], gtmp[:], ACT.Exp).then_inc(g_exp, 1)
            act.wait_ge(slot_mm, 1)
            seq(act.copy(slotT[:, 0:2, :].rearrange("p a t -> p (a t)"), ps[:, 2, :]))
            act.copy(slotT[:, 2, :], ps[:, 3, 0:T]).then_inc(slotT_out, 1)

            def gelu(tile, bank):
                act.wait_ge(u_used, tile * 2 + 2)
                act.activation(acts[:, bass.ds(tile, 1), :], ps[:, bank, 0:T], ACT.Gelu).then_inc(a_out, 1)

            def u_high(g, slot, first):
                act.wait_ge(u_tr, g + 1)
                if not first:
                    act.wait_ge(u_used, g - (RING - 1))
                act.copy(by_k(eH[:, slot, :]), turned(raw[:, slot, :])).then_inc(u_hi, 1)

            act.wait_ge(sc_mm, 8)
            act.wait_ge(qT_mm, KT)
            act.wait_ge(route_done, 1)

            def u_tile(tile, j, first):
                u_high(tile * 2, (2 * j) % RING, first and j < 2)
                u_high(tile * 2 + 1, (2 * j + 1) % RING, first and j < 1)
                if not (first and j == 0):
                    gelu(tile - 1, (j - 1) % 3)

            for j in range(3):
                u_tile(j, j, True)
            with act.Fori(1, TILES // 3) as r:
                for j in range(3):
                    u_tile(r * 3 + j, j, False)
            for j in range(2):
                u_tile(TILES - 2 + j, j, False)
            gelu(TILES - 1, 1)

            def v_tile(tile, j, first, rounds):
                if not first:
                    act.wait_ge(v_used, tile * 2 - 4)
                act.copy(aH[j][:], acts[:, bass.ds(tile, 1), :]).then_inc(act_hi, 1)
                for h in range(2):
                    g = 2 * j + h
                    slot = g % RING
                    act.wait_ge(v_in[slot], rounds(g))
                    if not (first and g < RING):
                        act.wait_ge(v_used, tile * 2 + (h - RING + 1))
                    act.copy(eH[:, slot, :], raw[:, slot, :]).then_inc(v_hi, 1)

            act.wait_ge(gated, T // 4)
            act.wait_ge(hot_mm, T // 4)
            for j in range(3):
                v_tile(j, j, True, lambda g: 16 * (g // RING + 1))
            with act.Fori(1, TILES // 3) as r:
                for j in range(3):
                    v_tile(r * 3 + j, j, False, lambda g: r * 32 + 16 * (g // RING + 1))
            for j in range(2):
                v_tile(TILES - 2 + j, j, False, lambda g: 32 * (TILES // 3) + 16 * (g // RING + 1))

            act.wait_ge(v_used, 2 * TILES)
            for tt in range(TT):
                seq(act.activation(raw[:, 0:2, :].rearrange("p a b -> p (a b)"),
                                   ps[:, 4 * tt:4 * tt + 4, :].rearrange("p a b -> p (a b)"), ACT.Square,
                                   accum_out=stat[:, 46 + tt:47 + tt]))
            act.nop().then_inc(y2_sq, 1)
            act.wait_ge(y2_rc, 1)
            act.activation(stat[:, 50:52], stat[:, 48:50], ACT.Sqrt).then_inc(y2_rs, 1)

        @block.vector
        def _(dve):
            count = [0]

            def seq(ins):
                count[0] += 1
                ins.then_inc(dve_chain, 1)
                dve.wait_ge(dve_chain, count[0])

            def ada(n):
                ring_arrived(dve, ("ada", n))
                dve.wait_ge(init_in[n % 2], 16 * (n // 2 + 1))
                if n >= 2:
                    dve.wait_ge(acc_used, n - 1)
                w = wide(("ada", n))
                a = acc[:, n % 2, :]
                for k in range(KT):
                    ins = dve.scalar_tensor_tensor(a, w[:, k, :], c_act[:, k:k + 1],
                                                   init[:, n % 2, :] if k == 0 else a, ALU.mult, ALU.add)
                    if k < KT - 1:
                        seq(ins)
                ins.then_inc(acc_ready, 1)

            def inverse_mean(dst, src, width):
                seq(dve.tensor_scalar(dst, src, 1.0 / width, EPS, ALU.mult, ALU.add))
                seq(dve.reciprocal(dst, dst))

            dve.wait_ge(vec_t, 1)
            seq(dve.tensor_copy(vcols[:], ps[:, 1, 0:V_ALL]))
            dve.nop().then_inc(vec_cols, 1)
            seq(dve.tensor_copy(pos_f[:], pos_i[:]))
            for tt in range(TT):
                seq(dve.tensor_scalar(ang[:, 0, tt * HALF:(tt + 1) * HALF], freq[:], pos_f[:, tt:tt + 1], None,
                                      ALU.mult))
            magic = 12582912.0
            seq(dve.tensor_scalar(ang[:, 3, :], ang[:, 0, :], 1.0 / (TWO_PI_A + TWO_PI_B + TWO_PI_C), None, ALU.mult))
            seq(dve.tensor_scalar(ang[:, 3, :], ang[:, 3, :], magic, None, ALU.add))
            seq(dve.tensor_scalar(ang[:, 3, :], ang[:, 3, :], magic, None, ALU.subtract))
            seq(dve.scalar_tensor_tensor(ang[:, 1, :], ang[:, 3, :], -TWO_PI_A, ang[:, 0, :], ALU.mult, ALU.add))
            seq(dve.scalar_tensor_tensor(ang[:, 1, :], ang[:, 3, :], -TWO_PI_B, ang[:, 1, :], ALU.mult, ALU.add))
            seq(dve.scalar_tensor_tensor(ang[:, 1, :], ang[:, 3, :], -TWO_PI_C, ang[:, 1, :], ALU.mult, ALU.add))
            pi = 3.1415925
            seq(dve.tensor_scalar(ang[:, 1, :], ang[:, 1, :], pi, -pi, ALU.min, ALU.max))
            seq(dve.tensor_scalar(ang[:, 2, :], ang[:, 1, :], -1.0, None, ALU.mult))
            seq(dve.tensor_tensor(ang[:, 2, :], ang[:, 2, :], ang[:, 1, :], ALU.max))
            seq(dve.tensor_scalar(ang[:, 2, :], ang[:, 2, :], -1.0, 1.5707963267948966, ALU.mult, ALU.add))
            dve.nop().then_inc(trig_arg, 1)

            dve.wait_ge(silu_done, 1)
            for n in range(2):
                ada(n)
            dve.wait_ge(x_sq, 1)
            inverse_mean(stat[:, 2:4], stat[:, 0:2], D)
            dve.nop().then_inc(x_rs, 1)
            for n in range(2, 4):
                ada(n)
            dve.wait_ge(x_rs, 2)
            for tt in range(TT):
                seq(dve.tensor_scalar(diag[:, tt, :], ident, stat[:, 4 + tt:5 + tt], None, ALU.mult))
                dve.nop().then_inc(diag1, 1)
            for n in range(4, 8):
                ada(n)
            dve.wait_ge(acc_used, 8)
            seq(dve.tensor_copy(mod1[:, 1, :], ps[:, 0, 0:KT]))
            dve.nop().then_inc(mod1_ready, 1)
            seq(dve.scalar_tensor_tensor(mod1[:, 0, :], ps[:, 0, KT:2 * KT], 1.0, vcols[:, V_G1:V_G1 + KT],
                                         ALU.add, ALU.mult))
            dve.nop().then_inc(mod1_ready, 1)
            for n in range(8, 10):
                ada(n)

            t2, t4 = zT, uT
            dve.wait_ge(u_out, 8)
            for g, w in enumerate(WINDOWS):
                u = uT[:, 2 * g:2 * g + 2, :]
                z = zT[:, 2 * g:2 * g + 2, :]
                s = pool_tmp = [catT[:, 0:2, :], catT[:, 2:4, :]]
                src = u
                step = 1
                i = 0
                while step < w:
                    d = s[i % 2]
                    seq(dve.tensor_copy(d[:, :, 0:step], src[:, :, 0:step]))
                    seq(dve.tensor_tensor(d[:, :, step:T], src[:, :, step:T], src[:, :, 0:T - step], ALU.add))
                    src = d
                    step *= 2
                    i += 1
                seq(dve.scalar_tensor_tensor(z, src, 1.0 / w, u, ALU.mult, ALU.subtract))
                for ct in range(2):
                    o = s[i % 2][:, ct, 0:16]
                    seq(dve.tensor_tensor(o, src[:, ct, 0:16], cnt[:, g, :], ALU.mult))
                    seq(dve.tensor_tensor(z[:, ct, 0:16], o, u[:, ct, 0:16], ALU.subtract))
                dve.nop().then_inc(z_ready, 1)
            ada(10)

            dve.wait_ge(lat_sq, 1)
            seq(dve.tensor_scalar(stat[:, 12:14], stat[:, 8:10], 1.0 / QR, EPS, ALU.mult, ALU.add))
            seq(dve.tensor_scalar(stat[:, 14:16], stat[:, 10:12], 1.0 / KVR, EPS, ALU.mult, ALU.add))
            seq(dve.reciprocal(stat[:, 12:16], stat[:, 12:16]))
            dve.nop().then_inc(lat_sq, 1)
            dve.wait_ge(lat_sq, 3)
            dve.wait_ge(xT_done, KT)
            for tt in range(TT):
                seq(dve.tensor_scalar(diag[:, tt, :], ident, stat[:, 16 + tt:17 + tt], None, ALU.mult))
                dve.nop().then_inc(lat_diag, 1)
                seq(dve.tensor_scalar(tmpr[:, tt, 0:P], ident, stat[:, 18 + tt:19 + tt], None, ALU.mult))
                dve.nop().then_inc(lat_diag, 1)
            dve.wait_ge(trig_ready, 2)
            dve.wait_ge(lat_out, 4)

            def rotate(dst, src, tt, heads, t1):
                cos, sin = (trig[:, i, tt, :].unsqueeze(1).broadcast_to([P, heads, HALF]) for i in range(2))
                x1_, x2_ = src[:, :, 0:HALF], src[:, :, HALF:ROPE]
                tv = t1[:, 0:heads * HALF].rearrange("p (h f) -> p h f", h=heads)
                seq(dve.tensor_tensor(tv, x2_, sin, ALU.mult))
                seq(dve.tensor_tensor(dst[:, :, 0:HALF], x1_, cos, ALU.mult))
                seq(dve.tensor_tensor(dst[:, :, 0:HALF], dst[:, :, 0:HALF], tv, ALU.subtract))
                seq(dve.tensor_tensor(tv, x1_, sin, ALU.mult))
                seq(dve.tensor_tensor(dst[:, :, HALF:ROPE], x2_, cos, ALU.mult))
                seq(dve.tensor_tensor(dst[:, :, HALF:ROPE], dst[:, :, HALF:ROPE], tv, ALU.add))

            for tt in range(TT):
                kp = krope[:, tt, :].rearrange("p (h f) -> p h f", h=2)
                rotate(kp[:, 0:1, :], lat[:, tt, QR + KVR:LAT].rearrange("p (h f) -> p h f", h=1), tt, 1,
                       ang[:, 0, :])
                seq(dve.tensor_copy(kp[:, 1:2, :], kp[:, 0:1, :]))
            dve.nop().then_inc(k_roped, 1)
            dve.wait_ge(qpe_mm, 2)
            dve.wait_ge(cT_mm, 6)
            for tt in range(TT):
                rotate(qrope[:, tt, :].rearrange("p (h f) -> p h f", h=HEADS),
                       ps[:, 2 + tt, :].rearrange("p (h f) -> p h f", h=HEADS), tt, HEADS, tmpr[:, 0, :])
            dve.nop().then_inc(q_roped, 1)
            ada(11)

            def maxima(h):
                dve.wait_ge(s_mm, h + 1)
                if h >= 2:
                    dve.wait_ge(pT_mm, h - 1)
                s = s_sb[:, h % 2, :]
                seq(dve.scalar_tensor_tensor(s, ps[:, 4 + h % 2, 0:3 * P], SCALE, mask[:], ALU.mult, ALU.add))
                for qb in range(TT):
                    m = stat[:, 20 + 2 * (h % 2) + qb:21 + 2 * (h % 2) + qb]
                    seq(dve.tensor_reduce(m, s[:, qb * P:qb * P + (qb + 1) * P], AX_X, ALU.max, negate=True))
                dve.nop().then_inc(s_max, 1)

            def normalise(h):
                dve.wait_ge(s_exp, 2 * (h + 1))
                r = stat[:, 24 + 2 * (h % 2):26 + 2 * (h % 2)]
                seq(dve.reciprocal(r, r))
                for qb in range(TT):
                    s = s_sb[:, h % 2, qb * P:qb * P + (qb + 1) * P]
                    seq(dve.tensor_scalar(s, s, r[:, qb:qb + 1], None, ALU.mult))
                dve.nop().then_inc(s_norm, 1)

            for h in range(HEADS + 1):
                if h < HEADS:
                    maxima(h)
                if h >= 1:
                    normalise(h - 1)
            for n in range(12, 20):
                ada(n)

            dve.wait_ge(acc_used, 20)
            seq(dve.tensor_copy(mod2[:, 1, :], ps[:, 0, 64:64 + KT]))
            dve.nop().then_inc(mod2_ready, 1)
            seq(dve.scalar_tensor_tensor(mod2[:, 0, :], ps[:, 0, 64 + KT:64 + 2 * KT], 1.0,
                                         vcols[:, V_G2:V_G2 + KT], ALU.add, ALU.mult))
            dve.nop().then_inc(mod2_ready, 1)
            dve.wait_ge(g1_in, 32)
            seq(dve.tensor_tensor(gate1[:], gate1[:], post1[:], ALU.mult))
            dve.wait_ge(y_out, 8)
            for tt in range(TT):
                seq(dve.tensor_reduce(stat[:, 36 + tt:37 + tt], stat[:, 28 + 4 * tt:32 + 4 * tt], AX_X, ALU.add))
            inverse_mean(stat[:, 36:38], stat[:, 36:38], D)
            dve.nop().then_inc(y_rc, 1)
            dve.wait_ge(y_rs, 1)
            for tt in range(TT):
                seq(dve.scalar_tensor_tensor(y1[:, tt, :], y1[:, tt, :], stat[:, 38 + tt:39 + tt], gate1[:],
                                             ALU.mult, ALU.mult))
                seq(dve.tensor_tensor(x1q[:, tt, :].rearrange("p (k q l) -> p q k l", q=4, l=QUAD),
                                      xs[:, tt, :].rearrange("p (q k l) -> p q k l", q=4, l=QUAD),
                                      y1[:, tt, :].rearrange("p (q k l) -> p q k l", q=4, l=QUAD), ALU.add))
            dve.nop().then_inc(x1_done, 1)
            for n in range(20, 24):
                ada(n)
            dve.wait_ge(x1_sq, 1)
            inverse_mean(stat[:, 42:44], stat[:, 40:42], D)
            dve.nop().then_inc(x1_rs, 1)
            dve.wait_ge(x1_rs, 2)
            dve.wait_ge(cT_mm, 6)
            for tt in range(TT):
                seq(dve.tensor_scalar(diag[:, tt, :], ident, stat[:, 44 + tt:45 + tt], None, ALU.mult))
                dve.nop().then_inc(diag2, 1)
            for k in range(KT):
                dve.wait_ge(h2H_out, k + 1)
                dve.tensor_tensor(h2L[:, k, :], h2T[:, k, :], h2H[:, k, :].bitcast(F32),
                                  ALU.subtract).then_inc(h2L_out, 1)

            for tt in range(TT):
                for hp in range(KT):
                    if hp % 4 == 0:
                        dve.wait_ge(sc_out, tt * 4 + hp // 4 + 1)
                    s = sc[:, tt, hp, :]
                    a, b = s16[:, tt, hp, 0:8], s16[:, tt, hp, 8:16]
                    seq(dve.max(a, s))
                    seq(dve.max_index(i16u[:, tt, hp, 0:8], a, s))
                    seq(dve.match_replace(tmpk[:, 0:NK], a, s, -BIG))
                    seq(dve.max(b, tmpk[:, 0:NK]))
                    seq(dve.max_index(i16u[:, tt, hp, 8:16], b, tmpk[:, 0:NK]))
            seq(dve.tensor_copy(i16f[:], i16u[:]))
            for tt in range(TT):
                for h in range(PH):
                    cand = tmpk[:, 0:256]
                    s0 = s16[:, tt, 2 * h, :].unsqueeze(2).broadcast_to([P, TOPK, TOPK])
                    s1 = s16[:, tt, 2 * h + 1, :].unsqueeze(1).broadcast_to([P, TOPK, TOPK])
                    seq(dve.tensor_tensor(cand.rearrange("p (a b) -> p a b", a=TOPK), s0, s1, ALU.add))
                    a, b = (best[:, tt, h * TOPK + o:h * TOPK + o + 8] for o in (0, 8))
                    ia, ib = (posu[:, tt, h * TOPK + o:h * TOPK + o + 8] for o in (0, 8))
                    seq(dve.max(a, cand))
                    seq(dve.max_index(ia, a, cand))
                    seq(dve.match_replace(tmpk[:, 256:512], a, cand, -BIG))
                    seq(dve.max(b, tmpk[:, 256:512]))
                    seq(dve.max_index(ib, b, tmpk[:, 256:512]))
            bv = best[:].rearrange("p t (h k) -> p (t h) k", h=PH)
            gv = gtmp[:].rearrange("p t (h k) -> p (t h) k", h=PH)
            n_h = TT * PH
            seq(dve.tensor_tensor(gv, bv, bv[:, :, 0:1].broadcast_to([P, n_h, TOPK]), ALU.subtract))
            dve.nop().then_inc(g_shift, 1)
            dve.wait_ge(g_exp, 1)
            gs = gsum[:].rearrange("p t h -> p (t h)")
            seq(dve.tensor_reduce(gs, gv, AX_X, ALU.add))
            seq(dve.reciprocal(gs, gs))
            seq(dve.tensor_tensor(slots[:, 2].rearrange("p t (h k) -> p (t h) k", h=PH), gv,
                                  gs.unsqueeze(2).broadcast_to([P, n_h, TOPK]), ALU.mult))
            seq(dve.tensor_scalar(posa[:], posu[:], 4, None, ALU.logical_shift_right))
            seq(dve.tensor_copy(posf[:, 0], posa[:]))
            seq(dve.tensor_scalar(posa[:], posu[:], 15, None, ALU.bitwise_and))
            seq(dve.tensor_copy(posf[:, 1], posa[:]))
            for tt in range(TT):
                for p in range(2):
                    eq = tmpk[:].rearrange("p (h k a) -> p h k a", h=PH, k=TOPK)
                    pr = tmpk2[:].rearrange("p (h k a) -> p h k a", h=PH, k=TOPK)
                    pf = posf[:, p, tt, :].rearrange("p (h k) -> p h k", h=PH).unsqueeze(3)
                    seq(dve.tensor_tensor(
                        eq.rearrange("p h k a -> p (h k) a"),
                        posf[:, p, tt, :].unsqueeze(2).broadcast_to([P, PH * TOPK, TOPK]),
                        i16[:].unsqueeze(1).broadcast_to([P, PH * TOPK, TOPK]), ALU.is_equal))
                    tab = i16f[:, tt].rearrange("p (h s) a -> p h s a", s=2)[:, :, p, :]
                    seq(dve.tensor_tensor(pr, eq, tab.unsqueeze(2).broadcast_to([P, PH, TOPK, TOPK]), ALU.mult))
                    seq(dve.tensor_reduce(slots[:, p, tt, :], pr.rearrange("p h k a -> p (h k) a"), AX_X, ALU.add))
            dve.nop().then_inc(slots_ready, 1)
            dve.nop().then_inc(route_done, 1)

            def transpose_u(g, slot, rounds):
                dve.wait_ge(raw_in[slot], rounds)
                dve.transpose(raw[:, slot, :], raw[:, slot, :]).then_inc(u_tr, 1)

            def u_low(g, slot, first=False):
                dve.wait_ge(u_hi, g + 1)
                if not first:
                    dve.wait_ge(u_used, g - (RING - 1))
                dve.tensor_tensor(by_k(eL[:, slot, :]), turned(raw[:, slot, :]),
                                  by_k(eH[:, slot, :].bitcast(F32)), ALU.subtract).then_inc(u_lo, 1)

            dve.wait_ge(slot_mm, 1)
            for j in range(6):
                transpose_u(j, j % RING, 64 * (j // RING + 1))
                if j >= 1:
                    u_low(j - 1, (j - 1) % RING, j <= RING)
            with dve.Fori(1, TILES // 3) as r:
                for j in range(6):
                    transpose_u(r * 6 + j, j % RING, r * 128 + 64 * (j // RING + 1))
                    u_low(r * 6 + (j - 1), (j - 1) % RING)
            last = 2 * (TILES - 2)
            for j in range(4):
                transpose_u(last + j, j % RING, 128 * (TILES // 3) + 64 * (j // RING + 1))
                u_low(last + j - 1, (j - 1) % RING)
            u_low(2 * TILES - 1, 3 % RING)

            def hots(g, half, first):
                if not first:
                    dve.wait_ge(hot_mm, g - 1)
                for t in range(4):
                    i1, i2, gt = (slotT[:, m, bass.ds(g * 4 + t, 1)] for m in (0, 1, 2))
                    dve.tensor_scalar(hotA[:, half, t, :], iota, i2, None, ALU.is_equal)
                    last_ = dve.tensor_scalar(hotB[:, half, t, :], iota, i1, gt, ALU.is_equal, ALU.mult)
                last_.then_inc(hot_ready, 1)

            def apply_gates(g, half):
                dve.wait_ge(hot_mm, g + 1)
                a = acts[:, :, bass.ds(g * 4, 4)]
                dve.tensor_tensor(a, a, ps[:, half, :].rearrange("p (t i) -> p i t", t=4), ALU.mult).then_inc(gated, 1)

            dve.wait_ge(slotT_out, 1)
            dve.wait_ge(a_out, TILES)
            dve.wait_ge(u_used, 2 * TILES)
            hots(0, 0, True)
            hots(1, 1, True)
            apply_gates(0, 0)
            with dve.Fori(1, T // 8) as r:
                hots(r * 2, 0, False)
                apply_gates(r * 2 - 1, 1)
                hots(r * 2 + 1, 1, False)
                apply_gates(r * 2, 0)
            apply_gates(T // 4 - 1, 1)

            def v_tile(tile, j, first):
                dve.wait_ge(act_hi, tile + 1)
                if not first:
                    dve.wait_ge(v_used, tile * 2 - 4)
                dve.tensor_tensor(aL[j][:], acts[:, bass.ds(tile, 1), :].rearrange("p a t -> p (a t)"),
                                  aH[j][:].bitcast(F32), ALU.subtract).then_inc(act_lo, 1)
                for h in range(2):
                    slot = (2 * j + h) % RING
                    dve.wait_ge(v_hi, tile * 2 + (h + 1))
                    dve.tensor_tensor(eL[:, slot, :], raw[:, slot, :], eH[:, slot, :].bitcast(F32),
                                      ALU.subtract).then_inc(v_lo, 1)

            for j in range(3):
                v_tile(j, j, True)
            with dve.Fori(1, TILES // 3) as r:
                for j in range(3):
                    v_tile(r * 3 + j, j, False)
            for j in range(2):
                v_tile(TILES - 2 + j, j, False)

            dve.wait_ge(tail_in, 48)
            seq(dve.tensor_tensor(gate2[:], gate2[:], post2[:], ALU.mult))
            dve.wait_ge(y2_sq, 1)
            inverse_mean(stat[:, 48:50], stat[:, 46:48], D)
            dve.nop().then_inc(y2_rc, 1)
            dve.wait_ge(y2_rs, 1)
            for tt in range(TT):
                seq(dve.scalar_tensor_tensor(post2[:], ps[:, 4 * tt:4 * tt + 4, :].rearrange("p a b -> p (a b)"),
                                             stat[:, 50 + tt:51 + tt], gate2[:], ALU.mult, ALU.mult))
                seq(dve.tensor_tensor(post2[:].rearrange("p (q k l) -> p q k l", q=4, l=QUAD),
                                      x1[:, tt, :].rearrange("p (k q l) -> p q k l", q=4, l=QUAD),
                                      post2[:].rearrange("p (q k l) -> p q k l", q=4, l=QUAD), ALU.add))
                seq(dve.tensor_copy(x1[:, tt, :], post2[:]))
                dve.nop().then_inc(out_ready, 1)


def constant_table(np):
    t = np.zeros((P, C_ALL), np.float32)
    t[:, C_ID:C_ID + P] = np.eye(P)
    t[:, C_ONE:C_ONE + P] = 1.0
    t[:, C_IOTA:C_IOTA + P] = np.arange(P)
    for start in (C_MASK, C_MASK + 2 * P):
        t[0:P // 2, start + P // 2:start + P] = -1e30
    half = np.arange(HALF, dtype=np.float32) / np.float32(HALF)
    t[:, C_FREQ:C_FREQ + HALF] = np.float32(10000.0) ** (-half)
    for g, w in enumerate(WINDOWS):
        t[:, C_CNT + 16 * g:C_CNT + 16 * (g + 1)] = 1.0 / np.minimum(np.arange(16) + 1, w)
    t[:, C_I16:C_I16 + 16] = np.arange(16)
    return t


_INS = ['x', 'c', 'positions', 'ada_w', 'ada_b', 'pre_mix_g', 'post_mix_g', 'pre_ffn_g', 'post_ffn_g',
        'w_in', 'pool_w', 'pool_scale', 'q_norm_g', 'w_uq', 'kv_norm_g', 'w_ukv', 'w_out',
        'peer_wq', 'peer_sub_keys', 'peer_u', 'peer_v']
_OUTS = [((1, 256, 2048), 'float32')]


def kernel(**inputs):
    import numpy as _np
    import concourse.bacc as _bacc
    from concourse import mybir as _mybir
    from concourse.bass_utils import run_bass_kernel_spmd as _run

    nc = _bacc.Bacc("TRN2", target_bir_lowering=False, num_devices=1)
    arrays, args = {}, []
    for name in _INS:
        a = _np.ascontiguousarray(inputs[name])
        arrays[f"in_{name}_dram"] = a
        args.append(nc.dram_tensor(f"in_{name}_dram", a.shape, _mybir.dt.from_np(a.dtype), kind="ExternalInput").ap())
    table = constant_table(_np)
    arrays["consts_dram"] = table
    args.append(nc.dram_tensor("consts_dram", table.shape, _mybir.dt.float32, kind="ExternalInput").ap())
    for i, (shape, dtype) in enumerate(_OUTS):
        dt = _mybir.dt.from_np(_np.dtype(dtype))
        args.append(nc.dram_tensor(f"out_{i}_dram", shape, dt, kind="ExternalOutput").ap())
    hybrid_block(nc, *args)
    r = _run(nc, [arrays], core_ids=[0])
    got = tuple(r.results[0][f"out_{i}_dram"] for i in range(len(_OUTS)))
    return got[0]
```

```python
import concourse.bass as bass
from concourse import mybir

F32 = mybir.dt.float32
F32R = mybir.dt.float32r
U32 = mybir.dt.uint32
I32 = mybir.dt.int32
ALU = mybir.AluOpType
ACT = mybir.ActivationFunctionType
AX_X = mybir.AxisListType.X

P = 128
D = 2048
T = 256
TT = T // P
KT = D // P
W = 512
POOL_W = 1024
WINDOWS = (2, 4, 8, 16)
HEADS = 8
NOPE = 128
ROPE = 64
HALF = ROPE // 2
QR = 512
KVR = 256
LAT = QR + KVR + ROPE
SCALE = float(NOPE + ROPE) ** -0.5
EPS = 1e-6
PH = 8
NK = 128
TOPK = 16
QUAD = 32
TILES = NK * NK // P
HF = 1024
RING = 3
RAW = 4
ROUND = 6
ROUNDS = TILES // ROUND
KEY_ROUNDS = 8
PAIR_ROUNDS = 5
REST = KEY_ROUNDS + PAIR_ROUNDS
BIG = 3.0e38

C_ID, C_ONE, C_IOTA, C_MASK = 0, P, 2 * P, 3 * P
C_FREQ = C_MASK + 3 * P
C_CNT = C_FREQ + HALF
C_I16 = C_CNT + 4 * 16
C_ALL = C_I16 + 16

V_G1, V_G2 = 0, KT
V_QN = 2 * KT
V_KVN = V_QN + QR // P
V_PS = V_KVN + KVR // P
V_ALL = V_PS + POOL_W // P

TWO_PI_A = 6.28125
TWO_PI_B = 0.0019340515136718750
TWO_PI_C = 1.2556659146019e-06


def pair(i):
    return 2 * (i // 2 + 1)


def chunk_plan():
    return [
        (("ada", 0), 0), (("ada", 1), 1), (("ada", 2), 2), (("ada", 3), 0), (("win", 0), 1), (("ada", 4), 2),
        (("ada", 5), 0), (("ada", 6), 2), (("ada", 7), 0), (("win", 1), 2), (("ada", 8), 0), (("win", 2), 1),
        (("ada", 9), 0), (("win", 3), 2), (("ada", 10), 0), (("uq", 0), 1), (("ada", 11), 0), (("ukv", 0), 2),
        (("ada", 12), 0), (("ada", 13), 0), (("ada", 14), 2), (("wout", 0), 1), (("ada", 15), 0), (("ada", 16), 2), (("ada", 17), 0), (("wout", 1), 2), (("ada", 18), 0), (("wout", 2), 1), (("ada", 19), 0), (("wout", 3), 2), (("ada", 20), 0), (("wq", 0), 1), (("wq", 1), 2), (("ada", 21), 0), (("wq", 2), 1), (("ada", 22), 0), (("wq", 3), 2), (("ada", 23), 0), (("keys", 0), 0)]


def ada_chunk(n):
    return n + 4 if n < 4 else n - 4 if n < 8 else n


def hybrid_block(nc, x, c, positions, ada_w, ada_b, pre_mix_g, post_mix_g, pre_ffn_g, post_ffn_g,
                 w_in, pool_w, pool_scale, q_norm_g, w_uq, kv_norm_g, w_ukv, w_out,
                 peer_wq, peer_sub_keys, peer_u, peer_v, consts, out):
    plan = chunk_plan()
    where = {}
    per_slot = [0, 0, 0]
    for n, (key, slot) in enumerate(plan):
        per_slot[slot] += 64 if key[0] == "wq" else 32 if key[0] in ("uq",) else 16
        where[key] = (slot, per_slot[slot], n)

    base = (nc.sbuf_base + 31) // 32 * 32

    def at(name, off, shape, dt=F32):
        return nc.alloc_sbuf_tensor_at(name, [P] + shape, dt, offset=base + 4 * off)

    ring = [at(f"ring{s}", 8192 * s, [8192]) for s in range(3)]
    ring_low = [at(f"ring_low{s}", 8192 * s, [8192], F32R) for s in range(3)]
    xs = at("xs", 24576, [TT, D])
    hT = at("hT", 28672, [KT, T])
    qnT = at("qnT", 28672, [HEADS, T])
    knT = at("knT", 30720, [HEADS, T])
    y1 = at("y1", 28672, [TT, D])
    h2T = at("h2T", 28672, [KT, T])
    qT = at("qT", 24576, [KT, T])
    keyT = at("keyT", 8192, [KT, NK])
    sc = at("sc", 28672, [TT * KT, NK])
    tmpk = at("tmpk", 28672, [2048])
    tmpk2 = at("tmpk2", 30720, [2048])
    R = 24576
    s16 = at("s16", R, [TT * KT, TOPK])
    cand = at("cand", R + 512, [TOPK * TOPK])
    rest = at("rest", R + 768, [TOPK * TOPK])
    posa = at("posa", R + 512, [TT, PH * TOPK], U32)
    i16f = at("i16f", R + 1024, [TT * KT, TOPK])
    best = at("best", R + 1536, [TT * PH, TOPK])
    posu = at("posu", R + 1792, [TT * PH, TOPK], U32)
    posf = at("posf", R + 2048, [2, TT, PH * TOPK])
    slots = at("slots", R + 2560, [3, TT, PH * TOPK])
    gtmp = at("gtmp", R + 3328, [TT * PH, TOPK])
    gsum = at("gsum", R + 3584, [TT * PH])
    idle = at("idle", R + 3632, [1])
    picked = at("picked", R + 3600, [TOPK])
    picked_at = at("picked_at", R + 3616, [TOPK], U32)
    acts = at("acts", 0, [TILES, T])
    S = 32768
    cst = at("cst", S, [3 * P])
    vcols = at("vcols", S + 384, [V_ALL])
    mod1 = at("mod1", S + 432, [2, KT])
    mod2 = at("mod2", S + 464, [2, KT])
    stat = at("stat", S + 496, [64])
    c_col = at("c_col", S + 560, [KT])
    c_act = at("c_act", S + 576, [KT])
    i16 = at("i16", S + 592, [16])
    cnt = at("cnt", S + 608, [4, 16])
    pos_i = at("pos_i", S + 672, [TT], I32)
    pos_f = at("pos_f", S + 680, [TT])
    u_shift = at("u_shift", S + 680, [4])
    rowbuf = at("rowbuf", S + 688, [W])
    slotT = at("slotT", S + 1200, [3, T])
    aH = [at(f"aH{i}", S + 688 + 256 * i, [T], F32R) for i in range(2)]
    aL = [at(f"aL{i}", S + 1200 + 256 * i, [T], F32R) for i in range(2)]
    M = S + 1968
    uT = at("uT", M, [POOL_W // P, T])
    vv = at("vv", M, [TT, POOL_W])
    gate1 = at("gate1", M, [D])
    zT = at("zT", M + 2048, [POOL_W // P, T])
    s_sb = at("s_sb", M + 2048, [2, 384])
    pT = at("pT", M + 2816, [2, 384])
    post1 = at("post1", M + 2048, [D])
    catT = at("catT", M + 4096, [KT, T])
    acc = at("acc", M + 8192, [2, W])
    acc_b = at("acc_b", M + 17312, [2, W])
    init = at("init", M + 9216, [2, W])
    lat = at("lat", M + 10240, [TT, LAT])
    cT = at("cT", M + 11904, [6, T])
    qpeT = at("qpeT", M + 13440, [4, T])
    kpeT = at("kpeT", M + 14464, [T])
    qrope = at("qrope", M + 14720, [TT, 8 * ROPE])
    krope = at("krope", M + 15744, [TT, 2 * ROPE])
    trig = at("trig", M + 16000, [2, TT, HALF])
    tmpr = at("tmpr", M + 16128, [2, 256])
    x1q = at("x1q", M + 10240, [TT, D])
    mask = at("mask", M + 16640, [3 * P])
    freq = at("freq", M + 17024, [HALF])
    vrow = at("vrow", M, [P])
    ang = at("ang", M + 4096, [4, TT * HALF])
    diag = at("diag", M + 17056, [TT, P])
    junk = at("junk", M + 4096, [D])
    catL = at("catL", M + 4096, [KT, T], F32R)
    catH_a = at("catH_a", M + 10240, [12, T], F32R)
    catH_b = at("catH_b", M + 14720, [4, T], F32R)
    wout_high = [at(f"wout_high{i}", M + o, [W], F32R) for i, o in enumerate((13440, 13952, 15744, 16256))]
    wq_high = [at(f"wq_high{i}", M + 14336 + W * i, [W], F32R) for i in range(5)]
    h2H = at("h2H", M, [KT, T], F32R)
    h2L = at("h2L", M + 4096, [KT, T], F32R)
    x1 = at("x1", M, [TT, D])
    gate2 = at("gate2", M + 4096, [D])
    post2 = at("post2", M + 6144, [D])
    raw = at("raw", M + 8192, [RAW, HF])
    eL = at("eL", M + 12288, [RING, HF], F32R)
    eH = at("eH", M + 15360, [RING, HF], F32R)
    hotA = at("hotA", M + 15360, [2, 2, P])
    hotP = at("hotP", M + 17408, [4, 2, P])
    hotB = at("hotB", M + 16384, [2, 4, P])
    aH.append(at("aH2", M + 11264, [T], F32R))
    aL.append(at("aL2", M + 11520, [T], F32R))

    x1_dram = nc.dram_tensor("x1_dram", [TT, P, D], F32).ap()
    gate_dram = nc.dram_tensor("gate_dram", [2, D], F32).ap()

    from contextlib import ExitStack
    with ExitStack() as ctx:
        ps = ctx.enter_context(nc.psum_tensor("ps", [P, 8, W], F32))

        def sem(name):
            return ctx.enter_context(nc.semaphore(name))

        consts_in, vrow_in, x_in, c_in = sem("consts_in"), sem("vrow_in"), sem("x_in"), sem("c_in")
        ring_in = [sem(f"ring_in{s}") for s in range(3)]
        init_in = [sem("init_in0"), sem("init_in1")]
        init_zero = sem("init_zero")
        acc_ready, acc_used = sem("acc_ready"), sem("acc_used")
        row_ready, row_stored = sem("row_ready"), sem("row_stored")
        silu_done = sem("silu_done")
        vec_t, vec_cols = sem("vec_t"), sem("vec_cols")
        mod1_ready, mod2_ready = sem("mod1_ready"), sem("mod2_ready")
        x_sq, x_rs, diag1 = sem("x_sq"), sem("x_rs"), sem("diag1")
        xT_done, hT_done = sem("xT_done"), sem("hT_done")
        hA_used, hB_done, corr_mm, corr_out = sem("hA_used"), sem("hB_done"), sem("corr_mm"), sem("corr_out")
        u_mm, u_out = sem("u_mm"), sem("u_out")
        lat_mm, lat_out, lat_sq = sem("lat_mm"), sem("lat_out"), sem("lat_sq")
        trig_ready, trig_arg = sem("trig_ready"), sem("trig_arg")
        z_ready, k_roped, lat_diag = sem("z_ready"), sem("k_roped"), sem("lat_diag")
        cT_mm, cT_out = sem("cT_mm"), sem("cT_out")
        qn_mm, qn_out = sem("qn_mm"), sem("qn_out")
        qpe_mm, q_roped, qpeT_mm, qpeT_out = sem("qpe_mm"), sem("q_roped"), sem("qpeT_mm"), sem("qpeT_out")
        kn_mm, kn_out, v_mm, v_out = sem("kn_mm"), sem("kn_out"), sem("v_mm"), sem("v_out")
        pool_mm, pool_out = sem("pool_mm"), sem("pool_out")
        s_mm, s_max, s_exp, s_norm = sem("s_mm"), sem("s_max"), sem("s_exp"), sem("s_norm")
        pT_mm, pT_out, o_mm, o_out = sem("pT_mm"), sem("pT_out"), sem("o_mm"), sem("o_out")
        y_mm, y_out = sem("y_mm"), sem("y_out")
        y_rs, g1_in, x1_done, x1_sq, x1_rs, diag2 = (
            sem("y_rs"), sem("g1_in"), sem("x1_done"), sem("x1_sq"), sem("x1_rs"), sem("diag2"))
        y_rc, x1_stored = sem("y_rc"), sem("x1_stored")
        x1T_mm, h2_out, h2H_out, h2L_out = sem("x1T_mm"), sem("h2_out"), sem("h2H_out"), sem("h2L_out")
        qT_mm, qT_out, key_mm, key_out = sem("qT_mm"), sem("qT_out"), sem("key_mm"), sem("key_out")
        sc_mm, sc_out = sem("sc_mm"), sem("sc_out")
        g_shift, g_exp, slots_ready, slot_mm, slotT_out = (
            sem("g_shift"), sem("g_exp"), sem("slots_ready"), sem("slot_mm"), sem("slotT_out"))
        w_hi, w_lo, w_used, cat_hi, cat_lo = sem("w_hi"), sem("w_lo"), sem("w_used"), sem("cat_hi"), sem("cat_lo")
        raw_in = [sem(f"raw_in{s}") for s in range(RAW)]
        u_tr, u_hi, u_lo, u_lo_pool, u_used = sem("u_tr"), sem("u_hi"), sem("u_lo"), sem("u_lo_pool"), sem("u_used")
        a_out = sem("a_out")
        hot_pool, hot_act, hot_abs, hot_diff = sem("hot_pool"), sem("hot_act"), sem("hot_abs"), sem("hot_diff")
        hot_ready, hot_mm, gated = sem("hot_ready"), sem("hot_mm"), sem("gated")
        v_in = [sem(f"v_in{s}") for s in range(RING)]
        v_hi, v_lo, v_used = sem("v_hi"), sem("v_lo"), sem("v_used")
        act_hi, act_lo = sem("act_hi"), sem("act_lo")
        y2_sq, y2_rc, y2_rs, tail_in, out_ready, out_stored = (
            sem("y2_sq"), sem("y2_rc"), sem("y2_rs"), sem("tail_in"), sem("out_ready"),
            sem("out_stored"))
        dve_chain, act_chain, pick_chain = sem("dve_chain"), sem("act_chain"), sem("pick_chain")

        block = ctx.enter_context(nc.Block())

        ident = cst[:, 0:P]
        ones = cst[:, P:2 * P]
        iota = cst[:, 2 * P:3 * P]

        def ring_arrived(eng, key):
            slot, count, _ = where[key]
            eng.wait_ge(ring_in[slot], count)

        def last_use(key):
            kind, i = key
            return {"ada": (acc_ready, i + 1),
                    "win": ((corr_mm, 1), (u_mm, 8), (lat_mm, 2), (lat_mm, 4))[i % 4],
                    "uq": (pool_mm, 8), "ukv": (v_mm, 4), "wout": (y_mm, 2 * (i + 1)),
                    "wq": (qT_mm, 4 * (i + 1)), "keys": (key_mm, 4)}[kind]

        def wide(key, cols=W):
            return ring[where[key][0]][:, 0:KT * cols].rearrange("p (k n) -> p k n", k=KT)

        def wide_low(key):
            return ring_low[where[key][0]][:, 0:KT * W].rearrange("p (k n) -> p k n", k=KT)

        def high_of(kind, n, k):
            bufs = wout_high if kind == "wout" else wq_high
            return bufs[(KT * n + k) % len(bufs)]

        def piece(kind, n, k):
            return (0 if kind == "wout" else 4 * KT) + KT * n + k + 1

        def wait_high_free(eng, kind, n, k):
            before = KT * n + k - len(wout_high if kind == "wout" else wq_high)
            if before < 0:
                return
            m, kk = before // KT, before % KT
            if kk == KT - 1:
                eng.wait_ge(*last_use((kind, m)))
            else:
                eng.wait_ge(w_used, (0 if kind == "wout" else 4 * (KT - 1)) + (KT - 1) * m + kk + 1)

        def cat_high(j):
            return catH_a[:, j, :] if j < 12 else catH_b[:, j - 12, :]

        def turned(half_tile):
            return half_tile.rearrange("p (eb k el) -> p k eb el", eb=4, el=QUAD)

        def by_k(half_tile):
            return half_tile.rearrange("p (k eb el) -> p k eb el", eb=4, el=QUAD)

        def wait_low(eng, r, j):
            eng.wait_ge(u_lo_pool if j % 2 else u_lo, r * ROUND + (j // 2 + 1))

        ada_v = ada_w[0].rearrange("(p k) n -> p k n", k=KT)
        win_v = w_in[0].rearrange("(k p) n -> p k n", p=P)
        wout_v = w_out[0].rearrange("(k p) n -> p k n", p=P)
        wq_v = peer_wq[0].rearrange("(q k l) n -> q l k n", q=4, l=QUAD)
        ub = peer_u[0].rearrange("(i eb el) (q h dd) -> i h q el eb dd", el=QUAD, eb=4, q=4, h=2)
        vb = peer_v[0].rearrange("(i p) (h dd) -> i h p dd", p=P, h=2)

        @block.sync
        def _(sp):
            sp.dma_start(c_col[:], c.rearrange("o (p k) -> (o p) k", k=KT)).then_inc(c_in, 16)
            sp.dma_start(cst[:], consts[:, 0:3 * P]).then_inc(consts_in, 16)
            sp.dma_start(mask[:], consts[:, C_MASK:C_MASK + 3 * P]).then_inc(consts_in, 16)
            sp.dma_start(freq[:], consts[:, C_FREQ:C_FREQ + HALF]).then_inc(consts_in, 16)
            sp.dma_start(cnt[:], consts[:, C_CNT:C_CNT + 64].rearrange("p (g t) -> p g t", g=4)).then_inc(consts_in, 16)
            sp.dma_start(i16[:], consts[:, C_I16:C_I16 + 16]).then_inc(consts_in, 16)

            ada_n = 0
            in_slot = {}
            for n, ((kind, i), slot) in enumerate(plan):
                if n == 3:
                    sp.dma_start(xs[:], x[0].rearrange("(t p) d -> p t d", p=P)).then_inc(x_in, 16)
                if n >= 3:
                    sp.wait_ge(*last_use(in_slot[slot]))
                in_slot[slot] = (kind, i)
                dst = ring[slot]
                done = ring_in[slot]
                if kind == "ada":
                    cols = slice(ada_chunk(i) * W, (ada_chunk(i) + 1) * W)
                    sp.dma_start(wide((kind, i)), ada_v[:, :, cols]).then_inc(done, 16)
                    if ada_n == 0:
                        sp.wait_ge(init_zero, 1)
                    if ada_n >= 2:
                        sp.wait_ge(acc_ready, ada_n - 1)
                    sp.dma_start(init[0:1, ada_n % 2, :], ada_b[0:1, cols]).then_inc(init_in[ada_n % 2], 16)
                    ada_n += 1
                elif kind == "win":
                    cols = min(W, POOL_W + LAT - i * W)
                    sp.dma_start(wide((kind, i), cols), win_v[:, :, i * W:i * W + cols]).then_inc(done, 16)
                elif kind == "wout":
                    sp.dma_start(wide((kind, i)), wout_v[:, :, i * W:(i + 1) * W]).then_inc(done, 16)
                elif kind == "uq":
                    sp.dma_start(dst[:, 0:6144].rearrange("p (k n) -> p k n", k=4),
                                 w_uq[0].rearrange("(k p) n -> p k n", p=P)).then_inc(done, 16)
                    sp.dma_start(dst[:, 6144:8192].rearrange("p (g k n) -> p g k n", g=4, k=2),
                                 pool_w[0].rearrange("g (k p) n -> p g k n", p=P)).then_inc(done, 16)
                elif kind == "ukv":
                    sp.dma_start(dst[:, 0:4096].rearrange("p (k n) -> p k n", k=2),
                                 w_ukv[0].rearrange("(k p) n -> p k n", p=P)).then_inc(done, 16)
                elif kind == "wq":
                    for q in range(4):
                        sp.dma_start(wide((kind, i))[q * QUAD:(q + 1) * QUAD],
                                     wq_v[q, :, :, i * W:(i + 1) * W]).then_inc(done, 16)
                elif kind == "keys":
                    sp.dma_start(dst[:, 0:2048].rearrange("p (k n) -> p k n", k=KT),
                                 peer_sub_keys[0].rearrange("h s n d -> n (h s) d")).then_inc(done, 16)

            sp.wait_ge(acc_used, 24)
            sp.wait_ge(q_roped, 1)
            sp.wait_ge(qpeT_out, 1)
            sp.wait_ge(x1T_mm, KT)
            sp.wait_ge(x1_stored, 16)

            def load_u(tile, h, before, slot):
                if before:
                    wait_low(sp, *before)
                for q in range(4):
                    sp.dma_start(raw[q * QUAD:(q + 1) * QUAD, slot, :].rearrange("p (e d) -> p e d", e=4),
                                 ub[tile, h, q]).then_inc(raw_in[slot], 16)

            def load_u_round(r, tiles=ROUND, first=False):
                for j in range(2 * tiles):
                    before = (r, j - RAW) if j >= RAW else None if first else (r - 1, 2 * ROUND + j - RAW)
                    load_u(r * ROUND + j // 2, j % 2, before, j % RAW)

            load_u_round(0, first=True)
            with sp.Fori(1, ROUNDS) as r:
                load_u_round(r)
            load_u_round(ROUNDS, TILES % ROUND)

            def load_v(tile, h, g, slot):
                sp.wait_ge(v_lo, g - (RING - 1))
                sp.dma_start(raw[:, slot, :], vb[tile, h]).then_inc(v_in[slot], 16)

            def load_v3(t0):
                for j in range(6):
                    load_v(t0 + j // 2, j % 2, t0 * 2 + j, j % RING)

            wait_low(sp, ROUNDS, 2 * (TILES % ROUND) - 2)
            wait_low(sp, ROUNDS, 2 * (TILES % ROUND) - 1)
            for j in range(RING):
                sp.dma_start(raw[:, j, :], vb[j // 2, j % 2]).then_inc(v_in[j], 16)
            for j in range(RING, 6):
                load_v(j // 2, j % 2, j, j % RING)
            with sp.Fori(1, TILES // 3) as r:
                load_v3(r * 3)
            for j in range(4):
                load_v(TILES - 2 + j // 2, j % 2, 2 * (TILES - 2) + j, j % RING)

        @block.gpsimd
        def _(pool):
            vr = vrow[:, :]
            pool.memset(init[:], 0.0).then_inc(init_zero, 1)
            pool.memset(vrow[:], 0.0).then_inc(init_zero, 1)
            pool.wait_ge(init_zero, 2)
            pool.dma_start(vr[V_G1:V_G1 + KT], pre_mix_g[0].rearrange("(k p) -> k p", p=P)).then_inc(vrow_in, 16)
            g2q = pre_ffn_g[0].rearrange("(q k l) -> k q l", q=4, l=QUAD)
            pool.dma_start(vr[V_G2:V_G2 + KT].rearrange("k (q l) -> k q l", q=4), g2q).then_inc(vrow_in, 16)
            pool.dma_start(vr[V_QN:V_KVN], q_norm_g[0].rearrange("(k p) -> k p", p=P)).then_inc(vrow_in, 16)
            pool.dma_start(vr[V_KVN:V_PS], kv_norm_g[0].rearrange("(k p) -> k p", p=P)).then_inc(vrow_in, 16)
            pool.dma_start(vr[V_PS:V_ALL], pool_scale[0].rearrange("(k p) -> k p", p=P)).then_inc(vrow_in, 16)
            pool.dma_start(pos_i[:], positions[0].rearrange("(t p) -> p t", p=P),
                           allow_slow_non_contiguous=True).then_inc(vrow_in, 16)
            def cat_lows(n, j0, j1, high):
                pool.wait_ge(cat_hi, n)
                pool.tensor_tensor(catL[:, j0:j1, :], catT[:, j0:j1, :], high.bitcast(F32),
                                   ALU.subtract).then_inc(cat_lo, 1)

            cat_lows(1, 8, 9, catH_a[:, 8:9, :])
            cat_lows(2, 0, 8, catH_a[:, 0:8, :])
            for h in range(1, HEADS):
                high = catH_a[:, 8 + h:9 + h, :] if h < 4 else catH_b[:, h - 4:h - 3, :]
                cat_lows(h + 2, 8 + h, 9 + h, high)
            pool.wait_ge(row_stored, 64)
            pool.wait_ge(o_out, HEADS)
            pool.dma_start(gate1[:], gate_dram[0:1, :].broadcast_to([P, D])).then_inc(g1_in, 16)
            pool.dma_start(post1[:], post_mix_g[0:1, :].broadcast_to([P, D])).then_inc(g1_in, 16)

            def weight_lows(kind):
                for n in range(4):
                    for k in range(KT):
                        pool.wait_ge(w_hi, piece(kind, n, k))
                        pool.tensor_tensor(wide_low((kind, n))[:, k, :], wide((kind, n))[:, k, :],
                                           high_of(kind, n, k)[:].bitcast(F32), ALU.subtract).then_inc(w_lo, 1)

            weight_lows("wout")
            pool.wait_ge(x1_done, 2)
            pool.dma_start(x1_dram.rearrange("t p d -> p t d"), x1q[:]).then_inc(x1_stored, 16)
            weight_lows("wq")
            def low_round(r, tiles=ROUND, first=False):
                for j in range(1, 2 * tiles, 2):
                    pool.wait_ge(u_hi, r * (2 * ROUND) + (j + 1))
                    if not (first and j < RING):
                        pool.wait_ge(u_used, r * (2 * ROUND) + (j + 1 - RING))
                    pool.tensor_tensor(by_k(eL[:, j % RING, :]), turned(raw[:, j % RAW, :]),
                                       by_k(eH[:, j % RING, :].bitcast(F32)), ALU.subtract).then_inc(u_lo_pool, 1)

            low_round(0, first=True)
            with pool.Fori(1, ROUNDS) as r:
                low_round(r)
            low_round(ROUNDS, TILES % ROUND)

            def differences(g, q, first):
                if not first:
                    pool.wait_ge(hot_mm, g - 3)
                if q or not first:
                    pool.wait_ge(hot_diff, g)
                pool.tensor_tensor(hotP[:, q], iota.unsqueeze(1).broadcast_to([P, 2, P]),
                                   slotT[:, 1, bass.ds(g * 4 + 2, 2)].unsqueeze(2).broadcast_to([P, 2, P]),
                                   ALU.subtract).then_inc(hot_diff, 1)

            def where_zero(q):
                pool.tensor_scalar(hotP[:, q], hotP[:, q], 0.0, None, ALU.is_equal).then_inc(hot_pool, 1)

            pool.wait_ge(slotT_out, 1)
            pool.wait_ge(u_used, 2 * TILES)
            for q in range(4):
                differences(q, q, True)
                if q:
                    where_zero(q - 1)
            with pool.Fori(1, T // 16) as r:
                for q in range(4):
                    differences(r * 4 + q, q, False)
                    where_zero((q + 3) % 4)
            pool.wait_ge(hot_diff, T // 4)
            where_zero(3)

            pool.wait_ge(row_stored, 128)
            pool.wait_ge(x1_stored, 16)
            pool.wait_ge(u_used, 2 * TILES)
            pool.dma_start(x1[:], x1_dram.rearrange("t p d -> p t d")).then_inc(tail_in, 16)
            pool.dma_start(gate2[:], gate_dram[1:2, :].broadcast_to([P, D])).then_inc(tail_in, 16)
            pool.dma_start(post2[:], post_ffn_g[0:1, :].broadcast_to([P, D])).then_inc(tail_in, 16)
            for tt in range(TT):
                pool.wait_ge(out_ready, tt + 1)
                pool.dma_start(out[0, tt * P:(tt + 1) * P, :], x1[:, tt, :]).then_inc(out_stored, 16)
            pool.wait_ge(out_stored, 32)

        @block.tensor
        def _(pe):
            def transpose_vectors():
                pe.wait_ge(consts_in, 80)
                pe.wait_ge(vrow_in, 96)
                pe.transpose(ps[:, 1, 0:P], vrow[:, :], ident).then_inc(vec_t, 1)

            def ada_columns(n, quads):
                pe.wait_ge(acc_ready, n + 1)
                parts = (acc[:, n % 2, :], acc_b[:, n % 2, :])
                if not quads:
                    for j in range(4):
                        for i, b in enumerate(parts):
                            mm = pe.matmul(ps[:, 0, n * 4 + j:n * 4 + j + 1], b[:, j * P:(j + 1) * P],
                                           ones[:, 0:1], start=(i == 0), stop=(i == 1), skip_group_check=True)
                else:
                    m, q = (n - 12) // 4, (n - 12) % 4
                    for k in range(KT):
                        col = 64 + m * KT + k
                        for i, b in enumerate(parts):
                            mm = pe.matmul(ps[q * QUAD:(q + 1) * QUAD, 0, col:col + 1],
                                           b[:, k * QUAD:(k + 1) * QUAD], ones[:, 0:1], start=(i == 0),
                                           stop=(i == 1), skip_group_check=True)
                mm.then_inc(acc_used, 1)

            def ada_row(n, rows_before):
                pe.wait_ge(acc_ready, n + 1)
                if rows_before:
                    pe.wait_ge(row_ready, rows_before)
                pe.matmul(ps[0:1, 1, :], ones[:, 0:1], acc[:, n % 2, :], start=True, stop=False)
                pe.matmul(ps[0:1, 1, :], ones[:, 0:1], acc_b[:, n % 2, :], start=False, stop=True).then_inc(acc_used, 1)

            def turn(src, dst_bank, out_done, k, slots_, done, rhs):
                b, half = dst_bank
                for tt in range(TT):
                    mm = pe.matmul(ps[:, b, half * T + tt * P:half * T + (tt + 1) * P], src(tt), rhs(tt),
                                   start=True, stop=True, skip_group_check=True)
                mm.then_inc(done, 1)

            def mm_group(bank_ap, lhs, rhs, k_tiles):
                for k in range(k_tiles):
                    mm = pe.matmul(bank_ap, lhs(k), rhs(k), start=(k == 0), stop=(k == k_tiles - 1),
                                   skip_group_check=True)
                return mm

            def split3(o, lh, ll, rh, rl, start, stop):
                pe.matmul(o, lh, rh, start=start, stop=False, skip_group_check=True)
                pe.matmul(o, lh, rl, start=False, stop=False, skip_group_check=True)
                return pe.matmul(o, ll, rh, start=False, stop=stop, skip_group_check=True)

            for n in range(4):
                if n == 2:
                    transpose_vectors()
                ada_columns(n, False)
            pe.wait_ge(vec_cols, 1)

            pe.wait_ge(x_in, 16)
            pe.wait_ge(diag1, 2)
            for k in range(KT):
                if k >= 4 and k % 2 == 0:
                    pe.wait_ge(hT_done, k - 2)
                turn(lambda tt: xs[:, tt, k * P:(k + 1) * P], (2 + (k // 2) % 2, k % 2), None, k, 4,
                     xT_done, lambda tt: diag[:, tt, :])

            pe.wait_ge(hT_done, KT)
            pe.wait_ge(mod1_ready, 1)
            for n in range(2):
                if n == 1:
                    pe.wait_ge(mod1_ready, 2)
                    w0 = wide(("win", 0))
                    mm_group(ps[0:1, 1, :], lambda k: mod1[:, 1, k:k + 1], lambda k: w0[:, k, :],
                             KT).then_inc(corr_mm, 1)
                    pe.wait_ge(corr_out, 1)
                    for j in range(4):
                        pe.matmul(ps[:, 0, 480 + j:481 + j], rowbuf[0:1, j * P:(j + 1) * P], ones[0:1, 0:1],
                                  start=True, stop=True, skip_group_check=True).then_inc(u_mm, 1)
                    pe.wait_ge(hB_done, 4)
                ring_arrived(pe, ("win", n))
                w = wide(("win", n))
                for j in range(4):
                    b = 4 + 2 * n + j // 2
                    mm = mm_group(ps[:, b, (j % 2) * T:(j % 2 + 1) * T],
                                  lambda k: w[:, k, j * P:(j + 1) * P], lambda k: hT[:, k, :], KT)
                    if n == 1:
                        mm.then_inc(u_mm, 1)
                    else:
                        if j == 3:
                            mm.then_inc(hA_used, 1)
                        ada_columns(4 + j, False)
                if n == 1:
                    ada_row(8, 0)
            for n in range(2, 4):
                ring_arrived(pe, ("win", n))
                cols = min(W, POOL_W + LAT - n * W)
                w = wide(("win", n), cols)
                for tt in range(TT):
                    if tt == 0:
                        pe.wait_ge(u_out, 4 * (n - 1))
                    b = 4 + 2 * (n - 2) + tt
                    mm = mm_group(ps[:, b, 0:cols], lambda k: hT[:, k, tt * P:(tt + 1) * P],
                                  lambda k: w[:, k, :], KT)
                    mm.then_inc(lat_mm, 1)
                    if (n, tt) == (2, 0):
                        ada_row(9, 1)
                if n == 2:
                    ada_row(10, 2)

            ring_arrived(pe, ("uq", 0))
            uq_slot = ring[where[("uq", 0)][0]]
            wuq = uq_slot[:, 0:6144].rearrange("p (k h n) -> p k h n", k=4, h=HEADS)
            wpl = uq_slot[:, 6144:8192].rearrange("p (g k n) -> p g k n", g=4, k=2)
            pe.wait_ge(lat_diag, 4)
            for r in range(6):
                if r == 4:
                    pe.wait_ge(cT_out, 2)
                turn(lambda tt: lat[:, tt, r * P:(r + 1) * P], (2 + (r // 2) % 2, r % 2), None, r, 4,
                     cT_mm, lambda tt: diag[:, tt, :] if r < 4 else tmpr[:, tt, 0:P])
            pe.wait_ge(cT_out, 6)
            pe.wait_ge(lat_out, 4)
            for h in range(HEADS):
                b = 4 + h // 2
                mm_group(ps[:, b, (h % 2) * T:(h % 2 + 1) * T], lambda k: wuq[:, k, h, 0:NOPE],
                         lambda k: cT[:, k, :], 4).then_inc(qn_mm, 1)
            for tt in range(TT):
                mm_group(ps[:, 2 + tt, :], lambda k: cT[:, k, tt * P:(tt + 1) * P],
                         lambda k: wuq[:, k, :, NOPE:NOPE + ROPE], 4).then_inc(qpe_mm, 1)
            ada_row(11, 3)
            pe.wait_ge(z_ready, 4)
            for j in range(8):
                g = j // 2
                b = 4 + j // 2
                if j % 2 == 0:
                    pe.wait_ge(qn_out, j + 2)
                mm = mm_group(ps[:, b, (j % 2) * T:(j % 2 + 1) * T],
                              lambda k: wpl[:, g, k, (j % 2) * P:(j % 2 + 1) * P],
                              lambda k: zT[:, 2 * g + k, :], 2)
                mm.then_inc(pool_mm, 1)
            ring_arrived(pe, ("ukv", 0))
            wkv = ring[where[("ukv", 0)][0]][:, 0:4096].rearrange("p (k h n) -> p k h n", k=2, h=HEADS)
            for h in range(HEADS):
                b = 4 + h // 2
                if h % 2 == 0:
                    pe.wait_ge(pool_out, h + 2)
                mm_group(ps[:, b, (h % 2) * T:(h % 2 + 1) * T], lambda k: wkv[:, k, h, 0:NOPE],
                         lambda k: cT[:, 4 + k, :], 2).then_inc(kn_mm, 1)
            for tt in range(TT):
                for hh in range(2):
                    b = 4 + tt * 2 + hh
                    pe.wait_ge(kn_out, 2 * (tt * 2 + hh) + 2)
                    mm_group(ps[:, b, :], lambda k: cT[:, 4 + k, tt * P:(tt + 1) * P],
                             lambda k: wkv[:, k, 4 * hh:4 * hh + 4, NOPE:2 * NOPE], 2).then_inc(v_mm, 1)
            ada_columns(12, True)
            pe.wait_ge(k_roped, 1)
            pe.wait_ge(q_roped, 1)
            for tt in range(TT):
                for p in range(4):
                    pe.transpose(ps[:, 2 + p // 2, (p % 2) * T + tt * P:(p % 2) * T + (tt + 1) * P],
                                 qrope[:, tt, p * P:(p + 1) * P], ident)
                mm = pe.transpose(ps[:, 0, T + tt * P:T + (tt + 1) * P], krope[:, tt, :], ident)
            mm.then_inc(qpeT_mm, 1)

            pe.wait_ge(qpeT_out, 1)
            pe.wait_ge(kn_out, HEADS)
            pe.wait_ge(qn_out, HEADS)

            def scores(h):
                b = 4 + h % 2
                if h < 2:
                    pe.wait_ge(v_out, h + 1)
                else:
                    pe.wait_ge(s_max, h - 1)
                r0 = (h % 2) * ROPE
                for qb in range(TT):
                    kend = (qb + 1) * P
                    o = ps[:, b, qb * P:qb * P + kend]
                    pe.matmul(o, qnT[:, h, qb * P:(qb + 1) * P], knT[:, h, 0:kend], start=True, stop=False,
                              skip_group_check=True)
                    mm = pe.matmul(o, qpeT[r0:r0 + ROPE, h // 2, qb * P:(qb + 1) * P],
                                   kpeT[r0:r0 + ROPE, 0:kend], start=False, stop=True, skip_group_check=True)
                mm.then_inc(s_mm, 1)

            def turn_probs(h):
                b = 6 + h % 2
                if h < 2:
                    pe.wait_ge(v_out, h + 3)
                pe.wait_ge(s_norm, h + 1)
                if h >= 2:
                    pe.wait_ge(pT_out, h - 1)
                for j in range(3):
                    mm = pe.transpose(ps[:, b, j * P:(j + 1) * P], s_sb[:, h % 2, j * P:(j + 1) * P], ident)
                mm.then_inc(pT_mm, 1)

            def mix(h):
                b = 2 + h % 2
                pe.wait_ge(pT_out, h + 1)
                if h >= 2:
                    pe.wait_ge(o_out, h - 1)
                v0, v1 = (vv[:, t, h * P:(h + 1) * P] for t in range(2))
                pe.matmul(ps[:, b, 0:P], v0, pT[:, h % 2, 0:P], start=True, stop=True, skip_group_check=True)
                pe.matmul(ps[:, b, P:T], v0, pT[:, h % 2, P:T], start=True, stop=False, skip_group_check=True)
                pe.matmul(ps[:, b, P:T], v1, pT[:, h % 2, T:T + P], start=False, stop=True,
                          skip_group_check=True).then_inc(o_mm, 1)

            pe.wait_ge(v_out, 4)
            scores(0)
            scores(1)
            for h in range(HEADS):
                turn_probs(h)
                if h + 2 < HEADS:
                    scores(h + 2)
                mix(h)
                if h >= 3 and h % 2:
                    ada_columns(13 + (h - 3) // 2, True)
            ada_columns(16, True)

            pe.wait_ge(cat_hi, HEADS + 1)
            pe.wait_ge(cat_lo, HEADS + 1)
            for n in range(4):
                for k in range(KT):
                    pe.wait_ge(w_lo, piece("wout", n, k))
                    for tt in range(TT):
                        if n >= 2 and k == 0:
                            pe.wait_ge(y_out, (n - 2) * 2 + tt + 1)
                        mm = split3(ps[:, 4 + (n % 2) * 2 + tt, :], cat_high(k)[:, tt * P:(tt + 1) * P],
                                    catL[:, k, tt * P:(tt + 1) * P], high_of("wout", n, k)[:],
                                    wide_low(("wout", n))[:, k, :], k == 0, k == KT - 1)
                        if k == KT - 1:
                            mm.then_inc(y_mm, 1)
                    if k < KT - 1:
                        mm.then_inc(w_used, 1)
                if n < 3:
                    ada_columns(17 + n, True)

            pe.wait_ge(diag2, 2)
            for k in range(KT):
                if k >= 4 and k % 2 == 0:
                    pe.wait_ge(h2_out, k - 2)
                turn(lambda tt: x1q[:, tt, k * P:(k + 1) * P],
                     (2 + (k // 2) % 2, k % 2), None, k, 4, x1T_mm, lambda tt: diag[:, tt, :])

            q_bank = [4, 5, 6, 7, 2, 3]
            for n in range(4):
                if n == 1:
                    pe.wait_ge(h2_out, KT)
                for k in range(KT):
                    if n == 0:
                        pe.wait_ge(h2H_out, k + 1)
                        pe.wait_ge(h2L_out, k + 1)
                    pe.wait_ge(w_lo, piece("wq", n, k))
                    for j in range(4):
                        i = 4 * n + j
                        if i >= 6 and k == 0:
                            pe.wait_ge(qT_out, i - 5)
                        cols = slice(j * P, (j + 1) * P)
                        mm = split3(ps[:, q_bank[i % 6], 0:T], high_of("wq", n, k)[:, cols],
                                    wide_low(("wq", n))[:, k, cols], h2H[:, k, :], h2L[:, k, :],
                                    k == 0, k == KT - 1)
                        if k == KT - 1:
                            mm.then_inc(qT_mm, 1)
                    if k < KT - 1:
                        mm.then_inc(w_used, 1)
                ada_row(20 + n, 4 + n)
            ring_arrived(pe, ("keys", 0))
            keys = ring[where[("keys", 0)][0]][:, 0:2048].rearrange("p (k n) -> p k n", k=KT)
            pe.wait_ge(qT_out, 12)
            for i in range(KT):
                b = 2 + (i // 4) % 2
                if i >= 8:
                    pe.wait_ge(key_out, i // 4 - 1)
                mm = pe.transpose(ps[:, b, (i % 4) * P:(i % 4 + 1) * P], keys[:, i, :], ident)
                if i % 4 == 3:
                    mm.then_inc(key_mm, 1)
            pe.wait_ge(qT_out, KT)
            pe.wait_ge(key_out, 4)
            for j in range(8):
                b = 4 + j % 4
                if j >= 4:
                    pe.wait_ge(sc_out, j - 3)
                for i in range(4):
                    tt, hp = j // 4, (j % 4) * 4 + i
                    mm = pe.matmul(ps[:, b, i * P:(i + 1) * P], qT[:, hp, tt * P:(tt + 1) * P], keyT[:, hp, :],
                                   start=True, stop=True, skip_group_check=True)
                mm.then_inc(sc_mm, 1)
            def u_tile(r, i, first):
                tile, bank = r * ROUND + i, i % 3
                if not first:
                    pe.wait_ge(a_out, tile - 2)
                for h in range(2):
                    slot = (2 * i + h) % RING
                    wait_low(pe, r, 2 * i + h)
                    for k in range(KT // 2):
                        kk = h * (KT // 2) + k
                        mm = split3(ps[:, bank, 0:T], eH[:, slot, k * P:(k + 1) * P], eL[:, slot, k * P:(k + 1) * P],
                                    h2H[:, kk, :], h2L[:, kk, :], kk == 0, kk == KT - 1)
                    mm.then_inc(u_used, 1)

            pe.wait_ge(h2L_out, KT)
            pe.wait_ge(h2H_out, KT)
            for i in range(ROUND):
                u_tile(0, i, i < 3)
            with pe.Fori(1, REST + 3) as r:
                for i in range(ROUND):
                    u_tile(r, i, False)
            pe.wait_ge(slots_ready, 1)
            for m in range(3):
                for tt in range(TT):
                    mm = pe.transpose(ps[:, 4 + m // 2, (m % 2) * T + tt * P:(m % 2) * T + (tt + 1) * P],
                                      slots[:, m, tt, :], ident)
            mm.then_inc(slot_mm, 1)
            with pe.Fori(REST + 3, ROUNDS) as r:
                for i in range(ROUND):
                    u_tile(r, i, False)
            for i in range(TILES % ROUND):
                u_tile(ROUNDS, i, False)

            def scatter(g, q, first):
                half = q % 2
                if not first:
                    pe.wait_ge(gated, g - 1)
                pe.wait_ge(hot_ready, g + 1)
                pe.wait_ge(hot_pool, g + 1)
                pe.wait_ge(hot_act, g + 1)
                for t in range(4):
                    hot = hotA[:, half, t, :] if t < 2 else hotP[:, q, t - 2, :]
                    mm = pe.matmul(ps[:, half, t * P:(t + 1) * P], hot, hotB[:, half, t, :],
                                   start=True, stop=True, skip_group_check=True)
                mm.then_inc(hot_mm, 1)

            pe.wait_ge(a_out, TILES)
            for q in range(4):
                scatter(q, q, q < 2)
            with pe.Fori(1, T // 16) as r:
                for q in range(4):
                    scatter(r * 4 + q, q, False)

            def v_tile(tile, j, start, stop):
                pe.wait_ge(act_lo, tile + 1)
                for h in range(2):
                    slot = (2 * j + h) % RING
                    pe.wait_ge(v_lo, tile * 2 + (h + 1))
                    for tt in range(TT):
                        lh, ll = (a[j][:, tt * P:(tt + 1) * P] for a in (aH, aL))
                        o = [ps[:, tt * 4 + h * 2 + n, :] for n in range(2)]
                        vh, vl = ([e[:, slot, n * W:(n + 1) * W] for n in range(2)] for e in (eH, eL))
                        for n in range(2):
                            pe.matmul(o[n], lh, vh[n], start=start, stop=False, skip_group_check=True)
                            pe.matmul(o[n], lh, vl[n], start=False, stop=False, skip_group_check=True)
                        for n in range(2):
                            mm = pe.matmul(o[n], ll, vh[n], start=False, stop=stop, skip_group_check=True)
                    mm.then_inc(v_used, 1)

            pe.wait_ge(gated, T // 4)
            for j in range(3):
                v_tile(j, j, j == 0, False)
            with pe.Fori(1, TILES // 3) as r:
                for j in range(3):
                    v_tile(r * 3 + j, j, False, False)
            v_tile(TILES - 2, 0, False, False)
            v_tile(TILES - 1, 1, False, True)

        @block.scalar
        def _(act):
            count = [0]

            def seq(ins):
                count[0] += 1
                ins.then_inc(act_chain, 1)
                act.wait_ge(act_chain, count[0])

            act.wait_ge(c_in, 16)
            act.activation(c_act[:], c_col[:], ACT.Silu).then_inc(silu_done, 1)
            act.wait_ge(x_in, 16)
            for tt in range(TT):
                seq(act.activation(hT[:].rearrange("p k t -> p (k t)")[:, 0:D], xs[:, tt, :], ACT.Square,
                                   accum_out=stat[:, tt:tt + 1]))
            act.nop().then_inc(x_sq, 1)
            act.wait_ge(trig_arg, 1)
            act.activation(trig[:, 0].rearrange("p t f -> p (t f)"), ang[:, 2, :], ACT.Sin).then_inc(trig_ready, 1)
            act.activation(trig[:, 1].rearrange("p t f -> p (t f)"), ang[:, 1, :], ACT.Sin).then_inc(trig_ready, 1)
            act.wait_ge(x_rs, 1)
            act.activation(stat[:, 4:6], stat[:, 2:4], ACT.Sqrt).then_inc(x_rs, 1)
            act.wait_ge(mod1_ready, 1)
            act.wait_ge(act_chain, count[0])
            for k in range(KT):
                act.wait_ge(xT_done, pair(k))
                b, half = 2 + (k // 2) % 2, k % 2
                act.activation(hT[:, k, :], ps[:, b, half * T:(half + 1) * T], ACT.Identity,
                               scale=mod1[:, 0, k:k + 1]).then_inc(hT_done, 1)

            def gate_row(n, stored):
                act.wait_ge(acc_used, n + 1)
                if stored:
                    act.wait_ge(row_stored, stored)
                act.copy(rowbuf[0:1, :], ps[0:1, 1, :]).then_inc(row_ready, 1)
                i = stored // 16
                act.wait_ge(row_ready, i + 1)
                act.dma_start(gate_dram[i // 4:i // 4 + 1, (i % 4) * W:(i % 4 + 1) * W],
                              rowbuf[0:1, :]).then_inc(row_stored, 16)

            def weight_high(kind, n, k):
                if k == 0:
                    ring_arrived(act, (kind, n))
                wait_high_free(act, kind, n, k)
                act.copy(high_of(kind, n, k)[:], wide((kind, n))[:, k, :]).then_inc(w_hi, 1)

            act.wait_ge(corr_mm, 1)
            act.copy(rowbuf[0:1, :], ps[0:1, 1, :]).then_inc(corr_out, 1)
            act.wait_ge(u_mm, 4)
            seq(act.copy(u_shift[:], ps[:, 0, 480:484]))
            for j in range(8):
                act.wait_ge(u_mm, pair(j))
                src = ps[:, 4 + j // 2, (j % 2) * T:(j % 2 + 1) * T]
                if j < 4:
                    act.activation(uT[:, j, :], src, ACT.Identity, bias=u_shift[:, j:j + 1]).then_inc(u_out, 1)
                else:
                    act.copy(uT[:, j, :], src).then_inc(u_out, 1)
            gate_row(8, 0)
            for n in range(2):
                cols = W if n == 0 else LAT - W
                for tt in range(TT):
                    act.wait_ge(lat_mm, 2 * n + tt + 1)
                    act.copy(lat[:, tt, n * W:n * W + cols], ps[:, 4 + 2 * n + tt, 0:cols]).then_inc(lat_out, 1)
                    r = QR if n == 0 else KVR
                    seq(act.activation(qrope[:, 0, 0:r], ps[:, 4 + 2 * n + tt, 0:r], ACT.Square,
                                       accum_out=stat[:, 8 + 2 * n + tt:9 + 2 * n + tt]))
                    if n == 0:
                        gate_row(9 + tt, 16 + 16 * tt)
            act.nop().then_inc(lat_sq, 1)
            act.wait_ge(lat_sq, 2)
            act.activation(stat[:, 16:20], stat[:, 12:16], ACT.Sqrt).then_inc(lat_sq, 1)
            for r in range(6):
                act.wait_ge(cT_mm, pair(r))
                act.activation(cT[:, r, :], ps[:, 2 + (r // 2) % 2, (r % 2) * T:(r % 2 + 1) * T], ACT.Identity,
                               scale=vcols[:, V_QN + r:V_QN + r + 1]).then_inc(cT_out, 1)
            for h in range(HEADS):
                act.wait_ge(qn_mm, pair(h))
                if h == 0:
                    act.wait_ge(u_mm, 8)
                act.copy(qnT[:, h, :], ps[:, 4 + h // 2, (h % 2) * T:(h % 2 + 1) * T]).then_inc(qn_out, 1)
            for j in range(8):
                act.wait_ge(pool_mm, pair(j))
                act.activation(catT[:, j, :], ps[:, 4 + j // 2, (j % 2) * T:(j % 2 + 1) * T], ACT.Identity,
                               scale=vcols[:, V_PS + j:V_PS + j + 1]).then_inc(pool_out, 1)
            gate_row(11, 48)
            for h in range(HEADS):
                act.wait_ge(kn_mm, pair(h))
                act.copy(knT[:, h, :], ps[:, 4 + h // 2, (h % 2) * T:(h % 2 + 1) * T]).then_inc(kn_out, 1)
            for j in range(4):
                act.wait_ge(v_mm, j + 1)
                act.copy(vv[:, j // 2, (j % 2) * W:(j % 2 + 1) * W], ps[:, 4 + j, :]).then_inc(v_out, 1)
            act.wait_ge(qpeT_mm, 1)
            seq(act.copy(qpeT[:].rearrange("p a t -> p (a t)"), ps[:, 2:4, :].rearrange("p a t -> p (a t)")))
            seq(act.copy(kpeT[:], ps[:, 0, T:2 * T]))
            act.nop().then_inc(qpeT_out, 1)

            def exps(h):
                act.wait_ge(s_max, h + 1)
                for qb in range(TT):
                    s = s_sb[:, h % 2, qb * P:qb * P + (qb + 1) * P]
                    e = act.activation(s, s, ACT.Exp, bias=stat[:, 20 + 2 * (h % 2) + qb:21 + 2 * (h % 2) + qb],
                                       accum_out=stat[:, 24 + 2 * (h % 2) + qb:25 + 2 * (h % 2) + qb])
                    e.then_inc(s_exp, 1)

            def outs(h):
                act.wait_ge(pT_mm, h + 1)
                if h >= 2:
                    act.wait_ge(o_mm, h - 1)
                act.copy(pT[:, h % 2, :], ps[:, 6 + h % 2, 0:3 * P]).then_inc(pT_out, 1)
                act.wait_ge(o_mm, h + 1)
                act.copy(catT[:, 8 + h, :], ps[:, 2 + h % 2, 0:T]).then_inc(o_out, 1)
                act.wait_ge(o_out, h + 1)
                act.copy(cat_high(8 + h), catT[:, 8 + h, :]).then_inc(cat_hi, 1)

            act.wait_ge(k_roped, 1)
            for h in range(HEADS + 1):
                if h < HEADS:
                    exps(h)
                if h >= 1:
                    outs(h - 1)
                if h == 1:
                    act.wait_ge(pool_out, 8)
                    act.copy(catH_a[:, 0:8, :], catT[:, 0:8, :]).then_inc(cat_hi, 1)

            def y_chunk(n):
                for tt in range(TT):
                    act.wait_ge(y_mm, 2 * n + tt + 1)
                    b = 4 + (n % 2) * 2 + tt
                    seq(act.activation(y1[:, tt, n * W:(n + 1) * W], ps[:, b, :], ACT.Square,
                                       accum_out=stat[:, 28 + tt * 4 + n:29 + tt * 4 + n]))
                    act.copy(y1[:, tt, n * W:(n + 1) * W], ps[:, b, :]).then_inc(y_out, 1)

            act.wait_ge(s_mm, HEADS)
            act.wait_ge(s_max, HEADS)
            for n in range(4):
                for k in range(KT):
                    weight_high("wout", n, k)
                    if n and k == len(wout_high) - 1:
                        y_chunk(n - 1)
            y_chunk(3)
            for k in range(len(wq_high)):
                weight_high("wq", 0, k)
            act.wait_ge(y_rc, 1)
            act.activation(stat[:, 38:40], stat[:, 36:38], ACT.Sqrt).then_inc(y_rs, 1)
            for tt in range(TT):
                act.wait_ge(x1_done, tt + 1)
                seq(act.activation(junk[:], x1q[:, tt, :], ACT.Square, accum_out=stat[:, 40 + tt:41 + tt]))
            act.nop().then_inc(x1_sq, 1)
            act.wait_ge(x1_rs, 1)
            act.activation(stat[:, 44:46], stat[:, 42:44], ACT.Sqrt).then_inc(x1_rs, 1)
            act.wait_ge(mod2_ready, 2)
            for k in range(KT):
                act.wait_ge(x1T_mm, pair(k))
                b, half = 2 + (k // 2) % 2, k % 2
                act.activation(h2T[:, k, :], ps[:, b, half * T:(half + 1) * T], ACT.Identity,
                               bias=mod2[:, 1, k:k + 1], scale=mod2[:, 0, k:k + 1]).then_inc(h2_out, 1)
                if k == 0:
                    act.wait_ge(y_mm, 8)
                act.wait_ge(h2_out, k + 1)
                act.copy(h2H[:, k, :], h2T[:, k, :]).then_inc(h2H_out, 1)
            act.wait_ge(x1_stored, 16)
            act.wait_ge(x1T_mm, KT)
            def q_chunk(n):
                for i in range(4 * n, 4 * n + 4):
                    act.wait_ge(qT_mm, i + 1)
                    act.copy(qT[:, i, :], ps[:, [4, 5, 6, 7, 2, 3][i % 6], 0:T]).then_inc(qT_out, 1)
                gate_row(20 + n, 64 + 16 * n)

            for n in range(4):
                for k in range(KT):
                    if n or k >= len(wq_high):
                        weight_high("wq", n, k)
                    if n and k == len(wq_high) - 1:
                        q_chunk(n - 1)
            q_chunk(3)
            for j in range(4):
                act.wait_ge(key_mm, j + 1)
                act.copy(keyT[:, 4 * j:4 * j + 4, :].rearrange("p k n -> p (k n)"),
                         ps[:, 2 + j % 2, :]).then_inc(key_out, 1)
            for j in range(8):
                act.wait_ge(sc_mm, j + 1)
                act.copy(sc[:, 4 * j:4 * j + 4, :].rearrange("p k n -> p (k n)"),
                         ps[:, 4 + j % 4, :]).then_inc(sc_out, 1)
            def gelu(tile, bank):
                act.wait_ge(u_used, tile * 2 + 2)
                act.activation(acts[:, bass.ds(tile, 1), :], ps[:, bank, 0:T], ACT.Gelu).then_inc(a_out, 1)

            def u_round(r, tiles=ROUND, first=False):
                for j in range(2 * tiles):
                    act.wait_ge(u_tr, r * (2 * ROUND) + (j + 1))
                    if not (first and j < RING):
                        act.wait_ge(u_used, r * (2 * ROUND) + (j + 1 - RING))
                    act.copy(by_k(eH[:, j % RING, :]), turned(raw[:, j % RAW, :])).then_inc(u_hi, 1)
                    if j % 2 == 1 and not (first and j == 1):
                        gelu(r * ROUND + (j // 2 - 1), (j // 2 - 1) % 3)

            u_round(0, first=True)
            with act.Fori(1, REST + 1) as r:
                u_round(r)
            act.wait_ge(g_shift, 1)
            act.activation(gtmp[:], gtmp[:], ACT.Exp).then_inc(g_exp, 1)
            u_round(REST + 1)
            u_round(REST + 2)
            act.wait_ge(slot_mm, 1)
            seq(act.copy(slotT[:, 0:2, :].rearrange("p a t -> p (a t)"), ps[:, 4, :]))
            act.copy(slotT[:, 2, :], ps[:, 5, 0:T]).then_inc(slotT_out, 1)
            with act.Fori(REST + 3, ROUNDS) as r:
                u_round(r)
            u_round(ROUNDS, TILES % ROUND)
            gelu(TILES - 1, 1)

            def hot_first(g, half, first):
                if not first:
                    act.wait_ge(hot_mm, g - 1)
                for t in range(2):
                    last_ = act.activation(hotA[:, half, t, :], iota, ACT.Abs,
                                           bias=slotT[:, 1, bass.ds(g * 4 + t, 1)], scale=-1.0)
                last_.then_inc(hot_abs, 1)
                act.wait_ge(hot_abs, g + 1)
                o = hotA[:, half, 0:2, :]
                act.activation(o, o, ACT.Relu, bias=ones[:, 0:1], scale=-1.0).then_inc(hot_act, 1)

            act.wait_ge(u_used, 2 * TILES)
            act.wait_ge(slotT_out, 1)
            hot_first(0, 0, True)
            hot_first(1, 1, True)
            with act.Fori(1, T // 8) as r:
                hot_first(r * 2, 0, False)
                hot_first(r * 2 + 1, 1, False)

            def v_tile(tile, j, first, rounds):
                if not first:
                    act.wait_ge(v_used, tile * 2 - 4)
                act.copy(aH[j][:], acts[:, bass.ds(tile, 1), :]).then_inc(act_hi, 1)
                for h in range(2):
                    g = 2 * j + h
                    slot = g % RING
                    act.wait_ge(v_in[slot], rounds(g))
                    if not (first and g < RING):
                        act.wait_ge(v_used, tile * 2 + (h - RING + 1))
                    act.copy(eH[:, slot, :], raw[:, slot, :]).then_inc(v_hi, 1)

            act.wait_ge(row_stored, 128)
            act.wait_ge(gated, T // 4)
            act.wait_ge(hot_mm, T // 4)
            for j in range(3):
                v_tile(j, j, True, lambda g: 16 * (g // RING + 1))
            with act.Fori(1, TILES // 3) as r:
                for j in range(3):
                    v_tile(r * 3 + j, j, False, lambda g: r * 32 + 16 * (g // RING + 1))
            for j in range(2):
                v_tile(TILES - 2 + j, j, False, lambda g: 32 * (TILES // 3) + 16 * (g // RING + 1))

            act.wait_ge(v_used, 2 * TILES)
            for tt in range(TT):
                seq(act.activation(raw[:, 0:2, :].rearrange("p a b -> p (a b)"),
                                   ps[:, 4 * tt:4 * tt + 4, :].rearrange("p a b -> p (a b)"), ACT.Square,
                                   accum_out=stat[:, 46 + tt:47 + tt]))
            act.nop().then_inc(y2_sq, 1)
            act.wait_ge(y2_rc, 1)
            act.activation(stat[:, 50:52], stat[:, 48:50], ACT.Sqrt).then_inc(y2_rs, 1)

        @block.vector
        def _(dve):
            count = [0]

            def seq(ins):
                count[0] += 1
                ins.then_inc(dve_chain, 1)
                dve.wait_ge(dve_chain, count[0])

            def ada(n, part=None):
                a, b = acc[:, n % 2, :], acc_b[:, n % 2, :]
                w = wide(("ada", n))
                if part != 1:
                    ring_arrived(dve, ("ada", n))
                    dve.wait_ge(init_in[n % 2], 16 * (n // 2 + 1))
                    if n >= 2:
                        dve.wait_ge(acc_used, n - 1)
                for k in {None: range(KT), 0: range(KT // 2), 1: range(KT // 2, KT)}[part]:
                    if k >= 2:
                        dve.wait_ge(dve_chain, count[0] - 1)
                    if k == 1:
                        ins = dve.tensor_scalar(b, w[:, k, :], c_act[:, k:k + 1], None, ALU.mult)
                    else:
                        s_ = b if k % 2 else a
                        ins = dve.scalar_tensor_tensor(s_, w[:, k, :], c_act[:, k:k + 1],
                                                       init[:, n % 2, :] if k == 0 else s_, ALU.mult, ALU.add)
                    if k < KT - 1:
                        count[0] += 1
                        ins.then_inc(dve_chain, 1)
                if part != 0:
                    ins.then_inc(acc_ready, 1)
                    dve.wait_ge(dve_chain, count[0])

            def inverse_mean(dst, src, width):
                seq(dve.tensor_scalar(dst, src, 1.0 / width, EPS, ALU.mult, ALU.add))
                seq(dve.reciprocal(dst, dst))

            dve.wait_ge(silu_done, 1)
            for n in range(2):
                ada(n)
            dve.wait_ge(vec_t, 1)
            seq(dve.tensor_copy(vcols[:], ps[:, 1, 0:V_ALL]))
            dve.nop().then_inc(vec_cols, 1)
            seq(dve.tensor_copy(pos_f[:], pos_i[:]))
            for tt in range(TT):
                seq(dve.tensor_scalar(ang[:, 0, tt * HALF:(tt + 1) * HALF], freq[:], pos_f[:, tt:tt + 1], None,
                                      ALU.mult))
            magic = 12582912.0
            seq(dve.tensor_scalar(ang[:, 3, :], ang[:, 0, :], 1.0 / (TWO_PI_A + TWO_PI_B + TWO_PI_C), None, ALU.mult))
            seq(dve.tensor_scalar(ang[:, 3, :], ang[:, 3, :], magic, None, ALU.add))
            seq(dve.tensor_scalar(ang[:, 3, :], ang[:, 3, :], magic, None, ALU.subtract))
            seq(dve.scalar_tensor_tensor(ang[:, 1, :], ang[:, 3, :], -TWO_PI_A, ang[:, 0, :], ALU.mult, ALU.add))
            seq(dve.scalar_tensor_tensor(ang[:, 1, :], ang[:, 3, :], -TWO_PI_B, ang[:, 1, :], ALU.mult, ALU.add))
            seq(dve.scalar_tensor_tensor(ang[:, 1, :], ang[:, 3, :], -TWO_PI_C, ang[:, 1, :], ALU.mult, ALU.add))
            pi = 3.1415925
            seq(dve.tensor_scalar(ang[:, 1, :], ang[:, 1, :], pi, -pi, ALU.min, ALU.max))
            seq(dve.tensor_scalar(ang[:, 2, :], ang[:, 1, :], -1.0, None, ALU.mult))
            seq(dve.tensor_tensor(ang[:, 2, :], ang[:, 2, :], ang[:, 1, :], ALU.max))
            seq(dve.tensor_scalar(ang[:, 2, :], ang[:, 2, :], -1.0, 1.5707963267948966, ALU.mult, ALU.add))
            dve.nop().then_inc(trig_arg, 1)

            ada(2)
            dve.wait_ge(x_sq, 1)
            inverse_mean(stat[:, 2:4], stat[:, 0:2], D)
            dve.nop().then_inc(x_rs, 1)
            dve.wait_ge(x_rs, 2)
            for tt in range(TT):
                seq(dve.tensor_scalar(diag[:, tt, :], ident, stat[:, 4 + tt:5 + tt], None, ALU.mult))
                dve.nop().then_inc(diag1, 1)
            ada(3)
            dve.wait_ge(acc_used, 4)
            seq(dve.scalar_tensor_tensor(mod1[:, 0, :], ps[:, 0, 0:KT], 1.0, vcols[:, V_G1:V_G1 + KT],
                                         ALU.add, ALU.mult))
            dve.nop().then_inc(mod1_ready, 1)
            for n in range(4, 8):
                ada(n)
            dve.wait_ge(acc_used, 8)
            seq(dve.tensor_copy(mod1[:, 1, :], ps[:, 0, KT:2 * KT]))
            dve.nop().then_inc(mod1_ready, 1)
            dve.wait_ge(hA_used, 1)
            for q in range(4):
                h = hT[:, 4 * q:4 * q + 4, :]
                dve.tensor_tensor(h, h, mod1[:, 1, 4 * q:4 * q + 4].unsqueeze(2).broadcast_to([P, 4, T]),
                                  ALU.add).then_inc(hB_done, 1)
            for n in range(8, 10):
                ada(n)
            dve.wait_ge(trig_ready, 2)

            t2, t4 = zT, uT
            dve.wait_ge(u_out, 8)
            for g, w in enumerate(WINDOWS):
                u = uT[:, 2 * g:2 * g + 2, :]
                z = zT[:, 2 * g:2 * g + 2, :]
                s = pool_tmp = [catT[:, 0:2, :], catT[:, 2:4, :]]
                src = u
                step = 1
                i = 0
                while step < w:
                    d = s[i % 2]
                    seq(dve.tensor_copy(d[:, :, 0:step], src[:, :, 0:step]))
                    seq(dve.tensor_tensor(d[:, :, step:T], src[:, :, step:T], src[:, :, 0:T - step], ALU.add))
                    src = d
                    step *= 2
                    i += 1
                seq(dve.scalar_tensor_tensor(z, src, 1.0 / w, u, ALU.mult, ALU.subtract))
                for ct in range(2):
                    o = s[i % 2][:, ct, 0:16]
                    seq(dve.tensor_tensor(o, src[:, ct, 0:16], cnt[:, g, :], ALU.mult))
                    seq(dve.tensor_tensor(z[:, ct, 0:16], o, u[:, ct, 0:16], ALU.subtract))
                dve.nop().then_inc(z_ready, 1)
            ada(10)

            dve.wait_ge(lat_sq, 1)
            seq(dve.tensor_scalar(stat[:, 12:14], stat[:, 8:10], 1.0 / QR, EPS, ALU.mult, ALU.add))
            seq(dve.tensor_scalar(stat[:, 14:16], stat[:, 10:12], 1.0 / KVR, EPS, ALU.mult, ALU.add))
            seq(dve.reciprocal(stat[:, 12:16], stat[:, 12:16]))
            dve.nop().then_inc(lat_sq, 1)
            dve.wait_ge(lat_sq, 3)
            dve.wait_ge(xT_done, KT)
            for tt in range(TT):
                seq(dve.tensor_scalar(diag[:, tt, :], ident, stat[:, 16 + tt:17 + tt], None, ALU.mult))
                dve.nop().then_inc(lat_diag, 1)
                seq(dve.tensor_scalar(tmpr[:, tt, 0:P], ident, stat[:, 18 + tt:19 + tt], None, ALU.mult))
                dve.nop().then_inc(lat_diag, 1)
            dve.wait_ge(trig_ready, 2)
            dve.wait_ge(lat_out, 4)

            def rotate(dst, src, tt, heads, t1):
                cos, sin = (trig[:, i, tt, :].unsqueeze(1).broadcast_to([P, heads, HALF]) for i in range(2))
                x1_, x2_ = src[:, :, 0:HALF], src[:, :, HALF:ROPE]
                tv = t1[:, 0:heads * HALF].rearrange("p (h f) -> p h f", h=heads)
                seq(dve.tensor_tensor(tv, x2_, sin, ALU.mult))
                seq(dve.tensor_tensor(dst[:, :, 0:HALF], x1_, cos, ALU.mult))
                seq(dve.tensor_tensor(dst[:, :, 0:HALF], dst[:, :, 0:HALF], tv, ALU.subtract))
                seq(dve.tensor_tensor(tv, x1_, sin, ALU.mult))
                seq(dve.tensor_tensor(dst[:, :, HALF:ROPE], x2_, cos, ALU.mult))
                seq(dve.tensor_tensor(dst[:, :, HALF:ROPE], dst[:, :, HALF:ROPE], tv, ALU.add))

            for tt in range(TT):
                kp = krope[:, tt, :].rearrange("p (h f) -> p h f", h=2)
                rotate(kp[:, 0:1, :], lat[:, tt, QR + KVR:LAT].rearrange("p (h f) -> p h f", h=1), tt, 1,
                       tmpr[:, 1, P:2 * P])
                seq(dve.tensor_copy(kp[:, 1:2, :], kp[:, 0:1, :]))
            dve.nop().then_inc(k_roped, 1)
            ada(11)
            dve.wait_ge(qpe_mm, 2)
            dve.wait_ge(cT_mm, 6)
            for tt in range(TT):
                rotate(qrope[:, tt, :].rearrange("p (h f) -> p h f", h=HEADS),
                       ps[:, 2 + tt, :].rearrange("p (h f) -> p h f", h=HEADS), tt, HEADS, tmpr[:, 0, :])
            dve.nop().then_inc(q_roped, 1)
            ada(12)

            def maxima(h):
                dve.wait_ge(s_mm, h + 1)
                if h >= 2:
                    dve.wait_ge(pT_mm, h - 1)
                s = s_sb[:, h % 2, :]
                seq(dve.scalar_tensor_tensor(s, ps[:, 4 + h % 2, 0:3 * P], SCALE, mask[:], ALU.mult, ALU.add))
                for qb in range(TT):
                    m = stat[:, 20 + 2 * (h % 2) + qb:21 + 2 * (h % 2) + qb]
                    seq(dve.tensor_reduce(m, s[:, qb * P:qb * P + (qb + 1) * P], AX_X, ALU.max, negate=True))
                dve.nop().then_inc(s_max, 1)

            def normalise(h):
                dve.wait_ge(s_exp, 2 * (h + 1))
                r = stat[:, 24 + 2 * (h % 2):26 + 2 * (h % 2)]
                seq(dve.reciprocal(r, r))
                for qb in range(TT):
                    s = s_sb[:, h % 2, qb * P:qb * P + (qb + 1) * P]
                    seq(dve.tensor_scalar(s, s, r[:, qb:qb + 1], None, ALU.mult))
                dve.nop().then_inc(s_norm, 1)

            for h in range(HEADS + 1):
                if h < HEADS:
                    maxima(h)
                if h >= 1:
                    normalise(h - 1)
                if h >= 1:
                    ada(13 + (h - 1) // 2, (h - 1) % 2)
            for n in range(17, 20):
                ada(n)

            dve.wait_ge(acc_used, 20)
            seq(dve.tensor_copy(mod2[:, 1, :], ps[:, 0, 64:64 + KT]))
            dve.nop().then_inc(mod2_ready, 1)
            seq(dve.scalar_tensor_tensor(mod2[:, 0, :], ps[:, 0, 64 + KT:64 + 2 * KT], 1.0,
                                         vcols[:, V_G2:V_G2 + KT], ALU.add, ALU.mult))
            dve.nop().then_inc(mod2_ready, 1)
            dve.wait_ge(g1_in, 32)
            seq(dve.tensor_tensor(gate1[:], gate1[:], post1[:], ALU.mult))
            dve.wait_ge(y_out, 8)
            for tt in range(TT):
                seq(dve.tensor_reduce(stat[:, 36 + tt:37 + tt], stat[:, 28 + 4 * tt:32 + 4 * tt], AX_X, ALU.add))
            inverse_mean(stat[:, 36:38], stat[:, 36:38], D)
            dve.nop().then_inc(y_rc, 1)
            dve.wait_ge(y_rs, 1)
            for tt in range(TT):
                seq(dve.scalar_tensor_tensor(y1[:, tt, :], y1[:, tt, :], stat[:, 38 + tt:39 + tt], gate1[:],
                                             ALU.mult, ALU.mult))
                seq(dve.tensor_tensor(x1q[:, tt, :].rearrange("p (k q l) -> p q k l", q=4, l=QUAD),
                                      xs[:, tt, :].rearrange("p (q k l) -> p q k l", q=4, l=QUAD),
                                      y1[:, tt, :].rearrange("p (q k l) -> p q k l", q=4, l=QUAD), ALU.add))
                dve.nop().then_inc(x1_done, 1)
            dve.wait_ge(x1_sq, 1)
            inverse_mean(stat[:, 42:44], stat[:, 40:42], D)
            dve.nop().then_inc(x1_rs, 1)
            dve.wait_ge(x1_rs, 2)
            dve.wait_ge(cT_mm, 6)
            for tt in range(TT):
                seq(dve.tensor_scalar(diag[:, tt, :], ident, stat[:, 44 + tt:45 + tt], None, ALU.mult))
                dve.nop().then_inc(diag2, 1)
            for k in range(KT):
                dve.wait_ge(h2H_out, k + 1)
                dve.tensor_tensor(h2L[:, k, :], h2T[:, k, :], h2H[:, k, :].bitcast(F32),
                                  ALU.subtract).then_inc(h2L_out, 1)

            for n in range(20, 24):
                ada(n)

            def row(t, i):
                return t[:, bass.ds(i, 1), :].rearrange("p a k -> p (a k)")

            def after(n):
                dve.wait_ge(pick_chain, n)

            def after_by_copy(n):
                after(n)
                dve.tensor_copy(idle[:], ones[:, 0:1]).then_inc(pick_chain, 1)

            def best_16(v, ix, c0):
                n = v.shape[-1]
                after_by_copy(c0 + 1)
                dve.max(picked[:, 0:8], v).then_inc(pick_chain, 1)
                after_by_copy(c0 + 3)
                dve.max_index(picked_at[:, 0:8], picked[:, 0:8], v).then_inc(pick_chain, 1)
                dve.match_replace(rest[:, 0:n], picked[:, 0:8], v, -BIG).then_inc(pick_chain, 1)
                after_by_copy(c0 + 6)
                dve.max(picked[:, 8:16], rest[:, 0:n]).then_inc(pick_chain, 1)
                after_by_copy(c0 + 8)
                dve.max_index(picked_at[:, 8:16], picked[:, 8:16], rest[:, 0:n]).then_inc(pick_chain, 1)
                after(c0 + 10)
                dve.tensor_copy(ix, picked_at[:]).then_inc(pick_chain, 1)

            def pick_keys(i, c0):
                dve.tensor_copy(cand[:, 0:NK], row(sc, i)).then_inc(pick_chain, 1)
                best_16(cand[:, 0:NK], row(i16f, i), c0)
                dve.tensor_copy(row(s16, i), picked[:]).then_inc(pick_chain, 1)

            def pick_pairs(i, c0):
                after(c0)
                s0 = row(s16, i * 2).unsqueeze(2).broadcast_to([P, TOPK, TOPK])
                s1 = row(s16, i * 2 + 1).unsqueeze(1).broadcast_to([P, TOPK, TOPK])
                dve.tensor_tensor(cand[:].rearrange("p (a b) -> p a b", a=TOPK), s0, s1,
                                  ALU.add).then_inc(pick_chain, 1)
                best_16(cand[:], row(posu, i), c0)
                dve.tensor_copy(row(best, i), picked[:]).then_inc(pick_chain, 1)

            def gates_before_exp():
                after(KEY_PICKS + PICK_STEPS * TT * PH)
                seq(dve.tensor_tensor(gtmp[:], best[:], best[:, :, 0:1].broadcast_to([P, TT * PH, TOPK]),
                                      ALU.subtract))
                dve.nop().then_inc(g_shift, 1)
                pu = posu[:].rearrange("p (t h) k -> p t (h k)", t=TT)
                seq(dve.tensor_scalar(posa[:], pu, 4, None, ALU.logical_shift_right))
                seq(dve.tensor_copy(posf[:, 0], posa[:]))
                seq(dve.tensor_scalar(posa[:], pu, 15, None, ALU.bitwise_and))
                seq(dve.tensor_copy(posf[:, 1], posa[:]))

            def gates_after_exp():
                dve.wait_ge(g_exp, 1)
                seq(dve.tensor_reduce(gsum[:], gtmp[:], AX_X, ALU.add))
                seq(dve.reciprocal(gsum[:], gsum[:]))
                seq(dve.tensor_tensor(slots[:, 2].rearrange("p t (h k) -> p (t h) k", h=PH), gtmp[:],
                                      gsum[:].unsqueeze(2).broadcast_to([P, TT * PH, TOPK]), ALU.mult))

            def sub_keys(step):
                tt, p, part = step // 6, step // 3 % 2, step % 3
                eq = tmpk[:].rearrange("p (h k a) -> p h k a", h=PH, k=TOPK)
                pr = tmpk2[:].rearrange("p (h k a) -> p h k a", h=PH, k=TOPK)
                if part == 0:
                    seq(dve.tensor_tensor(
                        eq.rearrange("p h k a -> p (h k) a"),
                        posf[:, p, tt, :].unsqueeze(2).broadcast_to([P, PH * TOPK, TOPK]),
                        i16[:].unsqueeze(1).broadcast_to([P, PH * TOPK, TOPK]), ALU.is_equal))
                elif part == 1:
                    tab = i16f[:, tt * KT:(tt + 1) * KT].rearrange("p (h s) a -> p h s a", s=2)[:, :, p, :]
                    seq(dve.tensor_tensor(pr, eq, tab.unsqueeze(2).broadcast_to([P, PH, TOPK, TOPK]), ALU.mult))
                else:
                    seq(dve.tensor_reduce(slots[:, p, tt, :], pr.rearrange("p h k a -> p (h k) a"), AX_X, ALU.add))

            def u_low(r, j, first=False):
                dve.wait_ge(u_hi, r * (2 * ROUND) + (j + 1))
                if not first:
                    dve.wait_ge(u_used, r * (2 * ROUND) + (j + 1 - RING))
                dve.tensor_tensor(by_k(eL[:, j % RING, :]), turned(raw[:, j % RAW, :]),
                                  by_k(eH[:, j % RING, :].bitcast(F32)), ALU.subtract).then_inc(u_lo, 1)

            def u_round(r, tiles=ROUND, first=False, beside=None):
                for j in range(2 * tiles):
                    dve.wait_ge(raw_in[j % RAW], r * (64 * 2 * ROUND // RAW) + 64 * (j // RAW + 1))
                    dve.transpose(raw[:, j % RAW, :], raw[:, j % RAW, :]).then_inc(u_tr, 1)
                    if j % 2:
                        u_low(r, j - 1, first and j - 1 < RING)
                    if beside:
                        beside(j)

            PICK_STEPS = 12
            KEY_PICKS = PICK_STEPS * TT * KT

            def beside_keys(r):
                def work(j):
                    if j % 3 == 0:
                        pick_keys(r * 4 + j // 3, r * (4 * PICK_STEPS) + PICK_STEPS * (j // 3))
                return work

            def beside_pairs(r):
                def work(j):
                    if j % 4 == 2:
                        pick_pairs((r - KEY_ROUNDS) * 3 + j // 4, 
                                   (r - KEY_ROUNDS) * (3 * PICK_STEPS) + (KEY_PICKS + PICK_STEPS * (j // 4)))
                return work

            def beside_rest(i):
                def work(j):
                    if i == 0 and j == 0:
                        pick_pairs(TT * PH - 1, KEY_PICKS + PICK_STEPS * (TT * PH - 1))
                    if i == 0 and j == 3:
                        gates_before_exp()
                    if i == 1 and j == 0:
                        gates_after_exp()
                    if j % 2 and j + 12 * i >= 7 and (j + 12 * i - 7) // 2 < 12:
                        sub_keys((j + 12 * i - 7) // 2)
                return work

            dve.wait_ge(sc_out, 8)
            u_round(0, first=True, beside=beside_keys(0))
            with dve.Fori(1, KEY_ROUNDS) as r:
                u_round(r, beside=beside_keys(r))
            with dve.Fori(KEY_ROUNDS, REST) as r:
                u_round(r, beside=beside_pairs(r))
            for i in range(3):
                u_round(REST + i, beside=beside_rest(i))
            dve.nop().then_inc(slots_ready, 1)
            with dve.Fori(REST + 3, ROUNDS) as r:
                u_round(r)
            u_round(ROUNDS, TILES % ROUND)

            def hots(g, half, first):
                if not first:
                    dve.wait_ge(hot_mm, g - 1)
                for t in range(4):
                    i1, gt = (slotT[:, m, bass.ds(g * 4 + t, 1)] for m in (0, 2))
                    last_ = dve.tensor_scalar(hotB[:, half, t, :], iota, i1, gt, ALU.is_equal, ALU.mult)
                last_.then_inc(hot_ready, 1)

            def apply_gates(g, half):
                dve.wait_ge(hot_mm, g + 1)
                a = acts[:, :, bass.ds(g * 4, 4)]
                dve.tensor_tensor(a, a, ps[:, half, :].rearrange("p (t i) -> p i t", t=4), ALU.mult).then_inc(gated, 1)

            dve.wait_ge(slotT_out, 1)
            dve.wait_ge(a_out, TILES)
            dve.wait_ge(u_used, 2 * TILES)
            hots(0, 0, True)
            hots(1, 1, True)
            apply_gates(0, 0)
            with dve.Fori(1, T // 8) as r:
                hots(r * 2, 0, False)
                apply_gates(r * 2 - 1, 1)
                hots(r * 2 + 1, 1, False)
                apply_gates(r * 2, 0)
            apply_gates(T // 4 - 1, 1)

            def v_tile(tile, j, first):
                dve.wait_ge(act_hi, tile + 1)
                if not first:
                    dve.wait_ge(v_used, tile * 2 - 4)
                dve.tensor_tensor(aL[j][:], acts[:, bass.ds(tile, 1), :].rearrange("p a t -> p (a t)"),
                                  aH[j][:].bitcast(F32), ALU.subtract).then_inc(act_lo, 1)
                for h in range(2):
                    slot = (2 * j + h) % RING
                    dve.wait_ge(v_hi, tile * 2 + (h + 1))
                    dve.tensor_tensor(eL[:, slot, :], raw[:, slot, :], eH[:, slot, :].bitcast(F32),
                                      ALU.subtract).then_inc(v_lo, 1)

            for j in range(3):
                v_tile(j, j, True)
            with dve.Fori(1, TILES // 3) as r:
                for j in range(3):
                    v_tile(r * 3 + j, j, False)
            for j in range(2):
                v_tile(TILES - 2 + j, j, False)

            dve.wait_ge(tail_in, 48)
            seq(dve.tensor_tensor(gate2[:], gate2[:], post2[:], ALU.mult))
            dve.wait_ge(y2_sq, 1)
            inverse_mean(stat[:, 48:50], stat[:, 46:48], D)
            dve.nop().then_inc(y2_rc, 1)
            dve.wait_ge(y2_rs, 1)
            for tt in range(TT):
                seq(dve.scalar_tensor_tensor(post2[:], ps[:, 4 * tt:4 * tt + 4, :].rearrange("p a b -> p (a b)"),
                                             stat[:, 50 + tt:51 + tt], gate2[:], ALU.mult, ALU.mult))
                seq(dve.tensor_tensor(post2[:].rearrange("p (q k l) -> p q k l", q=4, l=QUAD),
                                      x1[:, tt, :].rearrange("p (k q l) -> p q k l", q=4, l=QUAD),
                                      post2[:].rearrange("p (q k l) -> p q k l", q=4, l=QUAD), ALU.add))
                seq(dve.tensor_copy(x1[:, tt, :], post2[:]))
                dve.nop().then_inc(out_ready, 1)


def constant_table(np):
    t = np.zeros((P, C_ALL), np.float32)
    t[:, C_ID:C_ID + P] = np.eye(P)
    t[:, C_ONE:C_ONE + P] = 1.0
    t[:, C_IOTA:C_IOTA + P] = np.arange(P)
    for start in (C_MASK, C_MASK + 2 * P):
        t[0:P // 2, start + P // 2:start + P] = -1e30
    half = np.arange(HALF, dtype=np.float32) / np.float32(HALF)
    t[:, C_FREQ:C_FREQ + HALF] = np.float32(10000.0) ** (-half)
    for g, w in enumerate(WINDOWS):
        t[:, C_CNT + 16 * g:C_CNT + 16 * (g + 1)] = 1.0 / np.minimum(np.arange(16) + 1, w)
    t[:, C_I16:C_I16 + 16] = np.arange(16)
    return t


_INS = ['x', 'c', 'positions', 'ada_w', 'ada_b', 'pre_mix_g', 'post_mix_g', 'pre_ffn_g', 'post_ffn_g',
        'w_in', 'pool_w', 'pool_scale', 'q_norm_g', 'w_uq', 'kv_norm_g', 'w_ukv', 'w_out',
        'peer_wq', 'peer_sub_keys', 'peer_u', 'peer_v']
_OUTS = [((1, 256, 2048), 'float32')]


def kernel(**inputs):
    import numpy as _np
    import concourse.bacc as _bacc
    from concourse import mybir as _mybir
    from concourse.bass_utils import run_bass_kernel_spmd as _run

    nc = _bacc.Bacc("TRN2", target_bir_lowering=False, num_devices=1)
    arrays, args = {}, []
    for name in _INS:
        a = _np.ascontiguousarray(inputs[name])
        arrays[f"in_{name}_dram"] = a
        args.append(nc.dram_tensor(f"in_{name}_dram", a.shape, _mybir.dt.from_np(a.dtype), kind="ExternalInput").ap())
    table = constant_table(_np)
    arrays["consts_dram"] = table
    args.append(nc.dram_tensor("consts_dram", table.shape, _mybir.dt.float32, kind="ExternalInput").ap())
    for i, (shape, dtype) in enumerate(_OUTS):
        dt = _mybir.dt.from_np(_np.dtype(dtype))
        args.append(nc.dram_tensor(f"out_{i}_dram", shape, dt, kind="ExternalOutput").ap())
    hybrid_block(nc, *args)
    r = _run(nc, [arrays], core_ids=[0])
    got = tuple(r.results[0][f"out_{i}_dram"] for i in range(len(_OUTS)))
    return got[0]
```

```python
import concourse.bass as bass
from concourse import mybir

F32 = mybir.dt.float32
F32R = mybir.dt.float32r
U32 = mybir.dt.uint32
I32 = mybir.dt.int32
ALU = mybir.AluOpType
ACT = mybir.ActivationFunctionType
AX_X = mybir.AxisListType.X

P = 128
D = 2048
T = 256
TT = T // P
KT = D // P
W = 512
POOL_W = 1024
WINDOWS = (2, 4, 8, 16)
HEADS = 8
NOPE = 128
ROPE = 64
HALF = ROPE // 2
QR = 512
KVR = 256
LAT = QR + KVR + ROPE
SCALE = float(NOPE + ROPE) ** -0.5
EPS = 1e-6
PH = 8
NK = 128
TOPK = 16
QUAD = 32
TILES = NK * NK // P
HF = 1024
RING = 3
RAW = 4
ROUND = 6
ROUNDS = TILES // ROUND
KEY_ROUNDS = 8
PAIR_ROUNDS = 4
REST = KEY_ROUNDS + PAIR_ROUNDS
BIG = 3.0e38

C_ID, C_ONE, C_IOTA, C_MASK = 0, P, 2 * P, 3 * P
C_FREQ = C_MASK + 3 * P
C_CNT = C_FREQ + HALF
C_I16 = C_CNT + 4 * 16
C_ALL = C_I16 + 16

V_G1, V_G2 = 0, KT
V_QN = 2 * KT
V_KVN = V_QN + QR // P
V_PS = V_KVN + KVR // P
V_ALL = V_PS + POOL_W // P

TWO_PI_A = 6.28125
TWO_PI_B = 0.0019340515136718750
TWO_PI_C = 1.2556659146019e-06


def pair(i):
    return 2 * (i // 2 + 1)


def chunk_plan():
    return [
        (("ada", 0), 0), (("ada", 1), 1), (("ada", 2), 2), (("ada", 3), 0), (("win", 0), 1), (("ada", 4), 2),
        (("ada", 5), 0), (("ada", 6), 2), (("ada", 7), 0), (("win", 1), 2), (("ada", 8), 0), (("win", 2), 1),
        (("ada", 9), 0), (("win", 3), 2), (("ada", 10), 0), (("uq", 0), 1), (("ada", 11), 0), (("ukv", 0), 2),
        (("ada", 12), 0), (("ada", 13), 0), (("ada", 14), 2), (("wout", 0), 1), (("ada", 15), 0),
        (("ada", 16), 2), (("ada", 17), 0), (("wout", 1), 2), (("ada", 18), 0), (("wout", 2), 1),
        (("ada", 19), 0), (("wout", 3), 2), (("ada", 20), 0), (("wq", 0), 1), (("wq", 1), 2), (("ada", 21), 0),
        (("wq", 2), 1), (("ada", 22), 0), (("wq", 3), 2), (("ada", 23), 0), (("keys", 0), 0)]


def ada_chunk(n):
    return n + 4 if n < 4 else n - 4 if n < 8 else n


def hybrid_block(nc, x, c, positions, ada_w, ada_b, pre_mix_g, post_mix_g, pre_ffn_g, post_ffn_g,
                 w_in, pool_w, pool_scale, q_norm_g, w_uq, kv_norm_g, w_ukv, w_out,
                 peer_wq, peer_sub_keys, peer_u, peer_v, consts, out):
    plan = chunk_plan()
    where = {}
    per_slot = [0, 0, 0]
    for n, (key, slot) in enumerate(plan):
        per_slot[slot] += 64 if key[0] == "wq" else 32 if key[0] in ("uq",) else 16
        where[key] = (slot, per_slot[slot], n)

    base = (nc.sbuf_base + 31) // 32 * 32

    def at(name, off, shape, dt=F32):
        return nc.alloc_sbuf_tensor_at(name, [P] + shape, dt, offset=base + 4 * off)

    ring = [at(f"ring{s}", 8192 * s, [8192]) for s in range(3)]
    ring_low = [at(f"ring_low{s}", 8192 * s, [8192], F32R) for s in range(3)]
    xs = at("xs", 24576, [TT, D])
    hT = at("hT", 28672, [KT, T])
    qnT = at("qnT", 28672, [HEADS, T])
    knT = at("knT", 30720, [HEADS, T])
    y1 = at("y1", 28672, [TT, D])
    h2T = at("h2T", 28672, [KT, T])
    qT = at("qT", 24576, [KT, T])
    keyT = at("keyT", 8192, [KT, NK])
    sc = at("sc", 28672, [TT * KT, NK])
    tmpk = at("tmpk", 28672, [2048])
    tmpk2 = at("tmpk2", 30720, [2048])
    R = 24576
    s16 = at("s16", R, [TT * KT, TOPK])
    cand = at("cand", R + 512, [2, TOPK * TOPK])
    rest = at("rest", R + 2048, [2, TOPK * TOPK])
    posa = at("posa", R + 512, [TT, PH * TOPK], U32)
    i16f = at("i16f", R + 1024, [TT * KT, TOPK])
    best = at("best", R + 1536, [TT * PH, TOPK])
    posu = at("posu", R + 1792, [TT * PH, TOPK], U32)
    posf = at("posf", R + 2048, [2, TT, PH * TOPK])
    slots = at("slots", R + 2560, [3, TT, PH * TOPK])
    gtmp = at("gtmp", R + 3328, [TT * PH, TOPK])
    gsum = at("gsum", R + 3584, [TT * PH])
    picked = at("picked", R + 3600, [2, TOPK])
    picked_at = at("picked_at", R + 3632, [2, TOPK], U32)
    acts = at("acts", 0, [TILES, T])
    S = 32768
    cst = at("cst", S, [3 * P])
    vcols = at("vcols", S + 384, [V_ALL])
    mod1 = at("mod1", S + 432, [2, KT])
    mod2 = at("mod2", S + 464, [2, KT])
    stat = at("stat", S + 496, [64])
    c_col = at("c_col", S + 560, [KT])
    c_act = at("c_act", S + 576, [KT])
    i16 = at("i16", S + 592, [16])
    cnt = at("cnt", S + 608, [4, 16])
    pos_i = at("pos_i", S + 672, [TT], I32)
    pos_f = at("pos_f", S + 680, [TT])
    u_shift = at("u_shift", S + 680, [4])
    rowbuf = at("rowbuf", S + 688, [W])
    slotT = at("slotT", S + 1200, [3, T])
    aH = [at(f"aH{i}", S + 688 + 256 * i, [T], F32R) for i in range(2)]
    aL = [at(f"aL{i}", S + 1200 + 256 * i, [T], F32R) for i in range(2)]
    M = S + 1968
    uT = at("uT", M, [POOL_W // P, T])
    vv = at("vv", M, [TT, POOL_W])
    gate1 = at("gate1", M, [D])
    zT = at("zT", M + 2048, [POOL_W // P, T])
    s_sb = at("s_sb", M + 2048, [2, 384])
    pT = at("pT", M + 2816, [2, 384])
    post1 = at("post1", M + 2048, [D])
    catT = at("catT", M + 4096, [KT, T])
    acc = at("acc", M + 8192, [2, W])
    acc_b = at("acc_b", M + 17312, [2, W])
    init = at("init", M + 9216, [2, W])
    lat = at("lat", M + 10240, [TT, LAT])
    cT = at("cT", M + 11904, [6, T])
    qpeT = at("qpeT", M + 13440, [4, T])
    kpeT = at("kpeT", M + 14464, [T])
    qrope = at("qrope", M + 14720, [TT, 8 * ROPE])
    krope = at("krope", M + 15744, [TT, 2 * ROPE])
    trig = at("trig", M + 16000, [2, TT, HALF])
    tmpr = at("tmpr", M + 16128, [2, 256])
    x1q = at("x1q", M + 10240, [TT, D])
    mask = at("mask", M + 16640, [3 * P])
    freq = at("freq", M + 17024, [HALF])
    vrow = at("vrow", M, [P])
    ang = at("ang", M + 4096, [4, TT * HALF])
    diag = at("diag", M + 17056, [TT, P])
    junk = at("junk", M + 4096, [D])
    catL = at("catL", M + 4096, [KT, T], F32R)
    catH_a = at("catH_a", M + 10240, [12, T], F32R)
    catH_b = at("catH_b", M + 14720, [4, T], F32R)
    hH = at("hH", M + 11904, [KT, T], F32R)
    hL = at("hL", 28672, [KT, T], F32R)
    junk_lat = at("junk_lat", M + 7680, [W])
    win_high = [at(f"win_high{i}", M + 5120 + W * i, [W], F32R) for i in range(5)]
    wout_high = [at(f"wout_high{i}", M + o, [W], F32R) for i, o in enumerate((13440, 13952, 15744, 16256))]
    wq_high = [at(f"wq_high{i}", M + 14336 + W * i, [W], F32R) for i in range(5)]
    h2H = at("h2H", M, [KT, T], F32R)
    h2L = at("h2L", M + 4096, [KT, T], F32R)
    x1 = at("x1", M, [TT, D])
    result = at("result", 0, [TT, D])
    scaled = at("scaled", 4096, [TT, D])
    gate2 = at("gate2", M + 4096, [D])
    post2 = at("post2", M + 6144, [D])
    raw = at("raw", M + 8192, [RAW, HF])
    eL = at("eL", M + 12288, [RING, HF], F32R)
    eH = at("eH", M + 15360, [RING, HF], F32R)
    hotA = at("hotA", M + 15360, [2, 2, P])
    hotP = at("hotP", M + 17408, [4, 2, P])
    hotB = at("hotB", M + 16384, [2, 4, P])
    aH.append(at("aH2", M + 11264, [T], F32R))
    aL.append(at("aL2", M + 11520, [T], F32R))

    x1_dram = nc.dram_tensor("x1_dram", [TT, P, D], F32).ap()
    gate_dram = nc.dram_tensor("gate_dram", [2, D], F32).ap()

    from contextlib import ExitStack
    with ExitStack() as ctx:
        ps = ctx.enter_context(nc.psum_tensor("ps", [P, 8, W], F32))

        def sem(name):
            return ctx.enter_context(nc.semaphore(name))

        consts_in, vrow_in, x_in, c_in = sem("consts_in"), sem("vrow_in"), sem("x_in"), sem("c_in")
        ring_in = [sem(f"ring_in{s}") for s in range(3)]
        init_in = [sem("init_in0"), sem("init_in1")]
        init_zero = sem("init_zero")
        acc_ready, acc_used = sem("acc_ready"), sem("acc_used")
        row_ready, row_stored = sem("row_ready"), sem("row_stored")
        silu_done = sem("silu_done")
        vec_t, vec_cols = sem("vec_t"), sem("vec_cols")
        mod1_ready, mod2_ready = sem("mod1_ready"), sem("mod2_ready")
        x_sq, x_rs, diag1 = sem("x_sq"), sem("x_rs"), sem("diag1")
        xT_done, hT_done = sem("xT_done"), sem("hT_done")
        hA_used, hB_done, shift_row_mm, shift_row_out = sem("hA_used"), sem("hB_done"), sem("shift_row_mm"), sem("shift_row_out")
        h_hi, h_lo = sem("h_hi"), sem("h_lo")
        u_mm, u_out = sem("u_mm"), sem("u_out")
        lat_mm, lat_out, lat_sq = sem("lat_mm"), sem("lat_out"), sem("lat_sq")
        trig_ready, trig_arg = sem("trig_ready"), sem("trig_arg")
        z_ready, k_roped, lat_diag = sem("z_ready"), sem("k_roped"), sem("lat_diag")
        cT_mm, cT_out = sem("cT_mm"), sem("cT_out")
        qn_mm, qn_out = sem("qn_mm"), sem("qn_out")
        qpe_mm, q_roped, qpeT_mm, qpeT_out = sem("qpe_mm"), sem("q_roped"), sem("qpeT_mm"), sem("qpeT_out")
        kn_mm, kn_out, v_mm, v_out = sem("kn_mm"), sem("kn_out"), sem("v_mm"), sem("v_out")
        pool_mm, pool_out = sem("pool_mm"), sem("pool_out")
        s_mm, s_max, s_exp, s_norm = sem("s_mm"), sem("s_max"), sem("s_exp"), sem("s_norm")
        pT_mm, pT_out, o_mm, o_out = sem("pT_mm"), sem("pT_out"), sem("o_mm"), sem("o_out")
        y_mm, y_out = sem("y_mm"), sem("y_out")
        y_rs, g1_in, x1_done, x1_sq, x1_rs, diag2 = (
            sem("y_rs"), sem("g1_in"), sem("x1_done"), sem("x1_sq"), sem("x1_rs"), sem("diag2"))
        y_rc, x1_stored = sem("y_rc"), sem("x1_stored")
        x1T_mm, h2_out, h2H_out, h2L_out = sem("x1T_mm"), sem("h2_out"), sem("h2H_out"), sem("h2L_out")
        qT_mm, qT_out, key_mm, key_out = sem("qT_mm"), sem("qT_out"), sem("key_mm"), sem("key_out")
        sc_mm, sc_out = sem("sc_mm"), sem("sc_out")
        g_shift, g_exp, slots_ready, slot_mm, slotT_out = (
            sem("g_shift"), sem("g_exp"), sem("slots_ready"), sem("slot_mm"), sem("slotT_out"))
        w_hi, w_lo, w_used, cat_hi, cat_lo = sem("w_hi"), sem("w_lo"), sem("w_used"), sem("cat_hi"), sem("cat_lo")
        raw_in = [sem(f"raw_in{s}") for s in range(RAW)]
        u_tr, u_hi, u_lo, u_lo_pool, u_used = sem("u_tr"), sem("u_hi"), sem("u_lo"), sem("u_lo_pool"), sem("u_used")
        a_out = sem("a_out")
        hot_pool, hot_act, hot_abs, hot_diff = sem("hot_pool"), sem("hot_act"), sem("hot_abs"), sem("hot_diff")
        hot_ready, hot_mm, gated = sem("hot_ready"), sem("hot_mm"), sem("gated")
        v_in = [sem(f"v_in{s}") for s in range(RING)]
        v_hi, v_lo, v_used = sem("v_hi"), sem("v_lo"), sem("v_used")
        act_hi, act_lo = sem("act_hi"), sem("act_lo")
        y2_sq, y2_rc, y2_rs, tail_in = sem("y2_sq"), sem("y2_rc"), sem("y2_rs"), sem("tail_in")
        scaled_ready, out_stored = sem("scaled_ready"), sem("out_stored")
        out_ready = [sem("out_ready0"), sem("out_ready1")]
        dve_chain, act_chain, pick_chain = sem("dve_chain"), sem("act_chain"), sem("pick_chain")

        block = ctx.enter_context(nc.Block())

        ident = cst[:, 0:P]
        ones = cst[:, P:2 * P]
        iota = cst[:, 2 * P:3 * P]

        def ring_arrived(eng, key):
            slot, count, _ = where[key]
            eng.wait_ge(ring_in[slot], count)

        def last_use(key):
            kind, i = key
            return {"ada": (acc_ready, i + 1),
                    "win": ((shift_row_mm, 1), (u_mm, 8), (lat_mm, 2), (lat_mm, 4))[i % 4],
                    "uq": (pool_mm, 8), "ukv": (v_mm, 4), "wout": (y_mm, 2 * (i + 1)),
                    "wq": (qT_mm, 4 * (i + 1)), "keys": (key_mm, 4)}[kind]

        def wide(key, cols=W):
            return ring[where[key][0]][:, 0:KT * cols].rearrange("p (k n) -> p k n", k=KT)

        def wide_low(key, cols=W):
            return ring_low[where[key][0]][:, 0:KT * cols].rearrange("p (k n) -> p k n", k=KT)

        def win_cols(n):
            return min(W, POOL_W + LAT - n * W)

        SPLIT = {"win": (win_high, 1, 0), "wout": (wout_high, 0, 3), "wq": (wq_high, 0, 7)}

        def high_of(kind, n, k):
            bufs, first, _ = SPLIT[kind]
            return bufs[(KT * (n - first) + k) % len(bufs)]

        def piece(kind, n, k):
            _, first, before = SPLIT[kind]
            return KT * (before + n - first) + k + 1

        def wait_high_free(eng, kind, n, k):
            bufs, first, before = SPLIT[kind]
            last = KT * (n - first) + k - len(bufs)
            if last < 0:
                return
            m, kk = last // KT, last % KT
            if kk == KT - 1:
                eng.wait_ge(*last_use((kind, first + m)))
            else:
                eng.wait_ge(w_used, (KT - 1) * (before + m) + kk + 1)

        U_BANK = (6, 7, 2, 3)

        def cat_high(j):
            return catH_a[:, j, :] if j < 12 else catH_b[:, j - 12, :]

        def turned(half_tile):
            return half_tile.rearrange("p (eb k el) -> p k eb el", eb=4, el=QUAD)

        def by_k(half_tile):
            return half_tile.rearrange("p (k eb el) -> p k eb el", eb=4, el=QUAD)

        def wait_low(eng, r, j):
            eng.wait_ge(u_lo_pool if j % 2 else u_lo, r * ROUND + (j // 2 + 1))

        def add_x1(eng, tt):
            result_v, scaled_v = (t[:, tt, :].rearrange("p (q k l) -> p q k l", q=4, l=QUAD) for t in (result, scaled))
            eng.tensor_tensor(result_v, x1[:, tt, :].rearrange("p (k q l) -> p q k l", q=4, l=QUAD), scaled_v,
                              ALU.add).then_inc(out_ready[tt], 1)

        ada_v = ada_w[0].rearrange("(p k) n -> p k n", k=KT)
        win_v = w_in[0].rearrange("(k p) n -> p k n", p=P)
        wout_v = w_out[0].rearrange("(k p) n -> p k n", p=P)
        wq_v = peer_wq[0].rearrange("(q k l) n -> q l k n", q=4, l=QUAD)
        ub = peer_u[0].rearrange("(i eb el) (q h dd) -> i h q el eb dd", el=QUAD, eb=4, q=4, h=2)
        vb = peer_v[0].rearrange("(i p) (h dd) -> i h p dd", p=P, h=2)

        @block.sync
        def _(sp):
            sp.dma_start(c_col[:], c.rearrange("o (p k) -> (o p) k", k=KT)).then_inc(c_in, 16)
            sp.dma_start(cst[:], consts[:, 0:3 * P]).then_inc(consts_in, 16)
            sp.dma_start(mask[:], consts[:, C_MASK:C_MASK + 3 * P]).then_inc(consts_in, 16)
            sp.dma_start(freq[:], consts[:, C_FREQ:C_FREQ + HALF]).then_inc(consts_in, 16)
            sp.dma_start(cnt[:], consts[:, C_CNT:C_CNT + 64].rearrange("p (g t) -> p g t", g=4)).then_inc(consts_in, 16)
            sp.dma_start(i16[:], consts[:, C_I16:C_I16 + 16]).then_inc(consts_in, 16)

            ada_n = 0
            in_slot = {}
            for n, ((kind, i), slot) in enumerate(plan):
                if n == 3:
                    sp.dma_start(xs[:], x[0].rearrange("(t p) d -> p t d", p=P)).then_inc(x_in, 16)
                if n >= 3:
                    sp.wait_ge(*last_use(in_slot[slot]))
                in_slot[slot] = (kind, i)
                dst = ring[slot]
                done = ring_in[slot]
                if kind == "ada":
                    cols = slice(ada_chunk(i) * W, (ada_chunk(i) + 1) * W)
                    sp.dma_start(wide((kind, i)), ada_v[:, :, cols]).then_inc(done, 16)
                    if ada_n == 0:
                        sp.wait_ge(init_zero, 1)
                    if ada_n >= 2:
                        sp.wait_ge(acc_ready, ada_n - 1)
                    sp.dma_start(init[0:1, ada_n % 2, :], ada_b[0:1, cols]).then_inc(init_in[ada_n % 2], 16)
                    ada_n += 1
                elif kind == "win":
                    cols = min(W, POOL_W + LAT - i * W)
                    sp.dma_start(wide((kind, i), cols), win_v[:, :, i * W:i * W + cols]).then_inc(done, 16)
                elif kind == "wout":
                    sp.dma_start(wide((kind, i)), wout_v[:, :, i * W:(i + 1) * W]).then_inc(done, 16)
                elif kind == "uq":
                    sp.dma_start(dst[:, 0:6144].rearrange("p (k n) -> p k n", k=4),
                                 w_uq[0].rearrange("(k p) n -> p k n", p=P)).then_inc(done, 16)
                    sp.dma_start(dst[:, 6144:8192].rearrange("p (g k n) -> p g k n", g=4, k=2),
                                 pool_w[0].rearrange("g (k p) n -> p g k n", p=P)).then_inc(done, 16)
                elif kind == "ukv":
                    sp.dma_start(dst[:, 0:4096].rearrange("p (k n) -> p k n", k=2),
                                 w_ukv[0].rearrange("(k p) n -> p k n", p=P)).then_inc(done, 16)
                elif kind == "wq":
                    for q in range(4):
                        sp.dma_start(wide((kind, i))[q * QUAD:(q + 1) * QUAD],
                                     wq_v[q, :, :, i * W:(i + 1) * W]).then_inc(done, 16)
                elif kind == "keys":
                    sp.dma_start(dst[:, 0:2048].rearrange("p (k n) -> p k n", k=KT),
                                 peer_sub_keys[0].rearrange("h s n d -> n (h s) d")).then_inc(done, 16)

            sp.wait_ge(acc_used, 24)
            sp.wait_ge(q_roped, 1)
            sp.wait_ge(qpeT_out, 1)
            sp.wait_ge(x1T_mm, KT)
            sp.wait_ge(x1_stored, 16)

            def load_u(tile, h, before, slot):
                if before:
                    wait_low(sp, *before)
                for q in range(4):
                    sp.dma_start(raw[q * QUAD:(q + 1) * QUAD, slot, :].rearrange("p (e d) -> p e d", e=4),
                                 ub[tile, h, q]).then_inc(raw_in[slot], 16)

            def load_u_round(r, tiles=ROUND, first=False):
                for j in range(2 * tiles):
                    before = (r, j - RAW) if j >= RAW else None if first else (r - 1, 2 * ROUND + j - RAW)
                    load_u(r * ROUND + j // 2, j % 2, before, j % RAW)

            load_u_round(0, first=True)
            with sp.Fori(1, ROUNDS) as r:
                load_u_round(r)
            load_u_round(ROUNDS, TILES % ROUND)

            def load_v(tile, h, g, slot):
                sp.wait_ge(v_lo, g - (RING - 1))
                sp.dma_start(raw[:, slot, :], vb[tile, h]).then_inc(v_in[slot], 16)

            def load_v3(t0):
                for j in range(6):
                    load_v(t0 + j // 2, j % 2, t0 * 2 + j, j % RING)

            wait_low(sp, ROUNDS, 2 * (TILES % ROUND) - 2)
            wait_low(sp, ROUNDS, 2 * (TILES % ROUND) - 1)
            for j in range(RING):
                sp.dma_start(raw[:, j, :], vb[j // 2, j % 2]).then_inc(v_in[j], 16)
            for j in range(RING, 6):
                load_v(j // 2, j % 2, j, j % RING)
            with sp.Fori(1, TILES // 3) as r:
                load_v3(r * 3)
            for j in range(4):
                load_v(TILES - 2 + j // 2, j % 2, 2 * (TILES - 2) + j, j % RING)

        @block.gpsimd
        def _(pool):
            pool.memset(init[:], 0.0).then_inc(init_zero, 1)
            pool.memset(vrow[:], 0.0).then_inc(init_zero, 1)
            pool.wait_ge(init_zero, 2)
            pool.dma_start(vrow[V_G1:V_G1 + KT], pre_mix_g[0].rearrange("(k p) -> k p", p=P)).then_inc(vrow_in, 16)
            g2q = pre_ffn_g[0].rearrange("(q k l) -> k q l", q=4, l=QUAD)
            pool.dma_start(vrow[V_G2:V_G2 + KT].rearrange("k (q l) -> k q l", q=4), g2q).then_inc(vrow_in, 16)
            pool.dma_start(vrow[V_QN:V_KVN], q_norm_g[0].rearrange("(k p) -> k p", p=P)).then_inc(vrow_in, 16)
            pool.dma_start(vrow[V_KVN:V_PS], kv_norm_g[0].rearrange("(k p) -> k p", p=P)).then_inc(vrow_in, 16)
            pool.dma_start(vrow[V_PS:V_ALL], pool_scale[0].rearrange("(k p) -> k p", p=P)).then_inc(vrow_in, 16)
            pool.dma_start(pos_i[:], positions[0].rearrange("(t p) -> p t", p=P),
                           allow_slow_non_contiguous=True).then_inc(vrow_in, 16)
            def weight_lows(kind):
                for n in range(SPLIT[kind][1], 4):
                    cols = win_cols(n) if kind == "win" else W
                    for k in range(KT):
                        pool.wait_ge(w_hi, piece(kind, n, k))
                        pool.tensor_tensor(wide_low((kind, n), cols)[:, k, :], wide((kind, n), cols)[:, k, :],
                                           high_of(kind, n, k)[:, 0:cols].bitcast(F32), ALU.subtract).then_inc(w_lo, 1)

            weight_lows("win")
            def cat_lows(n, j0, j1, high):
                pool.wait_ge(cat_hi, n)
                pool.tensor_tensor(catL[:, j0:j1, :], catT[:, j0:j1, :], high.bitcast(F32),
                                   ALU.subtract).then_inc(cat_lo, 1)

            cat_lows(1, 8, 9, catH_a[:, 8:9, :])
            cat_lows(2, 0, 8, catH_a[:, 0:8, :])
            for h in range(1, HEADS):
                high = catH_a[:, 8 + h:9 + h, :] if h < 4 else catH_b[:, h - 4:h - 3, :]
                cat_lows(h + 2, 8 + h, 9 + h, high)
            pool.wait_ge(row_stored, 64)
            pool.wait_ge(o_out, HEADS)
            pool.dma_start(gate1[:], gate_dram[0:1, :].broadcast_to([P, D])).then_inc(g1_in, 16)
            pool.dma_start(post1[:], post_mix_g[0:1, :].broadcast_to([P, D])).then_inc(g1_in, 16)

            weight_lows("wout")
            pool.wait_ge(x1_done, 2)
            pool.dma_start(x1_dram.rearrange("t p d -> p t d"), x1q[:]).then_inc(x1_stored, 16)
            weight_lows("wq")
            def low_round(r, tiles=ROUND, first=False):
                for j in range(1, 2 * tiles, 2):
                    pool.wait_ge(u_hi, r * (2 * ROUND) + (j + 1))
                    if not (first and j < RING):
                        pool.wait_ge(u_used, r * (2 * ROUND) + (j + 1 - RING))
                    pool.tensor_tensor(by_k(eL[:, j % RING, :]), turned(raw[:, j % RAW, :]),
                                       by_k(eH[:, j % RING, :].bitcast(F32)), ALU.subtract).then_inc(u_lo_pool, 1)

            low_round(0, first=True)
            with pool.Fori(1, ROUNDS) as r:
                low_round(r)
            low_round(ROUNDS, TILES % ROUND)

            def differences(g, q, first):
                if not first:
                    pool.wait_ge(hot_mm, g - 3)
                if q or not first:
                    pool.wait_ge(hot_diff, g)
                pool.tensor_tensor(hotP[:, q], iota.unsqueeze(1).broadcast_to([P, 2, P]),
                                   slotT[:, 1, bass.ds(g * 4 + 2, 2)].unsqueeze(2).broadcast_to([P, 2, P]),
                                   ALU.subtract).then_inc(hot_diff, 1)

            def where_zero(q):
                pool.tensor_scalar(hotP[:, q], hotP[:, q], 0.0, None, ALU.is_equal).then_inc(hot_pool, 1)

            pool.wait_ge(slotT_out, 2)
            pool.wait_ge(u_used, 2 * TILES)
            for q in range(4):
                differences(q, q, True)
                if q:
                    where_zero(q - 1)
            with pool.Fori(1, T // 16) as r:
                for q in range(4):
                    differences(r * 4 + q, q, False)
                    where_zero((q + 3) % 4)
            pool.wait_ge(hot_diff, T // 4)
            where_zero(3)

            pool.wait_ge(row_stored, 128)
            pool.wait_ge(x1_stored, 16)
            pool.wait_ge(u_used, 2 * TILES)
            pool.dma_start(x1[:], x1_dram.rearrange("t p d -> p t d")).then_inc(tail_in, 16)
            pool.dma_start(gate2[:], gate_dram[1:2, :].broadcast_to([P, D])).then_inc(tail_in, 16)
            pool.dma_start(post2[:], post_ffn_g[0:1, :].broadcast_to([P, D])).then_inc(tail_in, 16)
            pool.wait_ge(tail_in, 48)
            pool.wait_ge(scaled_ready, 1)
            add_x1(pool, 0)
            for tt in range(TT):
                pool.wait_ge(out_ready[tt], 1)
                pool.dma_start(out[0, tt * P:(tt + 1) * P, :], result[:, tt, :]).then_inc(out_stored, 16)
            pool.wait_ge(out_stored, 32)

        @block.tensor
        def _(pe):
            def transpose_vectors():
                pe.wait_ge(consts_in, 80)
                pe.wait_ge(vrow_in, 96)
                pe.transpose(ps[:, 1, 0:P], vrow[:, :], ident).then_inc(vec_t, 1)

            def ada_columns(n, quads):
                pe.wait_ge(acc_ready, n + 1)
                parts = (acc[:, n % 2, :], acc_b[:, n % 2, :])
                if not quads:
                    for j in range(4):
                        for i, b in enumerate(parts):
                            mm = pe.matmul(ps[:, 0, n * 4 + j:n * 4 + j + 1], b[:, j * P:(j + 1) * P],
                                           ones[:, 0:1], start=(i == 0), stop=(i == 1), skip_group_check=True)
                else:
                    m, q = (n - 12) // 4, (n - 12) % 4
                    for k in range(KT):
                        col = 64 + m * KT + k
                        for i, b in enumerate(parts):
                            mm = pe.matmul(ps[q * QUAD:(q + 1) * QUAD, 0, col:col + 1],
                                           b[:, k * QUAD:(k + 1) * QUAD], ones[:, 0:1], start=(i == 0),
                                           stop=(i == 1), skip_group_check=True)
                mm.then_inc(acc_used, 1)

            def ada_row(n, rows_before):
                pe.wait_ge(acc_ready, n + 1)
                if rows_before:
                    pe.wait_ge(row_ready, rows_before)
                pe.matmul(ps[0:1, 1, :], ones[:, 0:1], acc[:, n % 2, :], start=True, stop=False)
                pe.matmul(ps[0:1, 1, :], ones[:, 0:1], acc_b[:, n % 2, :], start=False, stop=True).then_inc(acc_used, 1)

            def turn(src, k, done, rhs):
                b, half = 2 + (k // 2) % 2, k % 2
                for tt in range(TT):
                    mm = pe.matmul(ps[:, b, half * T + tt * P:half * T + (tt + 1) * P], src(tt), rhs(tt),
                                   start=True, stop=True, skip_group_check=True)
                mm.then_inc(done, 1)

            def mm_group(bank_ap, lhs, rhs, k_tiles):
                for k in range(k_tiles):
                    mm = pe.matmul(bank_ap, lhs(k), rhs(k), start=(k == 0), stop=(k == k_tiles - 1),
                                   skip_group_check=True)
                return mm

            def split3(o, lh, ll, rh, rl, start, stop):
                pe.matmul(o, lh, rh, start=start, stop=False, skip_group_check=True)
                pe.matmul(o, lh, rl, start=False, stop=False, skip_group_check=True)
                return pe.matmul(o, ll, rh, start=False, stop=stop, skip_group_check=True)

            for n in range(4):
                if n == 2:
                    transpose_vectors()
                ada_columns(n, False)
            pe.wait_ge(vec_cols, 1)

            pe.wait_ge(x_in, 16)
            pe.wait_ge(diag1, 2)
            for k in range(KT):
                if k >= 4 and k % 2 == 0:
                    pe.wait_ge(hT_done, k - 2)
                turn(lambda tt: xs[:, tt, k * P:(k + 1) * P], k, xT_done, lambda tt: diag[:, tt, :])

            pe.wait_ge(hT_done, KT)
            pe.wait_ge(mod1_ready, 1)
            ring_arrived(pe, ("win", 0))
            w0 = wide(("win", 0))
            for j in range(4):
                mm = mm_group(ps[:, 4 + j // 2, (j % 2) * T:(j % 2 + 1) * T],
                              lambda k: w0[:, k, j * P:(j + 1) * P], lambda k: hT[:, k, :], KT)
                if j == 3:
                    mm.then_inc(hA_used, 1)
                ada_columns(4 + j, False)
            pe.wait_ge(mod1_ready, 2)
            mm_group(ps[0:1, 1, :], lambda k: mod1[:, 1, k:k + 1], lambda k: w0[:, k, :], KT).then_inc(shift_row_mm, 1)
            pe.wait_ge(shift_row_out, 1)
            for j in range(4):
                pe.matmul(ps[:, 0, 480 + j:481 + j], rowbuf[0:1, j * P:(j + 1) * P], ones[0:1, 0:1],
                          start=True, stop=True, skip_group_check=True).then_inc(u_mm, 1)
            for k in range(KT):
                pe.wait_ge(h_lo, k // 4 + 1)
                pe.wait_ge(w_lo, piece("win", 1, k))
                for j in range(4):
                    cols = slice(j * P, (j + 1) * P)
                    mm = split3(ps[:, U_BANK[j], 0:T], high_of("win", 1, k)[:, cols],
                                wide_low(("win", 1))[:, k, cols], hH[:, k, :], hL[:, k, :], k == 0, k == KT - 1)
                    if k == KT - 1:
                        mm.then_inc(u_mm, 1)
                if k < KT - 1:
                    mm.then_inc(w_used, 1)
            ada_row(8, 0)
            for n in range(2, 4):
                cols = win_cols(n)
                pe.wait_ge(u_out, 4 * (n - 1))
                for k in range(KT):
                    pe.wait_ge(w_lo, piece("win", n, k))
                    for tt in range(TT):
                        rows = slice(tt * P, (tt + 1) * P)
                        mm = split3(ps[:, 4 + 2 * (n - 2) + tt, 0:cols], hH[:, k, rows], hL[:, k, rows],
                                    high_of("win", n, k)[:, 0:cols], wide_low(("win", n), cols)[:, k, :],
                                    k == 0, k == KT - 1)
                        if k == KT - 1:
                            mm.then_inc(lat_mm, 1)
                    if k < KT - 1:
                        mm.then_inc(w_used, 1)
                ada_row(7 + n, n - 1)

            ring_arrived(pe, ("uq", 0))
            uq_slot = ring[where[("uq", 0)][0]]
            wuq = uq_slot[:, 0:6144].rearrange("p (k h n) -> p k h n", k=4, h=HEADS)
            wpl = uq_slot[:, 6144:8192].rearrange("p (g k n) -> p g k n", g=4, k=2)
            pe.wait_ge(lat_diag, 4)
            for r in range(6):
                if r == 4:
                    pe.wait_ge(cT_out, 2)
                turn(lambda tt: lat[:, tt, r * P:(r + 1) * P], r, cT_mm,
                     lambda tt: diag[:, tt, :] if r < 4 else tmpr[:, tt, 0:P])
            pe.wait_ge(cT_out, 6)
            pe.wait_ge(lat_out, 4)
            for h in range(HEADS):
                b = 4 + h // 2
                mm_group(ps[:, b, (h % 2) * T:(h % 2 + 1) * T], lambda k: wuq[:, k, h, 0:NOPE],
                         lambda k: cT[:, k, :], 4).then_inc(qn_mm, 1)
            for tt in range(TT):
                mm_group(ps[:, 2 + tt, :], lambda k: cT[:, k, tt * P:(tt + 1) * P],
                         lambda k: wuq[:, k, :, NOPE:NOPE + ROPE], 4).then_inc(qpe_mm, 1)
            ada_row(11, 3)
            pe.wait_ge(z_ready, 4)
            for j in range(8):
                g = j // 2
                b = 4 + j // 2
                if j % 2 == 0:
                    pe.wait_ge(qn_out, j + 2)
                mm = mm_group(ps[:, b, (j % 2) * T:(j % 2 + 1) * T],
                              lambda k: wpl[:, g, k, (j % 2) * P:(j % 2 + 1) * P],
                              lambda k: zT[:, 2 * g + k, :], 2)
                mm.then_inc(pool_mm, 1)
            ring_arrived(pe, ("ukv", 0))
            wkv = ring[where[("ukv", 0)][0]][:, 0:4096].rearrange("p (k h n) -> p k h n", k=2, h=HEADS)
            for h in range(HEADS):
                b = 4 + h // 2
                if h % 2 == 0:
                    pe.wait_ge(pool_out, h + 2)
                mm_group(ps[:, b, (h % 2) * T:(h % 2 + 1) * T], lambda k: wkv[:, k, h, 0:NOPE],
                         lambda k: cT[:, 4 + k, :], 2).then_inc(kn_mm, 1)
            for tt in range(TT):
                for hh in range(2):
                    b = 4 + tt * 2 + hh
                    pe.wait_ge(kn_out, 2 * (tt * 2 + hh) + 2)
                    mm_group(ps[:, b, :], lambda k: cT[:, 4 + k, tt * P:(tt + 1) * P],
                             lambda k: wkv[:, k, 4 * hh:4 * hh + 4, NOPE:2 * NOPE], 2).then_inc(v_mm, 1)
            ada_columns(12, True)
            pe.wait_ge(k_roped, 1)
            pe.wait_ge(q_roped, 1)
            for tt in range(TT):
                for p in range(4):
                    pe.transpose(ps[:, 2 + p // 2, (p % 2) * T + tt * P:(p % 2) * T + (tt + 1) * P],
                                 qrope[:, tt, p * P:(p + 1) * P], ident)
                mm = pe.transpose(ps[:, 0, T + tt * P:T + (tt + 1) * P], krope[:, tt, :], ident)
            mm.then_inc(qpeT_mm, 1)

            pe.wait_ge(qpeT_out, 1)
            pe.wait_ge(kn_out, HEADS)
            pe.wait_ge(qn_out, HEADS)

            def scores(h):
                b = 4 + h % 2
                if h < 2:
                    pe.wait_ge(v_out, h + 1)
                else:
                    pe.wait_ge(s_max, h - 1)
                r0 = (h % 2) * ROPE
                for qb in range(TT):
                    kend = (qb + 1) * P
                    o = ps[:, b, qb * P:qb * P + kend]
                    pe.matmul(o, qnT[:, h, qb * P:(qb + 1) * P], knT[:, h, 0:kend], start=True, stop=False,
                              skip_group_check=True)
                    mm = pe.matmul(o, qpeT[r0:r0 + ROPE, h // 2, qb * P:(qb + 1) * P],
                                   kpeT[r0:r0 + ROPE, 0:kend], start=False, stop=True, skip_group_check=True)
                mm.then_inc(s_mm, 1)

            def turn_probs(h):
                b = 6 + h % 2
                if h < 2:
                    pe.wait_ge(v_out, h + 3)
                pe.wait_ge(s_norm, h + 1)
                if h >= 2:
                    pe.wait_ge(pT_out, h - 1)
                for j in range(3):
                    mm = pe.transpose(ps[:, b, j * P:(j + 1) * P], s_sb[:, h % 2, j * P:(j + 1) * P], ident)
                mm.then_inc(pT_mm, 1)

            def mix(h):
                b = 2 + h % 2
                pe.wait_ge(pT_out, h + 1)
                if h >= 2:
                    pe.wait_ge(o_out, h - 1)
                v0, v1 = (vv[:, t, h * P:(h + 1) * P] for t in range(2))
                pe.matmul(ps[:, b, 0:P], v0, pT[:, h % 2, 0:P], start=True, stop=True, skip_group_check=True)
                pe.matmul(ps[:, b, P:T], v0, pT[:, h % 2, P:T], start=True, stop=False, skip_group_check=True)
                pe.matmul(ps[:, b, P:T], v1, pT[:, h % 2, T:T + P], start=False, stop=True,
                          skip_group_check=True).then_inc(o_mm, 1)

            pe.wait_ge(v_out, 4)
            scores(0)
            scores(1)
            for h in range(HEADS):
                turn_probs(h)
                if h + 2 < HEADS:
                    scores(h + 2)
                mix(h)
                if h >= 3 and h % 2:
                    ada_columns(13 + (h - 3) // 2, True)
            ada_columns(16, True)

            pe.wait_ge(cat_hi, HEADS + 1)
            pe.wait_ge(cat_lo, HEADS + 1)
            for n in range(4):
                for k in range(KT):
                    pe.wait_ge(w_lo, piece("wout", n, k))
                    for tt in range(TT):
                        if n >= 2 and k == 0:
                            pe.wait_ge(y_out, (n - 2) * 2 + tt + 1)
                        mm = split3(ps[:, 4 + (n % 2) * 2 + tt, :], cat_high(k)[:, tt * P:(tt + 1) * P],
                                    catL[:, k, tt * P:(tt + 1) * P], high_of("wout", n, k)[:],
                                    wide_low(("wout", n))[:, k, :], k == 0, k == KT - 1)
                        if k == KT - 1:
                            mm.then_inc(y_mm, 1)
                    if k < KT - 1:
                        mm.then_inc(w_used, 1)
                if n < 3:
                    ada_columns(17 + n, True)

            pe.wait_ge(diag2, 2)
            for k in range(KT):
                if k >= 4 and k % 2 == 0:
                    pe.wait_ge(h2_out, k - 2)
                turn(lambda tt: x1q[:, tt, k * P:(k + 1) * P], k, x1T_mm, lambda tt: diag[:, tt, :])

            q_bank = [4, 5, 6, 7, 2, 3]
            for n in range(4):
                if n == 1:
                    pe.wait_ge(h2_out, KT)
                for k in range(KT):
                    if n == 0:
                        pe.wait_ge(h2H_out, k + 1)
                        pe.wait_ge(h2L_out, k + 1)
                    pe.wait_ge(w_lo, piece("wq", n, k))
                    for j in range(4):
                        i = 4 * n + j
                        if i >= 6 and k == 0:
                            pe.wait_ge(qT_out, i - 5)
                        cols = slice(j * P, (j + 1) * P)
                        mm = split3(ps[:, q_bank[i % 6], 0:T], high_of("wq", n, k)[:, cols],
                                    wide_low(("wq", n))[:, k, cols], h2H[:, k, :], h2L[:, k, :],
                                    k == 0, k == KT - 1)
                        if k == KT - 1:
                            mm.then_inc(qT_mm, 1)
                    if k < KT - 1:
                        mm.then_inc(w_used, 1)
                ada_row(20 + n, 4 + n)
            ring_arrived(pe, ("keys", 0))
            keys = ring[where[("keys", 0)][0]][:, 0:2048].rearrange("p (k n) -> p k n", k=KT)
            pe.wait_ge(qT_out, 12)
            for i in range(KT):
                b = 2 + (i // 4) % 2
                if i >= 8:
                    pe.wait_ge(key_out, i // 4 - 1)
                mm = pe.transpose(ps[:, b, (i % 4) * P:(i % 4 + 1) * P], keys[:, i, :], ident)
                if i % 4 == 3:
                    mm.then_inc(key_mm, 1)
            pe.wait_ge(qT_out, KT)
            pe.wait_ge(key_out, 4)
            for j in range(8):
                b = 4 + j % 4
                if j >= 4:
                    pe.wait_ge(sc_out, j - 3)
                for i in range(4):
                    tt, hp = j // 4, (j % 4) * 4 + i
                    mm = pe.matmul(ps[:, b, i * P:(i + 1) * P], qT[:, hp, tt * P:(tt + 1) * P], keyT[:, hp, :],
                                   start=True, stop=True, skip_group_check=True)
                mm.then_inc(sc_mm, 1)
            def u_tile(r, i, first):
                tile, bank = r * ROUND + i, i % 3
                if not first:
                    pe.wait_ge(a_out, tile - 2)
                for h in range(2):
                    slot = (2 * i + h) % RING
                    wait_low(pe, r, 2 * i + h)
                    for k in range(KT // 2):
                        kk = h * (KT // 2) + k
                        mm = split3(ps[:, bank, 0:T], eH[:, slot, k * P:(k + 1) * P], eL[:, slot, k * P:(k + 1) * P],
                                    h2H[:, kk, :], h2L[:, kk, :], kk == 0, kk == KT - 1)
                    mm.then_inc(u_used, 1)

            pe.wait_ge(h2L_out, KT)
            pe.wait_ge(h2H_out, KT)
            for i in range(ROUND):
                u_tile(0, i, i < 3)
            with pe.Fori(1, REST + 4) as r:
                for i in range(ROUND):
                    u_tile(r, i, False)
            pe.wait_ge(slots_ready, 1)
            for m in range(3):
                for tt in range(TT):
                    mm = pe.transpose(ps[:, 4 + m // 2, (m % 2) * T + tt * P:(m % 2) * T + (tt + 1) * P],
                                      slots[:, m, tt, :], ident)
            mm.then_inc(slot_mm, 1)
            with pe.Fori(REST + 4, ROUNDS) as r:
                for i in range(ROUND):
                    u_tile(r, i, False)
            for i in range(TILES % ROUND):
                u_tile(ROUNDS, i, False)

            def scatter(g, q, first):
                half = q % 2
                if not first:
                    pe.wait_ge(gated, g - 1)
                pe.wait_ge(hot_ready, g + 1)
                pe.wait_ge(hot_pool, g + 1)
                pe.wait_ge(hot_act, g + 1)
                for t in range(4):
                    hot = hotA[:, half, t, :] if t < 2 else hotP[:, q, t - 2, :]
                    mm = pe.matmul(ps[:, half, t * P:(t + 1) * P], hot, hotB[:, half, t, :],
                                   start=True, stop=True, skip_group_check=True)
                mm.then_inc(hot_mm, 1)

            pe.wait_ge(a_out, TILES)
            for q in range(4):
                scatter(q, q, q < 2)
            with pe.Fori(1, T // 16) as r:
                for q in range(4):
                    scatter(r * 4 + q, q, False)

            def v_tile(tile, j, start, stop):
                pe.wait_ge(act_lo, tile + 1)
                for h in range(2):
                    slot = (2 * j + h) % RING
                    pe.wait_ge(v_lo, tile * 2 + (h + 1))
                    for tt in range(TT):
                        lh, ll = (a[j][:, tt * P:(tt + 1) * P] for a in (aH, aL))
                        o = [ps[:, tt * 4 + h * 2 + n, :] for n in range(2)]
                        vh, vl = ([e[:, slot, n * W:(n + 1) * W] for n in range(2)] for e in (eH, eL))
                        for n in range(2):
                            pe.matmul(o[n], lh, vh[n], start=start, stop=False, skip_group_check=True)
                            pe.matmul(o[n], lh, vl[n], start=False, stop=False, skip_group_check=True)
                        for n in range(2):
                            mm = pe.matmul(o[n], ll, vh[n], start=False, stop=stop, skip_group_check=True)
                    mm.then_inc(v_used, 1)

            pe.wait_ge(gated, T // 4)
            for j in range(3):
                v_tile(j, j, j == 0, False)
            with pe.Fori(1, TILES // 3) as r:
                for j in range(3):
                    v_tile(r * 3 + j, j, False, False)
            v_tile(TILES - 2, 0, False, False)
            v_tile(TILES - 1, 1, False, True)

        @block.scalar
        def _(act):
            count = [0]

            def seq(ins):
                count[0] += 1
                ins.then_inc(act_chain, 1)
                act.wait_ge(act_chain, count[0])

            act.wait_ge(c_in, 16)
            act.activation(c_act[:], c_col[:], ACT.Silu).then_inc(silu_done, 1)
            act.wait_ge(x_in, 16)
            for tt in range(TT):
                seq(act.activation(hT[:].rearrange("p k t -> p (k t)")[:, 0:D], xs[:, tt, :], ACT.Square,
                                   accum_out=stat[:, tt:tt + 1]))
            act.nop().then_inc(x_sq, 1)
            act.wait_ge(trig_arg, 1)
            act.activation(trig[:, 0].rearrange("p t f -> p (t f)"), ang[:, 2, :], ACT.Sin).then_inc(trig_ready, 1)
            act.activation(trig[:, 1].rearrange("p t f -> p (t f)"), ang[:, 1, :], ACT.Sin).then_inc(trig_ready, 1)
            act.wait_ge(x_rs, 1)
            act.activation(stat[:, 4:6], stat[:, 2:4], ACT.Sqrt).then_inc(x_rs, 1)
            act.wait_ge(mod1_ready, 1)
            act.wait_ge(act_chain, count[0])
            for k in range(KT):
                act.wait_ge(xT_done, pair(k))
                b, half = 2 + (k // 2) % 2, k % 2
                act.activation(hT[:, k, :], ps[:, b, half * T:(half + 1) * T], ACT.Identity,
                               scale=mod1[:, 0, k:k + 1]).then_inc(hT_done, 1)

            def gate_row(n, stored):
                act.wait_ge(acc_used, n + 1)
                if stored:
                    act.wait_ge(row_stored, stored)
                act.copy(rowbuf[0:1, :], ps[0:1, 1, :]).then_inc(row_ready, 1)
                i = stored // 16
                act.wait_ge(row_ready, i + 1)
                act.dma_start(gate_dram[i // 4:i // 4 + 1, (i % 4) * W:(i % 4 + 1) * W],
                              rowbuf[0:1, :]).then_inc(row_stored, 16)

            def weight_high(kind, n, k):
                if k == 0:
                    ring_arrived(act, (kind, n))
                wait_high_free(act, kind, n, k)
                cols = win_cols(n) if kind == "win" else W
                act.copy(high_of(kind, n, k)[:, 0:cols], wide((kind, n), cols)[:, k, :]).then_inc(w_hi, 1)

            for q in range(4):
                act.wait_ge(hB_done, q + 1)
                act.copy(hH[:, 4 * q:4 * q + 4, :], hT[:, 4 * q:4 * q + 4, :]).then_inc(h_hi, 1)
            for k in range(5):
                weight_high("win", 1, k)
            act.wait_ge(shift_row_mm, 1)
            act.copy(rowbuf[0:1, :], ps[0:1, 1, :]).then_inc(shift_row_out, 1)
            act.wait_ge(u_mm, 4)
            seq(act.copy(u_shift[:], ps[:, 0, 480:484]))
            for j in range(4):
                act.activation(uT[:, j, :], ps[:, 4 + j // 2, (j % 2) * T:(j % 2 + 1) * T], ACT.Identity,
                               bias=u_shift[:, j:j + 1]).then_inc(u_out, 1)
            for k in range(5, KT):
                weight_high("win", 1, k)
            for k in range(KT):
                weight_high("win", 2, k)
                if k == 4:
                    for j in range(4):
                        act.wait_ge(u_mm, 5 + j)
                        act.copy(uT[:, 4 + j, :], ps[:, U_BANK[j], 0:T]).then_inc(u_out, 1)
                    gate_row(8, 0)

            def latents(n):
                cols = win_cols(2 + n)
                for tt in range(TT):
                    act.wait_ge(lat_mm, 2 * n + tt + 1)
                    act.copy(lat[:, tt, n * W:n * W + cols], ps[:, 4 + 2 * n + tt, 0:cols]).then_inc(lat_out, 1)
                    r = QR if n == 0 else KVR
                    seq(act.activation(junk_lat[:, 0:r], ps[:, 4 + 2 * n + tt, 0:r], ACT.Square,
                                       accum_out=stat[:, 8 + 2 * n + tt:9 + 2 * n + tt]))

            for k in range(KT):
                weight_high("win", 3, k)
                if k == 4:
                    latents(0)
                    gate_row(9, 16)
            latents(1)
            act.nop().then_inc(lat_sq, 1)
            act.wait_ge(lat_sq, 2)
            act.activation(stat[:, 16:20], stat[:, 12:16], ACT.Sqrt).then_inc(lat_sq, 1)
            for r in range(6):
                act.wait_ge(cT_mm, pair(r))
                act.activation(cT[:, r, :], ps[:, 2 + (r // 2) % 2, (r % 2) * T:(r % 2 + 1) * T], ACT.Identity,
                               scale=vcols[:, V_QN + r:V_QN + r + 1]).then_inc(cT_out, 1)
            gate_row(10, 32)
            for h in range(HEADS):
                act.wait_ge(qn_mm, pair(h))
                if h == 0:
                    act.wait_ge(u_mm, 8)
                act.copy(qnT[:, h, :], ps[:, 4 + h // 2, (h % 2) * T:(h % 2 + 1) * T]).then_inc(qn_out, 1)
            for j in range(8):
                act.wait_ge(pool_mm, pair(j))
                act.activation(catT[:, j, :], ps[:, 4 + j // 2, (j % 2) * T:(j % 2 + 1) * T], ACT.Identity,
                               scale=vcols[:, V_PS + j:V_PS + j + 1]).then_inc(pool_out, 1)
            gate_row(11, 48)
            for h in range(HEADS):
                act.wait_ge(kn_mm, pair(h))
                act.copy(knT[:, h, :], ps[:, 4 + h // 2, (h % 2) * T:(h % 2 + 1) * T]).then_inc(kn_out, 1)
            for j in range(4):
                act.wait_ge(v_mm, j + 1)
                act.copy(vv[:, j // 2, (j % 2) * W:(j % 2 + 1) * W], ps[:, 4 + j, :]).then_inc(v_out, 1)
            act.wait_ge(qpeT_mm, 1)
            seq(act.copy(qpeT[:].rearrange("p a t -> p (a t)"), ps[:, 2:4, :].rearrange("p a t -> p (a t)")))
            seq(act.copy(kpeT[:], ps[:, 0, T:2 * T]))
            act.nop().then_inc(qpeT_out, 1)

            def exps(h):
                act.wait_ge(s_max, h + 1)
                for qb in range(TT):
                    s = s_sb[:, h % 2, qb * P:qb * P + (qb + 1) * P]
                    e = act.activation(s, s, ACT.Exp, bias=stat[:, 20 + 2 * (h % 2) + qb:21 + 2 * (h % 2) + qb],
                                       accum_out=stat[:, 24 + 2 * (h % 2) + qb:25 + 2 * (h % 2) + qb])
                    e.then_inc(s_exp, 1)

            def outs(h):
                act.wait_ge(pT_mm, h + 1)
                if h >= 2:
                    act.wait_ge(o_mm, h - 1)
                act.copy(pT[:, h % 2, :], ps[:, 6 + h % 2, 0:3 * P]).then_inc(pT_out, 1)
                act.wait_ge(o_mm, h + 1)
                act.copy(catT[:, 8 + h, :], ps[:, 2 + h % 2, 0:T]).then_inc(o_out, 1)
                act.wait_ge(o_out, h + 1)
                act.copy(cat_high(8 + h), catT[:, 8 + h, :]).then_inc(cat_hi, 1)

            act.wait_ge(k_roped, 1)
            for h in range(HEADS + 1):
                if h < HEADS:
                    exps(h)
                if h >= 1:
                    outs(h - 1)
                if h == 1:
                    act.wait_ge(pool_out, 8)
                    act.copy(catH_a[:, 0:8, :], catT[:, 0:8, :]).then_inc(cat_hi, 1)

            def y_chunk(n):
                for tt in range(TT):
                    act.wait_ge(y_mm, 2 * n + tt + 1)
                    b = 4 + (n % 2) * 2 + tt
                    seq(act.activation(y1[:, tt, n * W:(n + 1) * W], ps[:, b, :], ACT.Square,
                                       accum_out=stat[:, 28 + tt * 4 + n:29 + tt * 4 + n]))
                    act.copy(y1[:, tt, n * W:(n + 1) * W], ps[:, b, :]).then_inc(y_out, 1)

            act.wait_ge(s_mm, HEADS)
            act.wait_ge(s_max, HEADS)
            for n in range(4):
                for k in range(KT):
                    weight_high("wout", n, k)
                    if n and k == len(wout_high) - 1:
                        y_chunk(n - 1)
            y_chunk(3)
            for k in range(len(wq_high)):
                weight_high("wq", 0, k)
            act.wait_ge(y_rc, 1)
            act.activation(stat[:, 38:40], stat[:, 36:38], ACT.Sqrt).then_inc(y_rs, 1)
            for tt in range(TT):
                act.wait_ge(x1_done, tt + 1)
                seq(act.activation(junk[:], x1q[:, tt, :], ACT.Square, accum_out=stat[:, 40 + tt:41 + tt]))
            act.nop().then_inc(x1_sq, 1)
            act.wait_ge(x1_rs, 1)
            act.activation(stat[:, 44:46], stat[:, 42:44], ACT.Sqrt).then_inc(x1_rs, 1)
            act.wait_ge(mod2_ready, 2)
            for k in range(KT):
                act.wait_ge(x1T_mm, pair(k))
                b, half = 2 + (k // 2) % 2, k % 2
                act.activation(h2T[:, k, :], ps[:, b, half * T:(half + 1) * T], ACT.Identity,
                               bias=mod2[:, 1, k:k + 1], scale=mod2[:, 0, k:k + 1]).then_inc(h2_out, 1)
                if k == 0:
                    act.wait_ge(y_mm, 8)
                act.wait_ge(h2_out, k + 1)
                act.copy(h2H[:, k, :], h2T[:, k, :]).then_inc(h2H_out, 1)
            act.wait_ge(x1_stored, 16)
            act.wait_ge(x1T_mm, KT)
            def q_chunk(n):
                for i in range(4 * n, 4 * n + 4):
                    act.wait_ge(qT_mm, i + 1)
                    act.copy(qT[:, i, :], ps[:, [4, 5, 6, 7, 2, 3][i % 6], 0:T]).then_inc(qT_out, 1)
                gate_row(20 + n, 64 + 16 * n)

            for n in range(4):
                for k in range(KT):
                    if n or k >= len(wq_high):
                        weight_high("wq", n, k)
                    if n and k == len(wq_high) - 1:
                        q_chunk(n - 1)
            q_chunk(3)
            for j in range(4):
                act.wait_ge(key_mm, j + 1)
                act.copy(keyT[:, 4 * j:4 * j + 4, :].rearrange("p k n -> p (k n)"),
                         ps[:, 2 + j % 2, :]).then_inc(key_out, 1)
            def u_high(r, j, first=False):
                act.wait_ge(u_tr, r * (2 * ROUND) + (j + 1))
                if not (first and j < RING):
                    act.wait_ge(u_used, r * (2 * ROUND) + (j + 1 - RING))
                act.copy(by_k(eH[:, j % RING, :]), turned(raw[:, j % RAW, :])).then_inc(u_hi, 1)

            for j in range(8):
                act.wait_ge(sc_mm, j + 1)
                act.copy(sc[:, 4 * j:4 * j + 4, :].rearrange("p k n -> p (k n)"),
                         ps[:, 4 + j % 4, :]).then_inc(sc_out, 1)
                if j in (5, 7):
                    u_high(0, (j - 5) // 2, True)

            def gelu(tile, bank):
                act.wait_ge(u_used, tile * 2 + 2)
                act.activation(acts[:, bass.ds(tile, 1), :], ps[:, bank, 0:T], ACT.Gelu).then_inc(a_out, 1)

            def u_round(r, tiles=ROUND, first=False, slots_too=False):
                for j in range(2 * tiles):
                    if slots_too and j == RING + 1:
                        act.wait_ge(slot_mm, 1)
                        act.copy(slotT[:, 0:2, :].rearrange("p a t -> p (a t)"), ps[:, 4, :]).then_inc(slotT_out, 1)
                        act.copy(slotT[:, 2, :], ps[:, 5, 0:T]).then_inc(slotT_out, 1)
                    if not (first and j < 2):
                        u_high(r, j, first)
                    if j % 2 == 1 and not (first and j == 1):
                        gelu(r * ROUND + (j // 2 - 1), (j // 2 - 1) % 3)

            u_round(0, first=True)
            with act.Fori(1, REST + 1) as r:
                u_round(r)
            act.wait_ge(g_shift, 1)
            act.activation(gtmp[:], gtmp[:], ACT.Exp).then_inc(g_exp, 1)
            with act.Fori(REST + 1, REST + 4) as r:
                u_round(r)
            u_round(REST + 4, slots_too=True)
            with act.Fori(REST + 5, ROUNDS) as r:
                u_round(r)
            u_round(ROUNDS, TILES % ROUND)
            gelu(TILES - 1, 1)

            def hot_first(g, half, first):
                if not first:
                    act.wait_ge(hot_mm, g - 1)
                for t in range(2):
                    last_ = act.activation(hotA[:, half, t, :], iota, ACT.Abs,
                                           bias=slotT[:, 1, bass.ds(g * 4 + t, 1)], scale=-1.0)
                last_.then_inc(hot_abs, 1)
                act.wait_ge(hot_abs, g + 1)
                o = hotA[:, half, 0:2, :]
                act.activation(o, o, ACT.Relu, bias=ones[:, 0:1], scale=-1.0).then_inc(hot_act, 1)

            act.wait_ge(u_used, 2 * TILES)
            act.wait_ge(slotT_out, 2)
            hot_first(0, 0, True)
            hot_first(1, 1, True)
            with act.Fori(1, T // 8) as r:
                hot_first(r * 2, 0, False)
                hot_first(r * 2 + 1, 1, False)

            def v_tile(tile, j, first, rounds):
                if not first:
                    act.wait_ge(v_used, tile * 2 - 4)
                act.copy(aH[j][:], acts[:, bass.ds(tile, 1), :]).then_inc(act_hi, 1)
                for h in range(2):
                    g = 2 * j + h
                    slot = g % RING
                    act.wait_ge(v_in[slot], rounds(g))
                    if not (first and g < RING):
                        act.wait_ge(v_used, tile * 2 + (h - RING + 1))
                    act.copy(eH[:, slot, :], raw[:, slot, :]).then_inc(v_hi, 1)

            act.wait_ge(row_stored, 128)
            act.wait_ge(gated, T // 4)
            act.wait_ge(hot_mm, T // 4)
            for j in range(3):
                v_tile(j, j, True, lambda g: 16 * (g // RING + 1))
            with act.Fori(1, TILES // 3) as r:
                for j in range(3):
                    v_tile(r * 3 + j, j, False, lambda g: r * 32 + 16 * (g // RING + 1))
            for j in range(2):
                v_tile(TILES - 2 + j, j, False, lambda g: 32 * (TILES // 3) + 16 * (g // RING + 1))

            act.wait_ge(v_used, 2 * TILES)
            for tt in range(TT):
                seq(act.activation(raw[:, 0:2, :].rearrange("p a b -> p (a b)"),
                                   ps[:, 4 * tt:4 * tt + 4, :].rearrange("p a b -> p (a b)"), ACT.Square,
                                   accum_out=stat[:, 46 + tt:47 + tt]))
            act.nop().then_inc(y2_sq, 1)
            act.wait_ge(y2_rc, 1)
            act.activation(stat[:, 50:52], stat[:, 48:50], ACT.Sqrt).then_inc(y2_rs, 1)

        @block.vector
        def _(dve):
            count = [0]

            def seq(ins):
                count[0] += 1
                ins.then_inc(dve_chain, 1)
                dve.wait_ge(dve_chain, count[0])

            def ada(n, part=None):
                a, b = acc[:, n % 2, :], acc_b[:, n % 2, :]
                w = wide(("ada", n))
                if part != 1:
                    ring_arrived(dve, ("ada", n))
                    dve.wait_ge(init_in[n % 2], 16 * (n // 2 + 1))
                    if n >= 2:
                        dve.wait_ge(acc_used, n - 1)
                for k in {None: range(KT), 0: range(KT // 2), 1: range(KT // 2, KT)}[part]:
                    if k >= 2:
                        dve.wait_ge(dve_chain, count[0] - 1)
                    if k == 1:
                        ins = dve.tensor_scalar(b, w[:, k, :], c_act[:, k:k + 1], None, ALU.mult)
                    else:
                        s_ = b if k % 2 else a
                        ins = dve.scalar_tensor_tensor(s_, w[:, k, :], c_act[:, k:k + 1],
                                                       init[:, n % 2, :] if k == 0 else s_, ALU.mult, ALU.add)
                    if k < KT - 1:
                        count[0] += 1
                        ins.then_inc(dve_chain, 1)
                if part != 0:
                    ins.then_inc(acc_ready, 1)
                    dve.wait_ge(dve_chain, count[0])

            def inverse_mean(dst, src, width):
                seq(dve.tensor_scalar(dst, src, 1.0 / width, EPS, ALU.mult, ALU.add))
                seq(dve.reciprocal(dst, dst))

            dve.wait_ge(silu_done, 1)
            for n in range(2):
                ada(n)
            dve.wait_ge(vec_t, 1)
            seq(dve.tensor_copy(vcols[:], ps[:, 1, 0:V_ALL]))
            dve.nop().then_inc(vec_cols, 1)
            seq(dve.tensor_copy(pos_f[:], pos_i[:]))
            for tt in range(TT):
                seq(dve.tensor_scalar(ang[:, 0, tt * HALF:(tt + 1) * HALF], freq[:], pos_f[:, tt:tt + 1], None,
                                      ALU.mult))
            magic = 12582912.0
            seq(dve.tensor_scalar(ang[:, 3, :], ang[:, 0, :], 1.0 / (TWO_PI_A + TWO_PI_B + TWO_PI_C), None, ALU.mult))
            seq(dve.tensor_scalar(ang[:, 3, :], ang[:, 3, :], magic, None, ALU.add))
            seq(dve.tensor_scalar(ang[:, 3, :], ang[:, 3, :], magic, None, ALU.subtract))
            seq(dve.scalar_tensor_tensor(ang[:, 1, :], ang[:, 3, :], -TWO_PI_A, ang[:, 0, :], ALU.mult, ALU.add))
            seq(dve.scalar_tensor_tensor(ang[:, 1, :], ang[:, 3, :], -TWO_PI_B, ang[:, 1, :], ALU.mult, ALU.add))
            seq(dve.scalar_tensor_tensor(ang[:, 1, :], ang[:, 3, :], -TWO_PI_C, ang[:, 1, :], ALU.mult, ALU.add))
            pi = 3.1415925
            seq(dve.tensor_scalar(ang[:, 1, :], ang[:, 1, :], pi, -pi, ALU.min, ALU.max))
            seq(dve.tensor_scalar(ang[:, 2, :], ang[:, 1, :], -1.0, None, ALU.mult))
            seq(dve.tensor_tensor(ang[:, 2, :], ang[:, 2, :], ang[:, 1, :], ALU.max))
            seq(dve.tensor_scalar(ang[:, 2, :], ang[:, 2, :], -1.0, 1.5707963267948966, ALU.mult, ALU.add))
            dve.nop().then_inc(trig_arg, 1)

            ada(2)
            dve.wait_ge(x_sq, 1)
            inverse_mean(stat[:, 2:4], stat[:, 0:2], D)
            dve.nop().then_inc(x_rs, 1)
            dve.wait_ge(x_rs, 2)
            for tt in range(TT):
                seq(dve.tensor_scalar(diag[:, tt, :], ident, stat[:, 4 + tt:5 + tt], None, ALU.mult))
                dve.nop().then_inc(diag1, 1)
            ada(3)
            dve.wait_ge(acc_used, 4)
            seq(dve.scalar_tensor_tensor(mod1[:, 0, :], ps[:, 0, 0:KT], 1.0, vcols[:, V_G1:V_G1 + KT],
                                         ALU.add, ALU.mult))
            dve.nop().then_inc(mod1_ready, 1)
            for n in range(4, 8):
                ada(n)
            dve.wait_ge(acc_used, 8)
            seq(dve.tensor_copy(mod1[:, 1, :], ps[:, 0, KT:2 * KT]))
            dve.nop().then_inc(mod1_ready, 1)
            dve.wait_ge(hA_used, 1)
            for q in range(4):
                h = hT[:, 4 * q:4 * q + 4, :]
                dve.tensor_tensor(h, h, mod1[:, 1, 4 * q:4 * q + 4].unsqueeze(2).broadcast_to([P, 4, T]),
                                  ALU.add).then_inc(hB_done, 1)
            for q in range(4):
                dve.wait_ge(h_hi, q + 1)
                dve.tensor_tensor(hL[:, 4 * q:4 * q + 4, :], hT[:, 4 * q:4 * q + 4, :],
                                  hH[:, 4 * q:4 * q + 4, :].bitcast(F32), ALU.subtract).then_inc(h_lo, 1)
            for n in range(8, 10):
                ada(n)
            dve.wait_ge(trig_ready, 2)

            dve.wait_ge(u_out, 8)
            for g, w in enumerate(WINDOWS):
                u = uT[:, 2 * g:2 * g + 2, :]
                z = zT[:, 2 * g:2 * g + 2, :]
                s = [catT[:, 0:2, :], catT[:, 2:4, :]]
                src = u
                step = 1
                i = 0
                while step < w:
                    d = s[i % 2]
                    seq(dve.tensor_copy(d[:, :, 0:step], src[:, :, 0:step]))
                    seq(dve.tensor_tensor(d[:, :, step:T], src[:, :, step:T], src[:, :, 0:T - step], ALU.add))
                    src = d
                    step *= 2
                    i += 1
                seq(dve.scalar_tensor_tensor(z, src, 1.0 / w, u, ALU.mult, ALU.subtract))
                for ct in range(2):
                    o = s[i % 2][:, ct, 0:16]
                    seq(dve.tensor_tensor(o, src[:, ct, 0:16], cnt[:, g, :], ALU.mult))
                    seq(dve.tensor_tensor(z[:, ct, 0:16], o, u[:, ct, 0:16], ALU.subtract))
                dve.nop().then_inc(z_ready, 1)
            ada(10)

            dve.wait_ge(lat_sq, 1)
            seq(dve.tensor_scalar(stat[:, 12:14], stat[:, 8:10], 1.0 / QR, EPS, ALU.mult, ALU.add))
            seq(dve.tensor_scalar(stat[:, 14:16], stat[:, 10:12], 1.0 / KVR, EPS, ALU.mult, ALU.add))
            seq(dve.reciprocal(stat[:, 12:16], stat[:, 12:16]))
            dve.nop().then_inc(lat_sq, 1)
            dve.wait_ge(lat_sq, 3)
            dve.wait_ge(xT_done, KT)
            for tt in range(TT):
                seq(dve.tensor_scalar(diag[:, tt, :], ident, stat[:, 16 + tt:17 + tt], None, ALU.mult))
                dve.nop().then_inc(lat_diag, 1)
                seq(dve.tensor_scalar(tmpr[:, tt, 0:P], ident, stat[:, 18 + tt:19 + tt], None, ALU.mult))
                dve.nop().then_inc(lat_diag, 1)
            dve.wait_ge(trig_ready, 2)
            dve.wait_ge(lat_out, 4)

            def rotate(dst, src, tt, heads, t1):
                cos, sin = (trig[:, i, tt, :].unsqueeze(1).broadcast_to([P, heads, HALF]) for i in range(2))
                x1_, x2_ = src[:, :, 0:HALF], src[:, :, HALF:ROPE]
                tv = t1[:, 0:heads * HALF].rearrange("p (h f) -> p h f", h=heads)
                seq(dve.tensor_tensor(tv, x2_, sin, ALU.mult))
                seq(dve.tensor_tensor(dst[:, :, 0:HALF], x1_, cos, ALU.mult))
                seq(dve.tensor_tensor(dst[:, :, 0:HALF], dst[:, :, 0:HALF], tv, ALU.subtract))
                seq(dve.tensor_tensor(tv, x1_, sin, ALU.mult))
                seq(dve.tensor_tensor(dst[:, :, HALF:ROPE], x2_, cos, ALU.mult))
                seq(dve.tensor_tensor(dst[:, :, HALF:ROPE], dst[:, :, HALF:ROPE], tv, ALU.add))

            for tt in range(TT):
                kp = krope[:, tt, :].rearrange("p (h f) -> p h f", h=2)
                rotate(kp[:, 0:1, :], lat[:, tt, QR + KVR:LAT].rearrange("p (h f) -> p h f", h=1), tt, 1,
                       tmpr[:, 1, P:2 * P])
                seq(dve.tensor_copy(kp[:, 1:2, :], kp[:, 0:1, :]))
            dve.nop().then_inc(k_roped, 1)
            ada(11)
            dve.wait_ge(qpe_mm, 2)
            dve.wait_ge(cT_mm, 6)
            for tt in range(TT):
                rotate(qrope[:, tt, :].rearrange("p (h f) -> p h f", h=HEADS),
                       ps[:, 2 + tt, :].rearrange("p (h f) -> p h f", h=HEADS), tt, HEADS, tmpr[:, 0, :])
            dve.nop().then_inc(q_roped, 1)
            ada(12)

            def maxima(h):
                dve.wait_ge(s_mm, h + 1)
                if h >= 2:
                    dve.wait_ge(pT_mm, h - 1)
                s = s_sb[:, h % 2, :]
                seq(dve.scalar_tensor_tensor(s, ps[:, 4 + h % 2, 0:3 * P], SCALE, mask[:], ALU.mult, ALU.add))
                for qb in range(TT):
                    m = stat[:, 20 + 2 * (h % 2) + qb:21 + 2 * (h % 2) + qb]
                    seq(dve.tensor_reduce(m, s[:, qb * P:qb * P + (qb + 1) * P], AX_X, ALU.max, negate=True))
                dve.nop().then_inc(s_max, 1)

            def normalise(h):
                dve.wait_ge(s_exp, 2 * (h + 1))
                r = stat[:, 24 + 2 * (h % 2):26 + 2 * (h % 2)]
                seq(dve.reciprocal(r, r))
                for qb in range(TT):
                    s = s_sb[:, h % 2, qb * P:qb * P + (qb + 1) * P]
                    seq(dve.tensor_scalar(s, s, r[:, qb:qb + 1], None, ALU.mult))
                dve.nop().then_inc(s_norm, 1)

            for h in range(HEADS + 1):
                if h < HEADS:
                    maxima(h)
                if h >= 1:
                    normalise(h - 1)
                if h >= 1:
                    ada(13 + (h - 1) // 2, (h - 1) % 2)
            def gated_y(n):
                dve.wait_ge(y_out, 2 * n + 2)
                g = gate1[:, n * W:(n + 1) * W].unsqueeze(1).broadcast_to([P, TT, W])
                seq(dve.tensor_tensor(y1[:, :, n * W:(n + 1) * W], y1[:, :, n * W:(n + 1) * W], g, ALU.mult))

            ada(17)
            dve.wait_ge(g1_in, 32)
            seq(dve.tensor_tensor(gate1[:], gate1[:], post1[:], ALU.mult))
            ada(18)
            gated_y(0)
            ada(19)
            gated_y(1)

            dve.wait_ge(acc_used, 20)
            seq(dve.tensor_copy(mod2[:, 1, :], ps[:, 0, 64:64 + KT]))
            dve.nop().then_inc(mod2_ready, 1)
            seq(dve.scalar_tensor_tensor(mod2[:, 0, :], ps[:, 0, 64 + KT:64 + 2 * KT], 1.0,
                                         vcols[:, V_G2:V_G2 + KT], ALU.add, ALU.mult))
            dve.nop().then_inc(mod2_ready, 1)
            gated_y(2)
            dve.wait_ge(y_out, 8)
            for tt in range(TT):
                seq(dve.tensor_reduce(stat[:, 36 + tt:37 + tt], stat[:, 28 + 4 * tt:32 + 4 * tt], AX_X, ALU.add))
            inverse_mean(stat[:, 36:38], stat[:, 36:38], D)
            dve.nop().then_inc(y_rc, 1)
            gated_y(3)
            dve.wait_ge(y_rs, 1)
            for tt in range(TT):
                xv, yv = (t[:, tt, :].rearrange("p (q k l) -> p q k l", q=4, l=QUAD) for t in (xs, y1))
                for q in range(4):
                    ins = dve.scalar_tensor_tensor(
                        x1q[:, tt, :].rearrange("p (k q l) -> p q k l", q=4, l=QUAD)[:, q], yv[:, q],
                        stat[:, 38 + tt:39 + tt], xv[:, q], ALU.mult, ALU.add)
                seq(ins)
                dve.nop().then_inc(x1_done, 1)
            dve.wait_ge(x1_sq, 1)
            inverse_mean(stat[:, 42:44], stat[:, 40:42], D)
            dve.nop().then_inc(x1_rs, 1)
            dve.wait_ge(x1_rs, 2)
            dve.wait_ge(cT_mm, 6)
            for tt in range(TT):
                seq(dve.tensor_scalar(diag[:, tt, :], ident, stat[:, 44 + tt:45 + tt], None, ALU.mult))
                dve.nop().then_inc(diag2, 1)
            for k in range(KT):
                dve.wait_ge(h2H_out, k + 1)
                dve.tensor_tensor(h2L[:, k, :], h2T[:, k, :], h2H[:, k, :].bitcast(F32),
                                  ALU.subtract).then_inc(h2L_out, 1)

            for n in range(20, 24):
                ada(n)

            def row(t, i):
                return t[:, bass.ds(i, 1), :].rearrange("p a k -> p (a k)")

            def after(n):
                dve.wait_ge(pick_chain, n)

            PICK_DONE = (2, 4, 8, 10, 12, 16)
            PICKS = PICK_DONE[-1]
            KEY_GROUPS = TT * KT // 2
            ALL_GROUPS = KEY_GROUPS + TT * PH // 2

            def pick_wait(group, step):
                done = PICK_DONE[step - 1] if step else 0
                if step or not (isinstance(group, int) and group == 0):
                    after(group * PICKS + done)

            def pick_step(group, step, pairs):
                n = TOPK * TOPK if pairs else NK
                for u in range(2):
                    i = (group - KEY_GROUPS if pairs else group) * 2 + u
                    v, w = cand[:, u, 0:n], rest[:, u, 0:n]
                    best8, next8 = picked[:, u, 0:8], picked[:, u, 8:16]
                    if step == 0 and pairs:
                        s0 = row(s16, i * 2).unsqueeze(2).broadcast_to([P, TOPK, TOPK])
                        s1 = row(s16, i * 2 + 1).unsqueeze(1).broadcast_to([P, TOPK, TOPK])
                        dve.tensor_tensor(v.rearrange("p (a b) -> p a b", a=TOPK), s0, s1,
                                          ALU.add).then_inc(pick_chain, 1)
                    elif step == 0:
                        dve.tensor_copy(v, row(sc, i)).then_inc(pick_chain, 1)
                    elif step == 1:
                        dve.max(best8, v).then_inc(pick_chain, 1)
                    elif step == 2:
                        dve.max_index(picked_at[:, u, 0:8], best8, v).then_inc(pick_chain, 1)
                        dve.match_replace(w, best8, v, -BIG).then_inc(pick_chain, 1)
                    elif step == 3:
                        dve.max(next8, w).then_inc(pick_chain, 1)
                    elif step == 4:
                        dve.max_index(picked_at[:, u, 8:16], next8, w).then_inc(pick_chain, 1)
                    else:
                        dve.tensor_copy(row(posu if pairs else i16f, i), picked_at[:, u, :]).then_inc(pick_chain, 1)
                        dve.tensor_copy(row(best if pairs else s16, i), picked[:, u, :]).then_inc(pick_chain, 1)

            def gates_before_exp():
                after(ALL_GROUPS * PICKS)
                seq(dve.tensor_tensor(gtmp[:], best[:], best[:, :, 0:1].broadcast_to([P, TT * PH, TOPK]),
                                      ALU.subtract))
                dve.nop().then_inc(g_shift, 1)
                pu = posu[:].rearrange("p (t h) k -> p t (h k)", t=TT)
                seq(dve.tensor_scalar(posa[:], pu, 4, None, ALU.logical_shift_right))
                seq(dve.tensor_copy(posf[:, 0], posa[:]))
                seq(dve.tensor_scalar(posa[:], pu, 15, None, ALU.bitwise_and))
                seq(dve.tensor_copy(posf[:, 1], posa[:]))

            def gates_after_exp():
                dve.wait_ge(g_exp, 1)
                seq(dve.tensor_reduce(gsum[:], gtmp[:], AX_X, ALU.add))
                seq(dve.reciprocal(gsum[:], gsum[:]))
                seq(dve.tensor_tensor(slots[:, 2].rearrange("p t (h k) -> p (t h) k", h=PH), gtmp[:],
                                      gsum[:].unsqueeze(2).broadcast_to([P, TT * PH, TOPK]), ALU.mult))

            def sub_keys(step):
                tt, p, part = step // 6, step // 3 % 2, step % 3
                eq = tmpk[:].rearrange("p (h k a) -> p h k a", h=PH, k=TOPK)
                pr = tmpk2[:].rearrange("p (h k a) -> p h k a", h=PH, k=TOPK)
                if part == 0:
                    seq(dve.tensor_tensor(
                        eq.rearrange("p h k a -> p (h k) a"),
                        posf[:, p, tt, :].unsqueeze(2).broadcast_to([P, PH * TOPK, TOPK]),
                        i16[:].unsqueeze(1).broadcast_to([P, PH * TOPK, TOPK]), ALU.is_equal))
                elif part == 1:
                    tab = i16f[:, tt * KT:(tt + 1) * KT].rearrange("p (h s) a -> p h s a", s=2)[:, :, p, :]
                    seq(dve.tensor_tensor(pr, eq, tab.unsqueeze(2).broadcast_to([P, PH, TOPK, TOPK]), ALU.mult))
                else:
                    seq(dve.tensor_reduce(slots[:, p, tt, :], pr.rearrange("p h k a -> p (h k) a"), AX_X, ALU.add))

            def u_low(r, j, first=False):
                dve.wait_ge(u_hi, r * (2 * ROUND) + (j + 1))
                if not first:
                    dve.wait_ge(u_used, r * (2 * ROUND) + (j + 1 - RING))
                dve.tensor_tensor(by_k(eL[:, j % RING, :]), turned(raw[:, j % RAW, :]),
                                  by_k(eH[:, j % RING, :].bitcast(F32)), ALU.subtract).then_inc(u_lo, 1)

            def u_round(r, tiles=ROUND, first=False, pairs=None, beside=None):
                for j in range(2 * tiles):
                    if pairs is not None and not (first and j < 2):
                        pick_wait(r * 2 + j // 6, j % 6)
                    dve.wait_ge(raw_in[j % RAW], r * (64 * 2 * ROUND // RAW) + 64 * (j // RAW + 1))
                    dve.transpose(raw[:, j % RAW, :], raw[:, j % RAW, :]).then_inc(u_tr, 1)
                    if j % 2:
                        u_low(r, j - 1, first and j - 1 < RING)
                    if first and j == 1:
                        dve.wait_ge(sc_out, 8)
                        pick_step(0, 0, pairs)
                        pick_wait(0, 1)
                    if pairs is not None and not (first and j == 0):
                        pick_step(r * 2 + j // 6, j % 6, pairs)
                    if beside:
                        beside(j)

            def beside_rest(i):
                def work(j):
                    if i == 0 and j == 0:
                        gates_before_exp()
                    if i == 1 and j == 0:
                        gates_after_exp()
                    at_ = j + 2 * ROUND * i - 4
                    if at_ >= 0 and at_ % 3 == 0 and at_ // 3 < 12:
                        sub_keys(at_ // 3)
                return work

            u_round(0, first=True, pairs=False)
            with dve.Fori(1, KEY_ROUNDS) as r:
                u_round(r, pairs=False)
            with dve.Fori(KEY_ROUNDS, REST) as r:
                u_round(r, pairs=True)
            for i in range(4):
                u_round(REST + i, beside=beside_rest(i))
            dve.nop().then_inc(slots_ready, 1)
            with dve.Fori(REST + 4, ROUNDS) as r:
                u_round(r)
            u_round(ROUNDS, TILES % ROUND)

            def hots(g, half, first):
                if not first:
                    dve.wait_ge(hot_mm, g - 1)
                for t in range(4):
                    i1, gt = (slotT[:, m, bass.ds(g * 4 + t, 1)] for m in (0, 2))
                    last_ = dve.tensor_scalar(hotB[:, half, t, :], iota, i1, gt, ALU.is_equal, ALU.mult)
                last_.then_inc(hot_ready, 1)

            def apply_gates(g, half):
                dve.wait_ge(hot_mm, g + 1)
                a = acts[:, :, bass.ds(g * 4, 4)]
                dve.tensor_tensor(a, a, ps[:, half, :].rearrange("p (t i) -> p i t", t=4), ALU.mult).then_inc(gated, 1)

            dve.wait_ge(slotT_out, 2)
            dve.wait_ge(a_out, TILES)
            dve.wait_ge(u_used, 2 * TILES)
            hots(0, 0, True)
            hots(1, 1, True)
            apply_gates(0, 0)
            with dve.Fori(1, T // 8) as r:
                hots(r * 2, 0, False)
                apply_gates(r * 2 - 1, 1)
                hots(r * 2 + 1, 1, False)
                apply_gates(r * 2, 0)
            apply_gates(T // 4 - 1, 1)

            def v_tile(tile, j, first):
                dve.wait_ge(act_hi, tile + 1)
                if not first:
                    dve.wait_ge(v_used, tile * 2 - 4)
                dve.tensor_tensor(aL[j][:], acts[:, bass.ds(tile, 1), :].rearrange("p a t -> p (a t)"),
                                  aH[j][:].bitcast(F32), ALU.subtract).then_inc(act_lo, 1)
                for h in range(2):
                    slot = (2 * j + h) % RING
                    dve.wait_ge(v_hi, tile * 2 + (h + 1))
                    dve.tensor_tensor(eL[:, slot, :], raw[:, slot, :], eH[:, slot, :].bitcast(F32),
                                      ALU.subtract).then_inc(v_lo, 1)

            for j in range(3):
                v_tile(j, j, True)
            with dve.Fori(1, TILES // 3) as r:
                for j in range(3):
                    v_tile(r * 3 + j, j, False)
            for j in range(2):
                v_tile(TILES - 2 + j, j, False)

            dve.wait_ge(tail_in, 48)
            seq(dve.tensor_tensor(gate2[:], gate2[:], post2[:], ALU.mult))
            dve.wait_ge(y2_sq, 1)
            inverse_mean(stat[:, 48:50], stat[:, 46:48], D)
            dve.nop().then_inc(y2_rc, 1)
            dve.wait_ge(y2_rs, 1)
            for tt in range(TT):
                seq(dve.scalar_tensor_tensor(scaled[:, tt, :], ps[:, 4 * tt:4 * tt + 4, :].rearrange("p a b -> p (a b)"),
                                             stat[:, 50 + tt:51 + tt], gate2[:], ALU.mult, ALU.mult))
                dve.nop().then_inc(scaled_ready, 1)
            add_x1(dve, 1)


def constant_table(np):
    t = np.zeros((P, C_ALL), np.float32)
    t[:, C_ID:C_ID + P] = np.eye(P)
    t[:, C_ONE:C_ONE + P] = 1.0
    t[:, C_IOTA:C_IOTA + P] = np.arange(P)
    for start in (C_MASK, C_MASK + 2 * P):
        t[0:P // 2, start + P // 2:start + P] = -1e30
    half = np.arange(HALF, dtype=np.float32) / np.float32(HALF)
    t[:, C_FREQ:C_FREQ + HALF] = np.float32(10000.0) ** (-half)
    for g, w in enumerate(WINDOWS):
        t[:, C_CNT + 16 * g:C_CNT + 16 * (g + 1)] = 1.0 / np.minimum(np.arange(16) + 1, w)
    t[:, C_I16:C_I16 + 16] = np.arange(16)
    return t


_INS = ['x', 'c', 'positions', 'ada_w', 'ada_b', 'pre_mix_g', 'post_mix_g', 'pre_ffn_g', 'post_ffn_g',
        'w_in', 'pool_w', 'pool_scale', 'q_norm_g', 'w_uq', 'kv_norm_g', 'w_ukv', 'w_out',
        'peer_wq', 'peer_sub_keys', 'peer_u', 'peer_v']
_OUTS = [((1, 256, 2048), 'float32')]


def kernel(**inputs):
    import numpy as _np
    import concourse.bacc as _bacc
    from concourse import mybir as _mybir
    from concourse.bass_utils import run_bass_kernel_spmd as _run

    nc = _bacc.Bacc("TRN2", target_bir_lowering=False, num_devices=1)
    arrays, args = {}, []
    for name in _INS:
        a = _np.ascontiguousarray(inputs[name])
        arrays[f"in_{name}_dram"] = a
        args.append(nc.dram_tensor(f"in_{name}_dram", a.shape, _mybir.dt.from_np(a.dtype), kind="ExternalInput").ap())
    table = constant_table(_np)
    arrays["consts_dram"] = table
    args.append(nc.dram_tensor("consts_dram", table.shape, _mybir.dt.float32, kind="ExternalInput").ap())
    for i, (shape, dtype) in enumerate(_OUTS):
        dt = _mybir.dt.from_np(_np.dtype(dtype))
        args.append(nc.dram_tensor(f"out_{i}_dram", shape, dt, kind="ExternalOutput").ap())
    hybrid_block(nc, *args)
    r = _run(nc, [arrays], core_ids=[0])
    got = tuple(r.results[0][f"out_{i}_dram"] for i in range(len(_OUTS)))
    return got[0]
```
